# Optimizing a Trainium2 kernel written in Bass

```python
import jax, jax.numpy as jnp
from jax import lax
import numpy as np
import math

D_MODEL = 1024
BATCH = 1
SEQ = 256
DEPTH = 2

D_CONV = D_MODEL // 2
D_POOL = D_MODEL // 2
CONV_K = 31
POOL_WINDOWS = (2, 4, 8, 16)
N_POOL_GROUPS = len(POOL_WINDOWS)
POOL_GROUP = D_POOL // N_POOL_GROUPS
POOL_OUT_GROUP = D_MODEL // N_POOL_GROUPS
N_BRANCHES = 2
D_IN = 2 * D_CONV + D_POOL + N_BRANCHES * D_MODEL

N_EXPERT_GROUPS = 4
EXPERTS_PER_GROUP = 8
N_EXPERTS = N_EXPERT_GROUPS * EXPERTS_PER_GROUP
TOP_K = 2
D_EXPERT = D_MODEL // 4

N_MOD = 6
EPS = 1e-6


def rms_norm(x, g):
    xf = x.astype(jnp.float32)
    y = xf * lax.rsqrt(jnp.mean(xf * xf, axis=-1, keepdims=True) + EPS)
    return (y * g.astype(jnp.float32)).astype(x.dtype)

def layer_norm(x, g, b):
    xf = x.astype(jnp.float32)
    mu = jnp.mean(xf, axis=-1, keepdims=True)
    var = jnp.mean(jnp.square(xf - mu), axis=-1, keepdims=True)
    y = (xf - mu) * lax.rsqrt(var + EPS)
    return (y * g.astype(jnp.float32) + b.astype(jnp.float32)).astype(x.dtype)

def modulate(h, shift, scale):
    return h * (1 + scale[:, None, :]) + shift[:, None, :]

def conformer_conv_branch(u, conv_w, conv_b, ln_g, ln_b, w_pw, b_pw):
    a, g = jnp.split(u, 2, axis=-1)
    v = a * jax.nn.sigmoid(g)
    v = lax.conv_general_dilated(
        v, conv_w[:, None, :], window_strides=(1,), padding=[(CONV_K - 1, 0)],
        dimension_numbers=("NWC", "WIO", "NWC"), feature_group_count=D_CONV) + conv_b
    v = jax.nn.silu(layer_norm(v, ln_g, ln_b))
    return v @ w_pw + b_pw

def causal_window_mean(u, w):
    s_len = u.shape[1]
    cs = jnp.cumsum(u.astype(jnp.float32), axis=1)
    shifted = jnp.pad(cs, ((0, 0), (w, 0), (0, 0)))[:, :s_len]
    count = jnp.minimum(jnp.arange(1, s_len + 1), w).astype(jnp.float32)
    return ((cs - shifted) / count[None, :, None]).astype(u.dtype)

def pool_branch(u, pool_w, pool_scale):
    b, s, _ = u.shape
    ug = u.reshape(b, s, N_POOL_GROUPS, POOL_GROUP)
    pooled = jnp.stack([causal_window_mean(ug[:, :, gi], w)
                        for gi, w in enumerate(POOL_WINDOWS)], axis=2) - ug
    y = jnp.einsum("bsgc,gco->bsgo", pooled, pool_w).reshape(b, s, D_MODEL)
    return y * pool_scale

def hierarchical_moe(h, w_rg, b_rg, w_re, b_re, w_g, w_u, w_d):
    b, s, d = h.shape
    t = h.reshape(b * s, d)
    n_tok = t.shape[0]
    group_probs = jax.nn.softmax((t @ w_rg + b_rg).astype(jnp.float32), axis=-1)
    p_group, g_idx = lax.top_k(group_probs, 1)
    exp_logits = (t @ w_re + b_re).astype(jnp.float32).reshape(n_tok, N_EXPERT_GROUPS, EXPERTS_PER_GROUP)
    in_group = jnp.take_along_axis(exp_logits, g_idx[:, :, None], axis=1)[:, 0]
    p_exp, e_idx = lax.top_k(jax.nn.softmax(in_group, axis=-1), TOP_K)
    weights = p_group * p_exp / jnp.sum(p_exp, axis=-1, keepdims=True)
    expert_id = g_idx * EXPERTS_PER_GROUP + e_idx
    combine = jnp.sum(jax.nn.one_hot(expert_id, N_EXPERTS, dtype=jnp.float32) * weights[..., None],
                      axis=1).astype(h.dtype)
    out = jnp.zeros_like(t)
    for gi in range(N_EXPERT_GROUPS):
        sl = slice(gi * EXPERTS_PER_GROUP, (gi + 1) * EXPERTS_PER_GROUP)
        act = jax.nn.silu(jnp.einsum("td,edh->teh", t, w_g[sl])) * jnp.einsum("td,edh->teh", t, w_u[sl])
        out = out + jnp.einsum("teh,ehd->td", act * combine[:, sl, None], w_d[sl])
    return out.reshape(b, s, d)

def first_inputs(seed: int = 0) -> dict:
    key = jax.random.key(seed)
    ks = jax.random.split(key, 24)
    f32 = jnp.float32
    nrm = lambda k, shape, scale: (jax.random.normal(k, shape, f32) * scale)
    return {
        "x": nrm(ks[0], (BATCH, SEQ, D_MODEL), 1.0),
        "c": nrm(ks[1], (BATCH, D_MODEL), 1.0),
        "mixer_norm_g": 1.0 + nrm(ks[2], (DEPTH, D_MODEL), 0.05),
        "w_ada": nrm(ks[3], (DEPTH, D_MODEL, N_MOD * D_MODEL), 0.5 * D_MODEL ** -0.5),
        "b_ada": nrm(ks[4], (DEPTH, N_MOD * D_MODEL), 0.02),
        "w_in": nrm(ks[5], (DEPTH, D_MODEL, D_IN), D_MODEL ** -0.5),
        "conv_w": nrm(ks[6], (DEPTH, CONV_K, D_CONV), CONV_K ** -0.5),
        "conv_b": nrm(ks[7], (DEPTH, D_CONV), 0.02),
        "conv_ln_g": 1.0 + nrm(ks[8], (DEPTH, D_CONV), 0.05),
        "conv_ln_b": nrm(ks[9], (DEPTH, D_CONV), 0.02),
        "w_conv_out": nrm(ks[10], (DEPTH, D_CONV, D_MODEL), D_CONV ** -0.5),
        "b_conv_out": nrm(ks[11], (DEPTH, D_MODEL), 0.02),
        "pool_w": nrm(ks[12], (DEPTH, N_POOL_GROUPS, POOL_GROUP, POOL_OUT_GROUP), POOL_GROUP ** -0.5),
        "pool_scale": 1.0 + nrm(ks[13], (DEPTH, D_MODEL), 0.1),
        "w_out": nrm(ks[14], (DEPTH, D_MODEL, D_MODEL), D_MODEL ** -0.5),
        "ffn_norm_g": 1.0 + nrm(ks[15], (DEPTH, D_MODEL), 0.05),
        "w_router_group": nrm(ks[16], (DEPTH, D_MODEL, N_EXPERT_GROUPS), D_MODEL ** -0.5),
        "b_router_group": nrm(ks[17], (DEPTH, N_EXPERT_GROUPS), 0.01),
        "w_router_expert": nrm(ks[18], (DEPTH, D_MODEL, N_EXPERTS), D_MODEL ** -0.5),
        "b_router_expert": nrm(ks[19], (DEPTH, N_EXPERTS), 0.01),
        "w_expert_gate": nrm(ks[20], (DEPTH, N_EXPERTS, D_MODEL, D_EXPERT), D_MODEL ** -0.5),
        "w_expert_up": nrm(ks[21], (DEPTH, N_EXPERTS, D_MODEL, D_EXPERT), D_MODEL ** -0.5),
        "w_expert_down": nrm(ks[22], (DEPTH, N_EXPERTS, D_EXPERT, D_MODEL), D_EXPERT ** -0.5),
        "final_norm_g": 1.0 + nrm(ks[23], (D_MODEL,), 0.05),
    }

def first_block(x, c, mixer_norm_g, w_ada, b_ada, w_in, conv_w, conv_b, conv_ln_g, conv_ln_b,
              w_conv_out, b_conv_out, pool_w, pool_scale, w_out, ffn_norm_g,
              w_router_group, b_router_group, w_router_expert, b_router_expert,
              w_expert_gate, w_expert_up, w_expert_down, final_norm_g):
    c_act = jax.nn.silu(c)
    for l in range(DEPTH):
        mod = c_act @ w_ada[l] + b_ada[l]
        sh1, sc1, g1, sh2, sc2, g2 = jnp.split(mod, N_MOD, axis=-1)
        h = modulate(rms_norm(x, mixer_norm_g[l]), sh1, sc1)
        proj = h @ w_in[l]
        u_conv = proj[..., :2 * D_CONV]
        u_pool = proj[..., 2 * D_CONV:2 * D_CONV + D_POOL]
        gate_a, gate_b = jnp.split(jax.nn.sigmoid(proj[..., 2 * D_CONV + D_POOL:]), N_BRANCHES, axis=-1)
        y_a = conformer_conv_branch(u_conv, conv_w[l], conv_b[l], conv_ln_g[l], conv_ln_b[l],
                                    w_conv_out[l], b_conv_out[l])
        y_b = pool_branch(u_pool, pool_w[l], pool_scale[l])
        mixed = gate_a * y_a + gate_b * y_b
        x = x + g1[:, None, :] * (mixed @ w_out[l])
        h2 = modulate(rms_norm(x, ffn_norm_g[l]), sh2, sc2)
        x = x + g2[:, None, :] * hierarchical_moe(h2, w_router_group[l], b_router_group[l],
                                                  w_router_expert[l], b_router_expert[l],
                                                  w_expert_gate[l], w_expert_up[l], w_expert_down[l])
    return rms_norm(x, final_norm_g)


HEAD_DIM = 64
N_HEADS = D_MODEL // HEAD_DIM
SWA_Q_HEADS = N_HEADS // 2
SWA_KV_HEADS = max(1, SWA_Q_HEADS // 4)
MOBA_HEADS = N_HEADS - SWA_Q_HEADS
SWA_WIDTH = SWA_Q_HEADS * HEAD_DIM
SWA_KV_WIDTH = SWA_KV_HEADS * HEAD_DIM
MOBA_WIDTH = MOBA_HEADS * HEAD_DIM
MIX_WIDTH = SWA_WIDTH + MOBA_WIDTH
IN_COLS = SWA_WIDTH + 2 * SWA_KV_WIDTH + 3 * MOBA_WIDTH
IN_SPLITS = (SWA_WIDTH,
             SWA_WIDTH + SWA_KV_WIDTH,
             SWA_WIDTH + 2 * SWA_KV_WIDTH,
             SWA_WIDTH + 2 * SWA_KV_WIDTH + MOBA_WIDTH,
             SWA_WIDTH + 2 * SWA_KV_WIDTH + 2 * MOBA_WIDTH)
SWA_WINDOW = 128
SWA_BLOCK = 128
MOBA_BLOCK = 256
MOBA_TOPK = 3
MOBA_Q_CHUNK = 128
T5_BUCKETS = 32
T5_MAX_DIST = 128
D_FF = ((8 * D_MODEL // 3 + 255) // 256) * 256
N_MOD_2 = 9
NEG = -1e30


def rmsnorm(x, g):
    xf = x.astype(jnp.float32)
    y = xf * lax.rsqrt(jnp.mean(xf * xf, axis=-1, keepdims=True) + EPS)
    return (y * g.astype(jnp.float32)).astype(x.dtype)

def t5_bucket(dist):
    n = jnp.maximum(dist, 0)
    max_exact = T5_BUCKETS // 2
    nf = jnp.maximum(n, 1).astype(jnp.float32)
    large = max_exact + (jnp.log(nf / max_exact) / math.log(T5_MAX_DIST / max_exact)
                         * (T5_BUCKETS - max_exact)).astype(jnp.int32)
    large = jnp.minimum(large, T5_BUCKETS - 1)
    return jnp.where(n < max_exact, n, large)

def swiglu(h, w_gate, w_up, w_down):
    return (jax.nn.silu(h @ w_gate) * (h @ w_up)) @ w_down

def swa_attention(q, k, v, sinks, table):
    B_, S, Hq, dh = q.shape
    Hkv = k.shape[2]
    G = Hq // Hkv
    L = SWA_BLOCK
    nblk = S // L
    qb = q.reshape(B_, nblk, L, Hkv, G, dh)
    kb = k.reshape(B_, nblk, L, Hkv, dh)
    vb = v.reshape(B_, nblk, L, Hkv, dh)
    pad = ((0, 0), (1, 0), (0, 0), (0, 0), (0, 0))
    kw = jnp.concatenate([jnp.pad(kb, pad)[:, :-1], kb], axis=2)
    vw = jnp.concatenate([jnp.pad(vb, pad)[:, :-1], vb], axis=2)
    s = jnp.einsum('bnqhgd,bnkhd->bnhgqk', qb, kw).astype(jnp.float32) * (dh ** -0.5)
    qi = jnp.arange(L)[:, None]
    kj = jnp.arange(2 * L)[None, :]
    dist = qi + L - kj
    bias = table.T[:, t5_bucket(dist)].astype(jnp.float32).reshape(Hkv, G, L, 2 * L)
    kpos = jnp.arange(nblk)[:, None, None] * L - L + kj[None]
    valid = (dist >= 0)[None] & (dist < SWA_WINDOW)[None] & (kpos >= 0)
    s = jnp.where(valid[None, :, None, None], s + bias, NEG)
    sink = jnp.broadcast_to(sinks.astype(jnp.float32).reshape(1, 1, Hkv, G, 1, 1),
                            s.shape[:-1] + (1,))
    p = jax.nn.softmax(jnp.concatenate([s, sink], axis=-1), axis=-1)[..., :-1]
    o = jnp.einsum('bnhgqk,bnkhd->bnqhgd', p.astype(v.dtype), vw)
    return o.reshape(B_, S, Hq, dh)

def moba_attention(q, k, v, table):
    B_, S, H, dh = q.shape
    L = MOBA_BLOCK
    C = MOBA_Q_CHUNK
    nb = -(-S // L)
    Sp = nb * L
    padw = ((0, 0), (0, Sp - S), (0, 0), (0, 0))
    q, k, v = jnp.pad(q, padw), jnp.pad(k, padw), jnp.pad(v, padw)
    kb = k.reshape(B_, nb, L, H, dh).transpose(0, 3, 1, 2, 4)
    vb = v.reshape(B_, nb, L, H, dh).transpose(0, 3, 1, 2, 4)
    kmean = jnp.mean(kb, axis=3)
    topk = min(MOBA_TOPK, nb)
    nchunk = Sp // C
    qc = q.reshape(B_, nchunk, C, H, dh).transpose(1, 0, 3, 2, 4)
    scale = dh ** -0.5
    tableT = table.T.astype(jnp.float32)
    bi = jnp.arange(B_)[:, None, None, None]
    hi = jnp.arange(H)[None, :, None, None]
    hi5 = jnp.arange(H)[None, :, None, None, None]

    def chunk_fn(args):
        qblk, ci = args
        q_pos = ci * C + jnp.arange(C)
        cur = (ci * C) // L
        gate = jnp.einsum('bhcd,bhnd->bhcn', qblk, kmean)
        gate = jnp.where(jnp.arange(nb) < cur, gate, NEG)
        _, sel = lax.top_k(gate, topk)
        sel_ok = jnp.arange(topk) < cur
        k_sel = kb[bi, hi, sel]
        v_sel = vb[bi, hi, sel].reshape(B_, H, C, topk * L, dh)
        s_sel = jnp.einsum('bhcd,bhctld->bhctl', qblk, k_sel).astype(jnp.float32) * scale
        k_pos_sel = sel[..., None] * L + jnp.arange(L)
        dist_sel = q_pos[None, None, :, None, None] - k_pos_sel
        s_sel = s_sel + tableT[hi5, t5_bucket(dist_sel)]
        s_sel = jnp.where(sel_ok[None, None, None, :, None], s_sel, NEG)
        s_sel = s_sel.reshape(B_, H, C, topk * L)
        k_own = lax.dynamic_index_in_dim(kb, cur, axis=2, keepdims=False)
        v_own = lax.dynamic_index_in_dim(vb, cur, axis=2, keepdims=False)
        dist_own = q_pos[:, None] - (cur * L + jnp.arange(L))[None, :]
        s_own = jnp.einsum('bhcd,bhld->bhcl', qblk, k_own).astype(jnp.float32) * scale
        s_own = jnp.where(dist_own >= 0, s_own + tableT[:, t5_bucket(dist_own)], NEG)
        p = jax.nn.softmax(jnp.concatenate([s_sel, s_own], axis=-1), axis=-1).astype(v.dtype)
        o = (jnp.einsum('bhck,bhckd->bhcd', p[..., :topk * L], v_sel)
             + jnp.einsum('bhcl,bhld->bhcd', p[..., topk * L:], v_own))
        return o

    out = lax.map(chunk_fn, (qc, jnp.arange(nchunk)))
    out = out.transpose(1, 0, 3, 2, 4).reshape(B_, Sp, H, dh)
    return out[:, :S]

def hybrid_mixer(h, w_in, b_in, w_out, sinks, group_gain, rel_bias):
    B_, S, _ = h.shape
    proj = h @ w_in + b_in
    qa, ka, va, qb, kb, vb = jnp.split(proj, IN_SPLITS, axis=-1)
    qa = qa.reshape(B_, S, SWA_Q_HEADS, HEAD_DIM)
    ka = ka.reshape(B_, S, SWA_KV_HEADS, HEAD_DIM)
    va = va.reshape(B_, S, SWA_KV_HEADS, HEAD_DIM)
    qb = qb.reshape(B_, S, MOBA_HEADS, HEAD_DIM)
    kb = kb.reshape(B_, S, MOBA_HEADS, HEAD_DIM)
    vb = vb.reshape(B_, S, MOBA_HEADS, HEAD_DIM)
    ya = swa_attention(qa, ka, va, sinks, rel_bias[:, :SWA_Q_HEADS]).reshape(B_, S, SWA_WIDTH)
    yb = moba_attention(qb, kb, vb, rel_bias[:, SWA_Q_HEADS:]).reshape(B_, S, MOBA_WIDTH)
    y = jnp.concatenate([rmsnorm(ya, group_gain[:SWA_WIDTH]),
                         rmsnorm(yb, group_gain[SWA_WIDTH:])], axis=-1)
    return y @ w_out

def second_inputs(seed: int = 0) -> dict:
    key = jax.random.key(seed)
    ks = jax.random.split(key, 16)
    f = jnp.float32

    def w(k, shape, fan_in, gain=1.0):
        return jax.random.normal(k, shape, f) * (gain * fan_in ** -0.5)

    return {
        'x': jax.random.normal(ks[0], (BATCH, SEQ, D_MODEL), f),
        'c': jax.random.normal(ks[1], (BATCH, D_MODEL), f),
        'rel_bias': 0.5 * jax.random.normal(ks[2], (T5_BUCKETS, N_HEADS), f),
        'ada_w': w(ks[3], (DEPTH, D_MODEL, N_MOD_2 * D_MODEL), D_MODEL, 0.5),
        'ada_b': 0.01 * jax.random.normal(ks[4], (DEPTH, N_MOD_2 * D_MODEL), f),
        'norm_pre': 1.0 + 0.05 * jax.random.normal(ks[5], (DEPTH, 3, D_MODEL), f),
        'norm_post': 1.0 + 0.05 * jax.random.normal(ks[6], (DEPTH, 3, D_MODEL), f),
        'ffn_w_gate': w(ks[7], (DEPTH, 2, D_MODEL, D_FF), D_MODEL),
        'ffn_w_up': w(ks[8], (DEPTH, 2, D_MODEL, D_FF), D_MODEL),
        'ffn_w_down': w(ks[9], (DEPTH, 2, D_FF, D_MODEL), D_FF),
        'mix_w_in': w(ks[10], (DEPTH, D_MODEL, IN_COLS), D_MODEL),
        'mix_b_in': 0.01 * jax.random.normal(ks[11], (DEPTH, IN_COLS), f),
        'mix_w_out': w(ks[12], (DEPTH, MIX_WIDTH, D_MODEL), MIX_WIDTH),
        'attn_sinks': jax.random.normal(ks[13], (DEPTH, SWA_Q_HEADS), f),
        'group_gain': 1.0 + 0.05 * jax.random.normal(ks[14], (DEPTH, MIX_WIDTH), f),
    }

def second_block(x, c, rel_bias, ada_w, ada_b, norm_pre, norm_post, ffn_w_gate, ffn_w_up,
              ffn_w_down, mix_w_in, mix_b_in, mix_w_out, attn_sinks, group_gain):
    c_act = jax.nn.silu(c)
    for l in range(DEPTH):
        mod = (c_act @ ada_w[l] + ada_b[l])[:, None, :]
        sh1, sc1, g1, sh2, sc2, g2, sh3, sc3, g3 = jnp.split(mod, N_MOD_2, axis=-1)
        h = rmsnorm(x, norm_pre[l, 0]) * (1.0 + sc1) + sh1
        y = swiglu(h, ffn_w_gate[l, 0], ffn_w_up[l, 0], ffn_w_down[l, 0])
        x = x + 0.5 * g1 * rmsnorm(y, norm_post[l, 0])
        h = rmsnorm(x, norm_pre[l, 1]) * (1.0 + sc2) + sh2
        y = hybrid_mixer(h, mix_w_in[l], mix_b_in[l], mix_w_out[l], attn_sinks[l],
                         group_gain[l], rel_bias)
        x = x + g2 * rmsnorm(y, norm_post[l, 1])
        h = rmsnorm(x, norm_pre[l, 2]) * (1.0 + sc3) + sh3
        y = swiglu(h, ffn_w_gate[l, 1], ffn_w_up[l, 1], ffn_w_down[l, 1])
        x = x + 0.5 * g3 * rmsnorm(y, norm_post[l, 2])
    return x


def setup_inputs(seed=0):
    out = dict(first_inputs(seed))
    for name, value in second_inputs(seed + 1).items():
        if name != "x":
            out[name + "_2"] = value
    return out


def reference(
    x, c, mixer_norm_g, w_ada, b_ada, w_in, conv_w, conv_b, conv_ln_g, conv_ln_b, w_conv_out,
    b_conv_out, pool_w, pool_scale, w_out, ffn_norm_g, w_router_group, b_router_group,
    w_router_expert, b_router_expert, w_expert_gate, w_expert_up, w_expert_down, final_norm_g,
    c_2, rel_bias_2, ada_w_2, ada_b_2, norm_pre_2, norm_post_2, ffn_w_gate_2, ffn_w_up_2,
    ffn_w_down_2, mix_w_in_2, mix_b_in_2, mix_w_out_2, attn_sinks_2, group_gain_2,
):
    x = first_block(
        x, c, mixer_norm_g, w_ada, b_ada, w_in, conv_w, conv_b, conv_ln_g, conv_ln_b,
        w_conv_out, b_conv_out, pool_w, pool_scale, w_out, ffn_norm_g, w_router_group,
        b_router_group, w_router_expert, b_router_expert, w_expert_gate, w_expert_up,
        w_expert_down, final_norm_g,
    )
    return second_block(
        x, c_2, rel_bias_2, ada_w_2, ada_b_2, norm_pre_2, norm_post_2, ffn_w_gate_2, ffn_w_up_2,
        ffn_w_down_2, mix_w_in_2, mix_b_in_2, mix_w_out_2, attn_sinks_2, group_gain_2,
    )


_drawn_inputs = setup_inputs


def setup_inputs(seed=0):
    import zlib

    import numpy as np

    out = dict(_drawn_inputs(seed))
    spreads = {}
    factors = {'conv_b': 4.547,
     'conv_ln_g': 3.743,
     'conv_ln_b': 7.085,
     'b_conv_out': 5.677,
     'b_router_group': 27.118,
     'b_router_expert': 6.597,
     'mix_b_in_2': 5.396,
     'attn_sinks_2': 4.4,
     'group_gain_2': 7.184,
     'ada_b_2': 2.836}
    for name, (base, spread) in spreads.items():
        noise = np.random.default_rng([zlib.crc32(name.encode()), seed]).standard_normal(out[name].shape)
        drawn = base * np.exp(spread * noise) if base else spread * noise
        out[name] = __import__('jax').numpy.asarray(drawn.astype(out[name].dtype))
    for name, factor in factors.items():
        out[name] = (out[name] * factor).astype(out[name].dtype)
    return out
```

```python
import math
from contextlib import ExitStack

import numpy as np

import concourse.bass as bass
from concourse import mybir

F32 = mybir.dt.float32
ALU = mybir.AluOpType
ACT = mybir.ActivationFunctionType
X = mybir.AxisListType.X

P = 128
T = 256
D = 1024
KD = D // P
TH = T // P
L = 2
EPS = 1e-6

DC = 512
KC = DC // P
TAPS = 31
PAD = TAPS - 1
WINDOWS = (2, 4, 8, 16)
UPAD = 16
GRP = 4
EPG = 8
NE = GRP * EPG
NL = GRP + NE

HD = 64
NH = 16
SWA = 8
WIN = 128
BUCKETS = 32
MAX_DIST = 128
NEG = -1e30
UNITS_FF = 2816 // 256

RING = 4
BUF = 3 * KD * 256
COLS = 768
AC = COLS // P

ADA_1 = [0, 1, 2, 4, 6, 8, 10, 12]
WIN_1 = [3, 5, 7, 9, 11]
BRANCH_1, OUT_1, EXPERT_1 = 13, [14, 15], 16
UNITS_1 = 48
ADA_2 = [0, 1, 2, 3] + [6 + 2 * i for i in range(8)]
FFN_2A = [4, 5] + [7 + 2 * i for i in range(8)] + [22]
MIX_2, OUT_2, FFN_2B = [23, 24, 25], [26, 27, 28], 29
UNITS_2 = 40
assert UNITS_1 % RING == 0 and UNITS_2 % RING == 0

WIN_GROUPS = [[0, 2, 1], [3, 4, 5], [6, 7, 8], [9, 10, 11], [12, 13]]

ROWS_1 = dict(norm1=(0, 8), ada=(8, 48), conv_b=(56, 4), ln_g=(60, 4), ln_b=(64, 4), out_b=(68, 8),
              pool_s=(76, 8), norm2=(84, 8))
NR_1 = 92
ROWS_2 = dict(ada=(0, 72), pre=(72, 24), post=(96, 24))
NR_2 = 120
ROWS_3 = dict(q=(0, 4), k=(4, 1), qb=(5, 4), kb=(9, 4), gain=(13, 8))
NR_3 = 21
SMALL_1, SMALL_2 = 13, 14

NAMES = ("vec_t vec ada_acc ada_sum ada_mod sq sum std rstd hn h proj ev v conv ln1 lnc lnq ln2 lnd lnr lnz lns "
         "upad pooled yb_t yb ya_t ya mix o_t xm log_t log ada_part lexp comb_t comb row_t row "
         "gu sil prod cb act down xe mm qk vv S sc nm e p T pt pv y yn post xp end").split()


class Named(dict):

    def __getattr__(self, name):
        return self[name]


def build(nc, a, out, scratch):
    with ExitStack() as ctx:
        def sb(name, shape):
            return ctx.enter_context(nc.sbuf_tensor(name, shape, F32))

        def sem(name):
            return ctx.enter_context(nc.semaphore(name))

        ring = sb("ring", [P, RING, BUF])
        x = sb("x", [P, KD, T])
        h = sb("h", [P, KD, T])
        tA = sb("tA", [P, KD, T])
        arena = sb("arena", [P, 10560])
        silu = sb("silu", [P, 2, T])
        prod = sb("prod", [P, 2, 2, T])
        act = sb("act", [P, 2, 2, T])
        bias = sb("bias", [P, NH, T])
        acc = sb("acc", [P, 2, COLS])
        std = sb("std", [P, 2 * T])
        rstd = sb("rstd", [P, 2 * T])
        ident = sb("ident", [P, P])
        ones = sb("ones", [P, P])
        eps = sb("eps", [P, 1])
        invc = sb("invc", [P, KC, UPAD])
        stg = sb("stg", [P, 2, P])
        vec = sb("vec", [P, 2, P])
        mod = sb("mod", [P, 72])
        gs = sb("gs", [P, KD])
        cvec = sb("cvec", [P, 2 * KD])
        fvec = sb("fvec", [P, KD])
        wr = sb("wr", [P, KD, NL])
        rb = sb("rb", [P, NL])
        vbias = sb("vbias", [P, 640])
        sinks = sb("sinks", [P, SWA])
        rt = sb("rt", [P, 640])
        iota = sb("iota", [P, EPG])
        stat = sb("stat", [P, 4, 8])
        ps = ctx.enter_context(nc.psum_tensor("ps", [P, 8, 512], F32))

        def carve(at, *shape):
            n = int(np.prod(shape))
            v = arena[:, at:at + n]
            if len(shape) == 2:
                v = v.rearrange("p (a b) -> p a b", a=shape[0])
            return v, at + n
        ga, at = carve(0, KD, T)
        gb, at = carve(at, KD, T)
        vpad, at = carve(at, KC, PAD + T)
        cv, at = carve(at, KC, T)
        sg, at = carve(at, KC, T)
        upad, at = carve(at, KC, UPAD + T)
        w1, at = carve(at, KC, UPAD + T)
        w2, at = carve(at, KC, UPAD + T)
        assert at <= 10560
        comb_row = arena[0:1, 0:NE * T]
        comb_t = arena[0:NE, NE * T:NE * T + T]
        qa, at = carve(0, 4, T)
        ka, at = carve(at, 1, T)
        va, at = carve(at, TH, P)
        qb, at = carve(at, 4, T)
        kb, at = carve(at, 4, T)
        vb, at = carve(at, TH, 2 * T)
        yT, at = carve(at, KD, T)
        sc, at = carve(at, 4, 384)
        pr, at = carve(at, 4, 384)
        pt, at = carve(at, 2, 384)
        assert at <= 10560

        landed = [sem(f"landed{i}") for i in range(RING)]
        free = [sem(f"free{i}") for i in range(RING)]
        small = [sem("small1"), sem("small2")]
        first_in, consts, init_t, init_v, bias_w, bias_r, bias_m, out_s, out_e, fin = (
            sem(n) for n in "first_in consts init_t init_v bias_w bias_r bias_m out_s out_e fin".split())
        arrived, all_in, layer_go = sem("arrived"), sem("all_in"), sem("layer_go")
        cleared = [sem(n) for n in NAMES] + [sem(n) for n in ("act_own", "dve_own", "pool_own", "pe_own")]
        S = Named(**{n: s for n, s in zip(NAMES, cleared)})
        act_own, dve_own, pool_own, pe_own = cleared[-4:]

        block = ctx.enter_context(nc.Block())

        class Own:

            def __init__(self, eng, s):
                self.eng, self.s, self.n = eng, s, 0

            def __call__(self, ins):
                self.n += 1
                ins.then_inc(self.s, 1)

            def wait(self):
                self.eng.wait_ge(self.s, self.n)

            def link(self, ins):
                self(ins)
                self.wait()

        def turn(blk, l, unit):
            return l * ((UNITS_1, UNITS_2)[blk] // RING) + (0, L * UNITS_1 // RING)[blk] + unit // RING

        def wait_landed(eng, blk, l, unit, extra=0):
            eng.wait_ge(landed[unit % RING], (turn(blk, l, unit) + extra + 1) * 48)

        def boundary(eng, own, n, clears=False):
            eng.drain().then_inc(arrived, 1)
            if clears:
                eng.wait_ge(arrived, (n + 1) * 4)
                eng.sem_inc(all_in, 1)
                first, last = cleared[0].num, cleared[-1].num
                assert last - first == len(cleared) - 1
                eng.sem_clear(range(first, last + 1))
                eng.drain().then_inc(layer_go, 1)
            eng.wait_ge(layer_go, n + 1)
            own.n = 0

        def w3(unit):
            return ring[:, unit % RING, :].rearrange("p (g k n) -> p g k n", g=3, k=KD)

        def wada(unit):
            return ring[:, unit % RING, :].rearrange("p (k n) -> p k n", k=KD)

        def wdown(unit):
            return ring[:, unit % RING, 2 * KD * 256:].rearrange("p (c n) -> p c n", c=2)

        def row(v, blk_rows, name, i=0, n=1):
            at = blk_rows[name][0] + i
            return v[:, at:at + n]

        vA, vB = vec[:, 0, :], vec[:, 1, :]

        @block.sync
        def _(sp):
            def acquire(blk, l, unit, extra=0):
                sp.wait_ge(free[unit % RING], turn(blk, l, unit) + extra + 1)

            def send(unit, dst, src):
                sp.dma_start(dst, src).then_inc(landed[unit % RING], 16)

            def kpn(w, cols, k0=0, k1=KD):
                return w[:, k0 * P:k1 * P, cols].rearrange("a (k p) n -> p (a k) n", p=P)

            THIRDS = ((0, 3), (3, 6), (6, 8))

            def ada_unit(blk, l, w, u, extra=0, col=None):
                unit = (ADA_1, ADA_2)[blk][u]
                acquire(blk, l, unit, extra)
                cols = slice(u * COLS, (u + 1) * COLS) if col is None else bass.ds(col, COLS)
                for k0, k1 in THIRDS:
                    send(unit, wada(unit)[:, k0:k1, :], kpn(w[bass.ds(l, 1)], cols, k0, k1))

            def group_unit(blk, l, unit, w, groups):
                acquire(blk, l, unit)
                wl = w[bass.ds(l, 1)]
                for g, col in enumerate(groups):
                    cols = slice(col * 256, (col + 1) * 256)
                    last = g == len(groups) - 1
                    parts = ((0, KD),) if not last or len(groups) == 3 else (
                        ((0, 4), (4, 8)) if len(groups) == 2 else THIRDS)
                    for k0, k1 in parts:
                        send(unit, w3(unit)[:, g, k0:k1, :], kpn(wl, cols, k0, k1))

            def expert_unit(blk, l, unit, e, extra=0):
                acquire(blk, l, unit, extra)
                for g, w in enumerate((a.w_expert_gate, a.w_expert_up)):
                    send(unit, w3(unit)[:, g], w[bass.ds(l, 1), bass.ds(e, 1)].rearrange(
                        "a b (k p) n -> p (a b k) n", p=P))
                send(unit, wdown(unit), a.w_expert_down[bass.ds(l, 1), bass.ds(e, 1)].rearrange(
                    "a b (k p) n -> p (a b k) n", p=P))

            def ffn_unit(l, f, unit, e, extra=0):
                acquire(1, l, unit, extra)
                for g, w in enumerate((a.ffn_w_gate_2, a.ffn_w_up_2)):
                    send(unit, w3(unit)[:, g], w[bass.ds(l, 1), f, :, bass.ds(e * 256, 256)].rearrange(
                        "a (k p) n -> p (a k) n", p=P))
                send(unit, wdown(unit), a.ffn_w_down_2[bass.ds(l, 1), f, bass.ds(e * 256, 256), :].rearrange(
                    "a (k p) n -> p (a k) n", p=P))

            xin = tA[:].rearrange("p k t -> p (k t)").rearrange("p (h d) -> p h d", h=TH)
            sp.dma_start(stg[0:8, 0, :], a.c[0].rearrange("(k p) -> k p", p=P)).then_inc(first_in, 16)
            sp.dma_start(stg[8:16, 0, :], a.c_2[0].rearrange("(k p) -> k p", p=P)).then_inc(first_in, 16)
            sp.dma_start(stg[16:24, 0, :], a.final_norm_g.rearrange("(k p) -> k p", p=P)).then_inc(first_in, 16)
            sp.dma_start(xin, a.x[0].rearrange("(h p) d -> p h d", p=P)).then_inc(first_in, 16)
            sp.dma_start(rt[0:BUCKETS, 0:NH], a.rel_bias_2).then_inc(first_in, 16)
            sp.dma_start(rt[0:BUCKETS, 16:16 + 384], a.bucket_onehot).then_inc(first_in, 16)
            sp.dma_start(gb.rearrange("p k t -> p (k t)")[0:NH, 0:384], a.mask).then_inc(first_in, 16)
            with sp.Fori(0, L) as l:
                for u in range(3):
                    ada_unit(0, l, a.w_ada, u)
                group_unit(0, l, WIN_1[0], a.w_in, WIN_GROUPS[0])
                sp.wait_ge(layer_go, l + 1)
                lc = bass.ds(l, 1)

                def rows(name, src):
                    at, n = ROWS_1[name]
                    sp.dma_start(stg[at:at + n, 0, :], src[lc, :].rearrange("a (k p) -> (a k) p", p=P)
                                 ).then_inc(small[0], 16)
                rows("norm1", a.mixer_norm_g)
                rows("ada", a.b_ada)
                rows("conv_b", a.conv_b)
                rows("ln_g", a.conv_ln_g)
                rows("ln_b", a.conv_ln_b)
                rows("out_b", a.b_conv_out)
                rows("pool_s", a.pool_scale)
                rows("norm2", a.ffn_norm_g)
                sp.dma_start(stg[0:TAPS * KC, 1, :], a.conv_w[lc].rearrange("a j (c p) -> (a j c) p", p=P)
                             ).then_inc(small[0], 16)
                sp.dma_start(wr[:, :, 0:GRP], a.w_router_group[lc].rearrange("a (k p) n -> p (a k) n", p=P)
                             ).then_inc(small[0], 16)
                sp.dma_start(wr[:, :, GRP:NL], a.w_router_expert[lc].rearrange("a (k p) n -> p (a k) n", p=P)
                             ).then_inc(small[0], 16)
                sp.dma_start(rb[:, 0:GRP], a.b_router_group[lc, :].to_broadcast([P, GRP])).then_inc(small[0], 16)
                sp.dma_start(rb[:, GRP:NL], a.b_router_expert[lc, :].to_broadcast([P, NE])).then_inc(small[0], 16)
                for u in range(3, 8):
                    ada_unit(0, l, a.w_ada, u)
                    if u < 7:
                        group_unit(0, l, WIN_1[u - 2], a.w_in, WIN_GROUPS[u - 2])
                acquire(0, l, BRANCH_1)
                wo = ring[:, BRANCH_1 % RING, 0:4 * D].rearrange("p (k n) -> p k n", k=KC)
                for half in range(2):
                    cols = slice(half * 512, half * 512 + 512)
                    send(BRANCH_1, wo[:, :, cols], kpn(a.w_conv_out[lc], cols, 0, KC))
                send(BRANCH_1, ring[:, BRANCH_1 % RING, 4 * D:5 * D].rearrange("p (g n) -> p g n", g=KC),
                     a.pool_w[lc].rearrange("a g p n -> p (a g) n"))
                for j in range(2):
                    group_unit(0, l, OUT_1[j], a.w_out, [2 * j, 2 * j + 1])
                with sp.Fori(0, NE // RING) as i:
                    for j in range(RING):
                        expert_unit(0, l, EXPERT_1 + j, i * RING + j, i)

            with sp.Fori(0, L) as l:
                for u in range(4):
                    ada_unit(1, l, a.ada_w_2, u)
                sp.wait_ge(layer_go, l + L + 2)
                lc = bass.ds(l, 1)

                def put(dst, src):
                    sp.dma_start(dst, src).then_inc(small[1], 16)
                kp = "a (k p) -> (a k) p"
                put(stg[0:72, 0, :], a.ada_b_2[lc, :].rearrange(kp, p=P))
                put(stg[72:96, 0, :], a.norm_pre_2[lc].rearrange("a j (k p) -> (a j k) p", p=P))
                put(stg[96:120, 0, :], a.norm_post_2[lc].rearrange("a j (k p) -> (a j k) p", p=P))
                mb = a.mix_b_in_2
                put(stg[0:4, 1, 0:HD], mb[lc, 0:256].rearrange(kp, p=HD))
                put(stg[0:4, 1, HD:P], mb[lc, 256:512].rearrange(kp, p=HD))
                put(stg[4:5, 1, :], mb[lc, 512:640].rearrange(kp, p=P))
                put(stg[5:9, 1, :], mb[lc, 768:1280].rearrange(kp, p=P))
                put(stg[9:13, 1, :], mb[lc, 1280:1792].rearrange(kp, p=P))
                put(stg[13:21, 1, :], a.group_gain_2[lc, :].rearrange(kp, p=P))
                put(vbias[:, 0:P], mb[lc, 640:768].to_broadcast([P, P]))
                put(vbias[:, P:384], mb[lc, 1792:2048].to_broadcast([P, 256]))
                put(vbias[:, 384:640], mb[lc, 2048:2304].to_broadcast([P, 256]))
                put(sinks[:, 0:4], a.attn_sinks_2[lc, 0:4].to_broadcast([P, 4]))
                put(sinks[:, 4:8], a.attn_sinks_2[lc, 4:8].to_broadcast([P, 4]))
                ffn_unit(l, 0, FFN_2A[0], 0)
                ffn_unit(l, 0, FFN_2A[1], 1)
                with sp.Fori(0, 2) as i:
                    for j in range(4):
                        ada_unit(1, l, a.ada_w_2, 4 + j, i * 2, (i * 4 + 4 + j) * COLS)
                        ffn_unit(l, 0, FFN_2A[2 + j], i * 4 + 2 + j, i * 2)
                ffn_unit(l, 0, FFN_2A[10], 10)
                for u in range(3):
                    group_unit(1, l, MIX_2[u], a.mix_w_in_2, [3 * u, 3 * u + 1, 3 * u + 2])
                group_unit(1, l, OUT_2[0], a.mix_w_out_2, [0, 1])
                group_unit(1, l, OUT_2[1], a.mix_w_out_2, [2])
                group_unit(1, l, OUT_2[2], a.mix_w_out_2, [3])
                with sp.Fori(0, 2) as i:
                    for j in range(4):
                        ffn_unit(l, 1, FFN_2B + j, i * 4 + j, i)
                for e in range(8, UNITS_FF):
                    ffn_unit(l, 1, FFN_2B + e, e)
            sp.wait_ge(out_e, 4)
            otile = tA[:].rearrange("p k t -> p (k t)").rearrange("p (h d) -> p h d", h=TH)
            sp.dma_start(out[0].rearrange("(h p) d -> p h d", p=P), otile).then_inc(fin, 16)
            sp.wait_ge(fin, 16)

        @block.tensor
        def _(pe):
            own = Own(pe, pe_own)
            mm = nc.tensor.matmul

            def project(dst, wk, rhs, n=KD):
                for k in range(n):
                    last = mm(dst, wk(k), rhs(k), start=(k == 0), stop=(k == n - 1))
                return last

            def hk(k):
                return h[:, k, :]

            def sum_squares(n, parts=1, bank=2):
                for k in range(KD):
                    pe.wait_ge(S.sq, 8 * n + k + 1)
                    half = k * parts // KD
                    per = KD // parts
                    last = mm(ps[:, bank, half * T:half * T + T], ones[:], tA[:, k, :],
                              start=(k % per == 0), stop=(k % per == per - 1))
                last.then_inc(S.sum, 1)

            def ada_sum(n, slot, bank):
                pe.wait_ge(S.ada_acc, n + 1)
                for c in range(AC):
                    last = mm(ps[:, bank, c:c + 1], acc[:, slot, c * P:(c + 1) * P], ones[:, 0:1],
                              start=True, stop=True)
                last.then_inc(S.ada_sum, 1)

            def vectors(n_a, n_b):
                pe.transpose(ps[:, 4, 0:n_a], stg[0:n_a, 0, :], ident[0:n_a, 0:n_a])
                pe.transpose(ps[:, 4, 128:128 + n_b], stg[0:n_b, 1, :], ident[0:n_b, 0:n_b]).then_inc(S.vec_t, 1)

            def gate_up(blk, l, unit, extra, base):
                wait_landed(pe, blk, l, unit, extra)
                w = w3(unit)
                for c in range(2):
                    if base is not None:
                        pe.wait_ge(S.prod, base + c)
                    for g in range(2):
                        last = project(ps[:, c, g * T:(g + 1) * T], lambda k: w[:, g, k, c * P:(c + 1) * P], hk)
                    last.then_inc(S.gu, 1)

            def down(unit, slot, count, first=False, final=False):
                pe.wait_ge(S.act, count)
                w = wdown(unit)
                for d in range(KD):
                    for c in range(2):
                        last = mm(ps[:, 4 + d // 2, d % 2 * T:d % 2 * T + T], w[:, c, d * P:(d + 1) * P],
                                  act[:, slot, c, :], start=(first and c == 0 and d % 2 == 0),
                                  stop=(final and c == 1), skip_group_check=True)
                last.then_inc(S.down, 1)
                pe.wait_ge(S.down, count)
                pe.sem_inc(free[unit % RING], 1)

            for b in free[:3]:
                pe.sem_inc(b, 1)
            pe.wait_ge(first_in, 16 * 7)
            pe.wait_ge(consts, 4)
            pe.transpose(ps[:, 4, 0:24], stg[0:24, 0, :], ident[0:24, 0:24]).then_inc(init_t, 1)
            for k in range(KD):
                for hf in range(TH):
                    at = k * T + hf * P
                    last = pe.transpose(ps[:, at // 512, at % 512:at % 512 + P],
                                        tA[:].rearrange("p k t -> p (k t)")[:, hf * D + k * P:hf * D + (k + 1) * P],
                                        ident[:])
            last.then_inc(init_t, 1)
            mm(ps[0:NH, 5, 0:384], rt[0:BUCKETS, 0:NH], rt[0:BUCKETS, 16:400], start=True, stop=True
               ).then_inc(init_t, 1)
            pe.wait_ge(bias_r, 32)
            pe.wait_ge(init_v, 4)
            for i in range(NH // 2):
                if i >= 4:
                    pe.wait_ge(bias_m, i - 3)
                mm(ps[:, 4 + i % 4, :], act[:].rearrange("p a b t -> p (a b t)")[:, 0:P],
                   ring[:, 3, i * 512:(i + 1) * 512], start=True, stop=True).then_inc(init_t, 1)
            pe.wait_ge(init_t, 3 + NH // 2)
            pe.sem_inc(free[3], 1)
            boundary(pe, own, 0)

            with pe.Fori(0, L) as l:
                sum_squares(0, bank=6)
                pe.wait_ge(small[0], (l + 1) * (16 * SMALL_1))
                vectors(NR_1, TAPS * KC)
                for u in range(3):
                    if u:
                        pe.wait_ge(S.ada_mod, u)
                    ada_sum(u, u % 2, 5)

                def ada_later(u):
                    pe.wait_ge(S.ada_mod, u)
                    ada_sum(u, u % 2, 5)

                for i in range(14):
                    u, g = divmod(i, 3)
                    unit = WIN_1[u]
                    if g == 0:
                        wait_landed(pe, 0, l, unit)
                    if i == 4:
                        pe.wait_ge(S.v, 1)
                    elif i == 5:
                        pe.wait_ge(S.ev, 1)
                    elif i == 6:
                        pe.wait_ge(S.v, 2)
                    elif i == 7:
                        pe.wait_ge(S.ev, 2)
                    elif i >= 8:
                        pe.wait_ge(S.ev, i - 5)
                    for c in range(2):
                        if i == 0 and c == 0:
                            for k in range(KD):
                                pe.wait_ge(S.h, k + 1)
                                mm(ps[:, 0, 0:T], w3(unit)[:, 0, k, 0:P], hk(k), start=(k == 0), stop=(k == KD - 1))
                        else:
                            last = project(ps[:, i % 4, c * T:(c + 1) * T],
                                           lambda k: w3(unit)[:, g, k, c * P:(c + 1) * P], hk)
                    last.then_inc(S.proj, 1)
                    if g == 2 or i == 13:
                        pe.wait_ge(S.proj, i + 1)
                        pe.sem_inc(free[unit % RING], 1)
                    if i in (8, 12):
                        ada_later(3 + (i == 12))
                ada_later(5)
                pe.wait_ge(S.ev, 12)
                wait_landed(pe, 0, l, BRANCH_1)
                pw = ring[:, BRANCH_1 % RING, 4 * D:5 * D].rearrange("p (g n) -> p g n", g=KC)
                pe.wait_ge(S.pooled, 1)
                for g in range(KC):
                    for c in range(2):
                        last = mm(ps[:, g, c * T:(c + 1) * T], pw[:, g, c * P:(c + 1) * P], w1[:, g, UPAD:],
                                  start=True, stop=True)
                    last.then_inc(S.yb_t, 1)
                for c in range(KC):
                    pe.wait_ge(S.conv, c + 1)
                    last = mm(ps[:, 6, 0:T], ones[:], cv[:, c, :], start=(c == 0), stop=(c == KC - 1))
                last.then_inc(S.ln1, 1)
                for c in range(KC):
                    pe.wait_ge(S.lnq, c + 1)
                    last = mm(ps[:, 7, 0:T], ones[:], sg[:, c, :], start=(c == 0), stop=(c == KC - 1))
                last.then_inc(S.ln2, 1)
                wo = ring[:, BRANCH_1 % RING, 0:4 * D].rearrange("p (k n) -> p k n", k=KC)
                pe.wait_ge(S.lns, KC)
                for j in range(4):
                    pe.wait_ge(S.yb, 2 * j + 2)
                    for c in range(2):
                        at = (2 * j + c) * P
                        last = project(ps[:, j, c * T:(c + 1) * T], lambda k: wo[:, k, at:at + P],
                                       lambda k: cv[:, k, :], KC)
                    last.then_inc(S.ya_t, 1)
                pe.wait_ge(S.ya_t, 4)
                pe.sem_inc(free[BRANCH_1 % RING], 1)
                pe.wait_ge(S.mix, 4)
                for j in range(4):
                    unit = OUT_1[j // 2]
                    if j % 2 == 0:
                        wait_landed(pe, 0, l, unit)
                    for c in range(2):
                        last = project(ps[:, j, c * T:(c + 1) * T],
                                       lambda k: w3(unit)[:, j % 2, k, c * P:(c + 1) * P], lambda k: ga[:, k, :])
                    last.then_inc(S.o_t, 1)
                    if j % 2:
                        pe.wait_ge(S.o_t, j + 1)
                        pe.sem_inc(free[unit % RING], 1)
                sum_squares(1, bank=6)
                for u in (6, 7):
                    ada_later(u)
                for k in range(KD):
                    pe.wait_ge(S.h, KD + k + 1)
                for hf in range(TH):
                    last = project(ps[:, 4, hf * NL:(hf + 1) * NL], lambda k: h[:, k, hf * P:(hf + 1) * P],
                                   lambda k: wr[:, k, :])
                last.then_inc(S.log_t, 1)
                gate_up(0, l, EXPERT_1, 0, None)
                gate_up(0, l, EXPERT_1 + 1, 0, 1)
                pe.wait_ge(S.comb_t, 1)
                for hf in range(TH):
                    last = pe.transpose(ps[0:NE, 5, hf * P:(hf + 1) * P], rt[:, 400 + hf * NE:400 + (hf + 1) * NE],
                                        ident[:])
                last.then_inc(S.row_t, 1)

                def combine_row(slot, e):
                    mm(ps[:, 2 + slot, 0:T], ones[0:1, :], comb_row[:, bass.ds(e * T, T)], start=True, stop=True
                       ).then_inc(S.cb, 1)
                pe.wait_ge(S.row, 16)
                combine_row(0, 0)
                combine_row(1, 1)
                down(EXPERT_1, 0, 1, first=True)
                with pe.Fori(0, (NE - 4) // 4) as i:
                    for j in range(4):
                        gate_up(0, l, EXPERT_1 + 2 + j, i, i * 8 + 2 * j + 3)
                        combine_row(j % 2, i * 4 + j + 2)
                        down(EXPERT_1 + 1 + j, (1 + j) % 2, i * 4 + j + 2)
                for e in range(NE - 3, NE):
                    if e + 1 < NE:
                        gate_up(0, l, EXPERT_1 + e + 1, 0, 2 * e + 1)
                        combine_row((e + 1) % 2, e + 1)
                    down(EXPERT_1 + e, e % 2, e + 1, final=(e == NE - 1))
                boundary(pe, own, l + 1)

            sum_squares(0)
            boundary(pe, own, L + 1)

            with pe.Fori(0, L) as l:
                sum_squares(0)
                pe.wait_ge(small[1], (l + 1) * (16 * SMALL_2))
                vectors(NR_2, NR_3)
                for u in range(4):
                    if u:
                        pe.wait_ge(S.ada_mod, u)
                    ada_sum(u, u % 2, 3)
                for f in range(2):
                    base = UNITS_FF * f
                    units = FFN_2A if f == 0 else [FFN_2B + e for e in range(UNITS_FF)]
                    step = 2 if f == 0 else 1
                    if f:
                        sum_squares(5)
                    for k in range(KD):
                        pe.wait_ge(S.h, 16 * f + k + 1)
                    pe.wait_ge(S.vec, 1)
                    gate_up(1, l, units[0], 0, None)
                    gate_up(1, l, units[1], 0, 2 * base + 1)
                    down(units[0], base % 2, base + 1, first=True)
                    with pe.Fori(0, 2) as i:
                        for j in range(4):
                            gate_up(1, l, units[2 + j], i * step, i * 8 + 2 * (base + j) + 3)
                            down(units[1 + j], (base + 1 + j) % 2, i * 4 + base + j + 2)
                            if f == 0:
                                pe.wait_ge(S.ada_mod, i * 4 + j + 4)
                                ada_sum(i * 4 + j + 4, j % 2, 3)
                    gate_up(1, l, units[10], 0, 2 * (base + 9) + 1)
                    down(units[9], (base + 9) % 2, base + 10)
                    down(units[10], (base + 10) % 2, base + 11, final=True)
                    sum_squares(1 if f == 0 else 6)
                    if f:
                        continue
                    sum_squares(2)
                    for k in range(KD):
                        pe.wait_ge(S.h, KD + k + 1)
                    pe.wait_ge(S.ada_mod, 12)

                    def evicted(s, n):
                        pe.wait_ge(s, n)

                    def pair(bank, unit, g, c0):
                        for c in range(2):
                            last = project(ps[:, bank, c * T:(c + 1) * T],
                                           lambda k: w3(unit)[:, g, k, c * P:(c + 1) * P], hk)
                        last.then_inc(S.mm, 1)
                    m0, m1, m2 = MIX_2
                    wait_landed(pe, 1, l, m0)
                    for b in range(2):
                        for c in range(2):
                            at = (2 * b + c) * HD
                            for g in range(2):
                                last = project(ps[g * HD:(g + 1) * HD, b, c * T:(c + 1) * T],
                                               lambda k: w3(m0)[:, g, k, at:at + HD], hk)
                        last.then_inc(S.mm, 1)
                    project(ps[:, 2, 0:T], lambda k: w3(m0)[:, 2, k, 0:P], hk)
                    for hf in range(TH):
                        last = project(ps[:, 2, T + hf * P:T + (hf + 1) * P],
                                       lambda k: h[:, k, hf * P:(hf + 1) * P], lambda k: w3(m0)[:, 2, k, P:2 * P])
                    last.then_inc(S.mm, 1)
                    pe.wait_ge(S.mm, 3)
                    pe.sem_inc(free[m0 % RING], 1)
                    wait_landed(pe, 1, l, m1)
                    pair(3, m1, 0, 0)
                    evicted(S.qk, 1)
                    pair(0, m1, 1, 0)
                    evicted(S.qk, 2)
                    pair(1, m1, 2, 0)
                    pe.wait_ge(S.mm, 6)
                    pe.sem_inc(free[m1 % RING], 1)
                    wait_landed(pe, 1, l, m2)
                    evicted(S.vv, 1)
                    pair(2, m2, 0, 0)
                    for hf in range(TH):
                        evicted(S.qk, 4 + hf)
                        project(ps[:, 3 * (1 - hf), :], lambda k: h[:, k, hf * P:(hf + 1) * P],
                                lambda k: w3(m2)[:, 1:3, k, :]).then_inc(S.mm, 1)
                    pe.wait_ge(S.mm, 9)
                    pe.sem_inc(free[m2 % RING], 1)

                    def head(i):
                        if i < SWA:
                            r = HD * (i // 4)
                            return qa[r:r + HD, i % 4, :], ka[r:r + HD, 0, :], lambda b: va[:, b, r:r + HD]
                        m = i - SWA
                        r = HD * (m % 2)
                        return qb[r:r + HD, m // 2, :], kb[r:r + HD, m // 2, :], lambda b: vb[:, b, m * HD:(m + 1) * HD]

                    evicted(S.qk, 7)
                    evicted(S.vv, 3)
                    for i in range(NH + 3):
                        if i < NH:
                            q, k, _ = head(i)
                            if i >= 2:
                                pe.wait_ge(S.sc, i - 1)
                            mm(ps[:, 4 + i % 2, 0:T], q[:, P:T], k, start=True, stop=True)
                            mm(ps[:, 4 + i % 2, T:384], q[:, 0:P], k[:, 0:P], start=True, stop=True).then_inc(S.S, 1)
                        t = i - 2
                        if 0 <= t < NH:
                            pe.wait_ge(S.p, t + 1)
                            if t >= 2:
                                pe.wait_ge(S.pt, t - 1)
                            for n, at in enumerate((T, 0, P)):
                                last = pe.transpose(ps[:, 6 + t % 2, n * P:(n + 1) * P], pr[:, t % 4, at:at + P],
                                                    ident[:])
                            last.then_inc(S.T, 1)
                        t = i - 3
                        if t >= 0:
                            _, _, v = head(t)
                            pe.wait_ge(S.pt, t + 1)
                            if t % 2 == 0 and t >= 4:
                                pe.wait_ge(S.y, t // 2 - 1)
                            r = HD * (t % 2)
                            bank = t // 2 % 2
                            mm(ps[r:r + HD, bank, 0:T], v(0), pt[:, t % 2, 0:T], start=True, stop=False)
                            mm(ps[r:r + HD, bank, P:T], v(1), pt[:, t % 2, T:384], start=False, stop=True
                               ).then_inc(S.pv, 1)
                    sum_squares(3, 2)
                    for k in range(KD):
                        pe.wait_ge(S.yn, k + 1)
                    for c in range(KD):
                        unit, g = ((OUT_2[0], c // 2), (OUT_2[1], 0), (OUT_2[2], 0))[max(0, c // 2 - 1)]
                        if c in (0, 4, 6):
                            wait_landed(pe, 1, l, unit)
                        project(ps[:, 4 + c // 2, c % 2 * T:c % 2 * T + T],
                                lambda k: w3(unit)[:, g, k, c % 2 * P:c % 2 * P + P], lambda k: yT[:, k, :]
                                ).then_inc(S.mm, 1)
                        if c in (3, 5, 7):
                            pe.wait_ge(S.mm, 9 + c + 1)
                            pe.sem_inc(free[unit % RING], 1)
                    sum_squares(4)
                boundary(pe, own, l + L + 2)

            for hf in range(TH):
                for k in range(KD):
                    at = hf * D + k * P
                    last = pe.transpose(ps[:, at // 512, at % 512:at % 512 + P], x[:, k, hf * P:(hf + 1) * P], ident[:])
                    if k % 4 == 3:
                        last.then_inc(out_s, 1)

        @block.scalar
        def _(eng):
            own = Own(eng, act_own)
            act_ = nc.scalar.activation

            def squares(n, src, ready, first, each=1):
                for k in range(KD):
                    if ready is not None:
                        eng.wait_ge(ready, first + k * each)
                    act_(tA[:, k, :], src(k), ACT.Square).then_inc(S.sq, 1)

            def root(n, width=D, bank=2, cols=T):
                eng.wait_ge(S.sum, n + 1)
                act_(std[:, 0:cols], ps[:, bank, 0:cols], ACT.Sqrt, bias=eps[:, 0:1], scale=1.0 / width
                     ).then_inc(S.std, 1)

            def shift(p, at, mods):
                eng.wait_ge(S.ada_mod, mods)
                for k in range(KD):
                    eng.wait_ge(S.hn, KD * p + k + 1)
                    act_(h[:, k, :], h[:, k, :], ACT.Identity, bias=mod[:, at + k:at + k + 1]).then_inc(S.h, 1)

            def xk(k):
                return x[:, k, :]

            def silu_chunk(c, count):
                eng.wait_ge(S.gu, count)
                act_(silu[:, c, :], ps[:, c, 0:T], ACT.Silu).then_inc(S.sil, 1)

            eng.wait_ge(init_t, 1)
            act_(cvec[:], ps[:, 4, 0:16], ACT.Silu).then_inc(init_v, 1)
            eng.wait_ge(init_v, 1)
            act_(fvec[:], ps[:, 4, 16:24], ACT.Identity).then_inc(init_v, 1)
            eng.wait_ge(bias_w, 1)
            eng.dma_start(scratch, ga.rearrange("p k t -> p (k t)")[0:NH, 0:384]).then_inc(bias_r, 16)
            eng.wait_ge(bias_r, 16)
            toeplitz = bass.AP(scratch.tensor, 0, [[1, P], [384, NH], [1, T]])
            eng.dma_start(ring[:, 3, 0:NH * T].rearrange("p (h t) -> p h t", h=NH), toeplitz).then_inc(bias_r, 16)
            boundary(eng, own, 0)

            with eng.Fori(0, L) as l:
                squares(0, xk, None, 0)
                root(0, bank=6)
                shift(0, 0, 3)
                n = 0
                for pair in range(2):
                    eng.wait_ge(S.proj, 2 + 2 * pair)
                    act_(sg[:, 2 * pair:2 * pair + 2, :], ps[:, 1 + 2 * pair, :].rearrange("p (c t) -> p c t", c=2),
                         ACT.Sigmoid).then_inc(S.ev, 1)
                for pair in range(2):
                    eng.wait_ge(S.proj, 5 + pair)
                    eng.wait_ge(S.upad, 1)
                    act_(upad[:, 2 * pair:2 * pair + 2, UPAD:], ps[:, pair, :].rearrange("p (c t) -> p c t", c=2),
                         ACT.Identity).then_inc(S.ev, 1)
                for i in range(6, 14):
                    eng.wait_ge(S.proj, i + 1)
                    gate, j = (ga, i - 6) if i < 10 else (gb, i - 10)
                    act_(gate[:, 2 * j:2 * j + 2, :], ps[:, i % 4, :].rearrange("p (c t) -> p c t", c=2),
                         ACT.Sigmoid).then_inc(S.ev, 1)
                for c in range(KC):
                    eng.wait_ge(S.lnc, c + 1)
                    act_(sg[:, c, :], cv[:, c, :], ACT.Square).then_inc(S.lnq, 1)
                eng.wait_ge(S.ln2, 1)
                act_(std[:, 0:T], ps[:, 7, 0:T], ACT.Sqrt, bias=eps[:, 0:1], scale=1.0 / DC).then_inc(S.lnd, 1)
                for c in range(KC):
                    eng.wait_ge(S.lnz, c + 1)
                    act_(cv[:, c, :], cv[:, c, :], ACT.Silu, bias=row(vA, ROWS_1, "ln_b", c),
                         scale=row(vA, ROWS_1, "ln_g", c)).then_inc(S.lns, 1)
                squares(1, xk, S.xm, 1)
                root(1, bank=6)
                shift(1, 24, 6)
                eng.wait_ge(S.log, 1)
                act_(rt[:, 80:88], rt[:, 72:80], ACT.Exp).then_inc(S.lexp, 1)
                eng.wait_ge(S.log, 2)
                act_(rt[:, 90:92], rt[:, 88:90], ACT.Exp).then_inc(S.lexp, 1)
                for e in range(2):
                    for c in range(2):
                        silu_chunk(c, 2 * e + c + 1)
                eng.wait_ge(S.row_t, 1)
                act_(comb_t, ps[0:NE, 5, 0:T], ACT.Identity).then_inc(S.comb, 1)
                eng.wait_ge(S.comb, 1)
                eng.dma_start(comb_row, comb_t).then_inc(S.row, 16)
                with eng.Fori(2, NE) as i:
                    for c in range(2):
                        silu_chunk(c, i * 2 + c + 1)
                boundary(eng, own, l + 1)

            squares(0, xk, None, 0)
            root(0)
            boundary(eng, own, L + 1)

            with eng.Fori(0, L) as l:
                squares(0, xk, None, 0)
                root(0)
                shift(0, 0, 3)
                for f in range(2):
                    if f:
                        squares(5, xk, S.xp, 9)
                        root(5)
                        shift(2, 48, 12)
                    with eng.Fori(0, UNITS_FF) as i:
                        for c in range(2):
                            silu_chunk(c, i * 2 + 2 * UNITS_FF * f + c + 1)
                    eng.wait_ge(S.down, UNITS_FF * (f + 1))
                    n = 6 * f + (1 - f)
                    squares(n, lambda k: ps[:, 4 + k // 2, k % 2 * T:k % 2 * T + T], None, 0)
                    root(n)
                    if f:
                        continue
                    squares(2, xk, S.xp, 1)
                    root(2)
                    shift(1, 24, 7)
                    tiles = [(qa, 0, 0, "q"), (qa, 2, 1, "q"), (ka, 0, 2, "k"), (qb, 0, 3, "qb"), (qb, 2, 0, "qb"),
                             (kb, 0, 1, "kb"), (kb, 2, 2, "kb")]
                    for n, (dst, c0, bank, name) in enumerate(tiles):
                        eng.wait_ge(S.mm, n + 1)
                        cs = range(1 if name == "k" else 2)
                        for c in cs:
                            last = act_(dst[:, c0 + c, :], ps[:, bank, c * T:(c + 1) * T], ACT.Identity,
                                        bias=row(vB, ROWS_3, name, c0 + c))
                        last.then_inc(S.qk, 1)
                    for i in range(NH + 3):
                        if i < NH:
                            st = stat[:, i % 4, :]
                            eng.wait_ge(S.nm, i + 1)
                            act_(pr[:, i % 4, 0:T], sc[:, i % 4, 0:T], ACT.Exp, bias=st[:, 2:3], accum_out=st[:, 4:5])
                            last = act_(pr[:, i % 4, T:384], sc[:, i % 4, T:384], ACT.Exp, bias=st[:, 3:4],
                                        accum_out=st[:, 5:6])
                            if i < SWA:
                                own(last)
                                last = act_(st[:, 6:8], st[:, 2:4], ACT.Exp, bias=sinks[:, i:i + 1])
                            last.then_inc(S.e, 1)
                        t = i - 2
                        if 0 <= t < NH:
                            eng.wait_ge(S.T, t + 1)
                            if t >= 2:
                                eng.wait_ge(S.pv, t - 1)
                            act_(pt[:, t % 2, :], ps[:, 6 + t % 2, 0:384], ACT.Identity).then_inc(S.pt, 1)
                        t = i - 3
                        if t >= 0 and t % 2:
                            eng.wait_ge(S.pv, t + 1)
                            act_(yT[:, t // 2, :], ps[:, t // 2 % 2, 0:T], ACT.Identity).then_inc(S.y, 1)
                    squares(3, lambda k: yT[:, k, :], S.y, 1)
                    root(3, DC, 2, 2 * T)
                    squares(4, lambda k: ps[:, 4 + k // 2, k % 2 * T:k % 2 * T + T], S.mm, 9 + 8, 0)
                    root(4)
                boundary(eng, own, l + L + 2)

            for j in range(4):
                eng.wait_ge(out_s, j + 1)
                act_(tA[:].rearrange("p k t -> p (k t)")[:, j * 512:(j + 1) * 512], ps[:, j, :], ACT.Identity
                     ).then_inc(out_e, 1)

        @block.vector
        def _(eng):
            v_ = nc.vector
            own = Own(eng, dve_own)

            def ada_unit(blk, l, unit, n, slot, cond, extra=0):
                wait_landed(eng, blk, l, unit, extra)
                w = wada(unit)
                if not isinstance(n, int) or n >= 2:
                    eng.wait_ge(S.ada_sum, n - 1)
                last = v_.tensor_scalar(acc[:, slot, :], w[:, 0, :], cvec[:, cond:cond + 1], None, ALU.mult)
                for k in range(1, KD):
                    last.then_inc(S.ada_part, 1)
                    eng.wait_ge(S.ada_part, n * (KD - 1) + k)
                    last = v_.scalar_tensor_tensor(acc[:, slot, :], w[:, k, :], cvec[:, cond + k:cond + k + 1],
                                                   acc[:, slot, :], ALU.mult, ALU.add)
                last.then_inc(S.ada_acc, 1)
                eng.wait_ge(S.ada_acc, n + 1)
                eng.sem_inc(free[unit % RING], 1)

            def ada_mod(n, bias_at, bank):
                eng.wait_ge(S.ada_sum, n + 1)
                v_.tensor_tensor(mod[:, bass.ds(n * AC, AC)], ps[:, bank, 0:AC], vA[:, bass.ds(n * AC + bias_at, AC)],
                                 ALU.add).then_inc(S.ada_mod, 1)

            def invert(n, cols=T):
                eng.wait_ge(S.std, n + 1)
                v_.reciprocal(rstd[:, 0:cols], std[:, 0:cols]).then_inc(S.rstd, 1)

            def normalize(n, p, scale_at, gain):
                own.link(v_.scalar_tensor_tensor(gs[:], mod[:, scale_at:scale_at + KD], 1.0, gain, ALU.add, ALU.mult))
                eng.wait_ge(S.rstd, n + 1)
                for k in range(KD):
                    v_.scalar_tensor_tensor(h[:, k, :], x[:, k, :], gs[:, k:k + 1], rstd[:, 0:T], ALU.mult, ALU.mult
                                            ).then_inc(S.hn, 1)

            def product(dst, c, count):
                eng.wait_ge(S.sil, count)
                v_.tensor_tensor(dst, silu[:, c, :], ps[:, c, T:2 * T], ALU.mult).then_inc(S.prod, 1)

            def copy_vectors(n_a, n_b):
                eng.wait_ge(S.vec_t, 1)
                own(v_.tensor_copy(vA[:, 0:n_a], ps[:, 4, 0:n_a]))
                own(v_.tensor_copy(vB[:, 0:n_b], ps[:, 4, 128:128 + n_b]))
                own.wait()

            v_.memset(ones[:], 1.0).then_inc(consts, 1)
            v_.memset(eps[:], EPS).then_inc(consts, 1)
            eng.wait_ge(init_t, 2)
            xf = x[:].rearrange("p k t -> p (k t)")
            eng.wait_ge(init_v, 2)
            for j in range(4):
                last = v_.tensor_copy(xf[:, j * 512:(j + 1) * 512], ps[:, j, :])
            last.then_inc(init_v, 1)
            eng.wait_ge(init_t, 3)
            v_.tensor_tensor(ga.rearrange("p k t -> p (k t)")[0:NH, 0:384], ps[0:NH, 5, 0:384],
                             gb.rearrange("p k t -> p (k t)")[0:NH, 0:384], ALU.add).then_inc(bias_w, 1)
            eng.wait_ge(bias_w, 1)
            eng.sem_inc(init_v, 1)
            for i in range(NH // 2):
                eng.wait_ge(init_t, 4 + i)
                v_.tensor_copy(bias[:, 2 * i:2 * i + 2, :], ps[:, 4 + i % 4, :].rearrange("p (c t) -> p c t", c=2)
                               ).then_inc(bias_m, 1)
            boundary(eng, own, 0, clears=True)

            with eng.Fori(0, L) as l:
                def ada1(u):
                    ada_unit(0, l, ADA_1[u], u, u % 2, 0)

                def mod1(u):
                    ada_mod(u, ROWS_1["ada"][0], 5)

                v_.memset(vpad[:, :, 0:PAD], 0.0)
                ada1(0)
                invert(0)
                copy_vectors(NR_1, TAPS * KC)
                mod1(0)
                ada1(1)
                mod1(1)
                ada1(2)
                mod1(2)
                eng.wait_ge(S.ada_mod, 3)
                normalize(0, 0, 8, row(vA, ROWS_1, "norm1", 0, KD))

                def glu(pair):
                    eng.wait_ge(S.ev, 1 + pair)
                    v_.tensor_tensor(vpad[:, 2 * pair:2 * pair + 2, PAD:], sg[:, 2 * pair:2 * pair + 2, :],
                                     ps[:, 2 * pair, :].rearrange("p (c t) -> p c t", c=2), ALU.mult
                                     ).then_inc(S.v, 1)
                    eng.wait_ge(S.v, pair + 1)

                def conv(c):
                    own(v_.tensor_scalar(cv[:, c, :], vpad[:, c, 0:T], vB[:, c:c + 1],
                                         row(vA, ROWS_1, "conv_b", c), ALU.mult, ALU.add))
                    for j in range(1, TAPS):
                        own.wait()
                        last = v_.scalar_tensor_tensor(cv[:, c, :], vpad[:, c, j:j + T],
                                                       vB[:, j * KC + c:j * KC + c + 1], cv[:, c, :],
                                                       ALU.mult, ALU.add)
                        if j < TAPS - 1:
                            own(last)
                    last.then_inc(S.conv, 1)
                glu(0)
                conv(0)
                glu(1)
                ada1(3)
                conv(1)
                mod1(3)
                ada1(4)
                conv(2)
                mod1(4)
                ada1(5)
                conv(3)
                mod1(5)
                for j in range(KD):
                    eng.wait_ge(S.yb_t, j // 2 + 1)
                    v_.scalar_tensor_tensor(gb[:, j, :], ps[:, j // 2, j % 2 * T:j % 2 * T + T],
                                            row(vA, ROWS_1, "pool_s", j), gb[:, j, :], ALU.mult, ALU.mult
                                            ).then_inc(S.yb, 1)
                eng.wait_ge(S.ln1, 1)
                for c in range(KC):
                    v_.scalar_tensor_tensor(cv[:, c, :], ps[:, 6, 0:T], -1.0 / DC, cv[:, c, :], ALU.mult, ALU.add
                                            ).then_inc(S.lnc, 1)
                ada1(6)
                eng.wait_ge(S.lnd, 1)
                own.link(v_.reciprocal(rstd[:, 0:T], std[:, 0:T]))
                for c in range(KC):
                    v_.tensor_tensor(cv[:, c, :], cv[:, c, :], rstd[:, 0:T], ALU.mult).then_inc(S.lnz, 1)
                for j in range(KD):
                    eng.wait_ge(S.ya_t, j // 2 + 1)
                    v_.scalar_tensor_tensor(ga[:, j, :], ps[:, j // 2, j % 2 * T:j % 2 * T + T],
                                            row(vA, ROWS_1, "out_b", j), ga[:, j, :], ALU.add, ALU.mult
                                            ).then_inc(S.ya, 1)
                eng.wait_ge(S.ada_mod, 6)
                for j in range(KD):
                    eng.wait_ge(S.o_t, j // 2 + 1)
                    v_.scalar_tensor_tensor(x[:, j, :], ps[:, j // 2, j % 2 * T:j % 2 * T + T],
                                            mod[:, 16 + j:17 + j], x[:, j, :], ALU.mult, ALU.add
                                            ).then_inc(S.xm, 1)
                invert(1)
                mod1(6)
                eng.wait_ge(S.ada_mod, 7)
                normalize(1, 1, 32, row(vA, ROWS_1, "norm2", 0, KD))
                ada1(7)
                mod1(7)

                lg = rt[:, 0:72].rearrange("p (h n) -> p h n", h=TH)
                dg, eg = rt[:, 72:80], rt[:, 80:88]
                d2, e2 = rt[:, 88:90], rt[:, 90:92]
                gmax, gsum, gmin = rt[:, 92:94], rt[:, 94:96], rt[:, 96:98]
                m1, c1, m2, c2 = (rt[:, 98 + 2 * i:100 + 2 * i] for i in range(4))
                wa, wb = rt[:, 106:108], rt[:, 108:110]
                og = rt[:, 112:120].rearrange("p (h n) -> p h n", h=TH)
                o1, o2, tin, cand = (rt[:, 120 + 16 * i:136 + 16 * i].rearrange("p (h n) -> p h n", h=TH)
                                     for i in range(4))
                cm8 = rt[:, 184:200].rearrange("p (h n) -> p h n", h=TH)
                cg = rt[:, 200:208].rearrange("p (h n) -> p h n", h=TH)
                sel = rt[:, 208:272].rearrange("p (h g e) -> p h g e", h=TH, g=GRP)
                comb = rt[:, 400:464].rearrange("p (h g e) -> p h g e", h=TH, g=GRP)

                def wide(v, n):
                    return v.unsqueeze(2).to_broadcast([P, TH, n])

                def first_of(dst, values, top, c, tmp, n):
                    own.link(v_.tensor_tensor(tmp, values, wide(top, n), ALU.is_equal))
                    for hf in range(TH):
                        own(v_.scalar_tensor_tensor(tmp[:, hf, :], tmp[:, hf, :], -64.0, iota[:, 0:n],
                                                    ALU.mult, ALU.add))
                    own.wait()
                    own.link(v_.tensor_reduce(c, tmp, X, ALU.min))
                    for hf in range(TH):
                        own(v_.tensor_scalar(tmp[:, hf, :], tmp[:, hf, :], c[:, hf:hf + 1], None, ALU.is_equal))
                    own.wait()
                    own.link(v_.tensor_copy(dst, tmp))

                eng.wait_ge(S.log_t, 1)
                for hf in range(TH):
                    own(v_.tensor_tensor(lg[:, hf, :], ps[:, 4, hf * NL:(hf + 1) * NL], rb[:], ALU.add))
                own.wait()
                own.link(v_.tensor_reduce(gmax, lg[:, :, 0:GRP], X, ALU.max))
                v_.tensor_tensor(dg.rearrange("p (h n) -> p h n", h=TH), lg[:, :, 0:GRP], wide(gmax, GRP),
                                 ALU.subtract).then_inc(S.log, 1)
                first_of(og, lg[:, :, 0:GRP], gmax, gmin, cg, GRP)
                for hf in range(TH):
                    for g in range(GRP):
                        own(v_.tensor_scalar(sel[:, hf, g, :], lg[:, hf, GRP + g * EPG:GRP + (g + 1) * EPG],
                                             og[:, hf, g:g + 1], None, ALU.mult))
                own.wait()
                own.link(v_.tensor_reduce(tin, sel.rearrange("p h g e -> p h e g"), X, ALU.add))
                own.link(v_.tensor_reduce(m1, tin, X, ALU.max))
                first_of(o1, tin, m1, c1, cand, EPG)
                own.link(v_.scalar_tensor_tensor(tin, o1, -3e38, tin, ALU.mult, ALU.add))
                own.link(v_.tensor_reduce(m2, tin, X, ALU.max))
                v_.tensor_tensor(d2, m2, m1, ALU.subtract).then_inc(S.log, 1)
                first_of(o2, tin, m2, c2, cand, EPG)
                eng.wait_ge(S.lexp, 2)
                own.link(v_.tensor_reduce(gsum, eg.rearrange("p (h n) -> p h n", h=TH), X, ALU.add))
                own.link(v_.scalar_tensor_tensor(wa, e2, 1.0, gsum, ALU.add, ALU.mult))
                own.link(v_.reciprocal(wa, wa))
                own.link(v_.tensor_tensor(wb, wa, e2, ALU.mult))
                for hf in range(TH):
                    own.link(v_.tensor_scalar(cm8[:, hf, :], o1[:, hf, :], wa[:, hf:hf + 1], None, ALU.mult))
                    own.link(v_.scalar_tensor_tensor(cm8[:, hf, :], o2[:, hf, :], wb[:, hf:hf + 1], cm8[:, hf, :],
                                                     ALU.mult, ALU.add))
                for hf in range(TH):
                    for g in range(GRP):
                        last = v_.tensor_scalar(comb[:, hf, g, :], cm8[:, hf, :], og[:, hf, g:g + 1], None, ALU.mult)
                last.then_inc(S.comb_t, 1)

                def expert(slot, c2_, e, held=True):
                    for c in range(2):
                        product(prod[:, slot, c, :], c, c2_ + c + 1)
                    eng.wait_ge(S.prod, c2_ + 2)
                    eng.wait_ge(S.cb, e + 1)
                    if held:
                        eng.wait_ge(S.down, e - 1)
                    v_.tensor_tensor(act[:, slot], prod[:, slot],
                                     ps[:, 2 + slot, 0:T].unsqueeze(1).to_broadcast([P, 2, T]), ALU.mult
                                     ).then_inc(S.act, 1)
                expert(0, 0, 0, False)
                expert(1, 2, 1, False)
                with eng.Fori(1, NE // 2) as i:
                    for j in range(2):
                        expert(j, i * 4 + 2 * j, i * 2 + j)
                eng.wait_ge(S.down, NE)
                eng.wait_ge(S.ada_mod, 8)
                for k in range(KD):
                    v_.scalar_tensor_tensor(x[:, k, :], ps[:, 4 + k // 2, k % 2 * T:k % 2 * T + T],
                                            mod[:, 40 + k:41 + k], x[:, k, :], ALU.mult, ALU.add)
                boundary(eng, own, l + 1, clears=True)

            invert(0)
            eng.wait_ge(S.rstd, 1)
            for k in range(KD):
                v_.scalar_tensor_tensor(x[:, k, :], x[:, k, :], fvec[:, k:k + 1], rstd[:, 0:T], ALU.mult, ALU.mult)
            boundary(eng, own, L + 1, clears=True)

            with eng.Fori(0, L) as l:
                def mod2(n):
                    ada_mod(n, 0, 3)

                def post(n, j, factor, gate_at, ready=None):
                    own.link(v_.scalar_tensor_tensor(gs[:], mod[:, gate_at:gate_at + KD], factor,
                                                     vA[:, 96 + 8 * j:104 + 8 * j], ALU.mult, ALU.mult))
                    invert(n)
                    eng.wait_ge(S.rstd, n + 1)
                    for k in range(KD):
                        v_.scalar_tensor_tensor(h[:, k, :], ps[:, 4 + k // 2, k % 2 * T:k % 2 * T + T],
                                                gs[:, k:k + 1], rstd[:, 0:T], ALU.mult, ALU.mult
                                                ).then_inc(S.post, 1)

                ada_unit(1, l, ADA_2[0], 0, 0, KD)
                invert(0)
                copy_vectors(NR_2, NR_3)
                v_.memset(iota[:, 0:1], 0.0).then_inc(S.vec, 1)
                mod2(0)
                for u in range(1, 4):
                    ada_unit(1, l, ADA_2[u], u, u % 2, KD)
                    mod2(u)
                eng.wait_ge(S.ada_mod, 3)
                normalize(0, 0, 8, vA[:, 72:80])
                for f in range(2):
                    base = UNITS_FF * f
                    if f:
                        invert(5)
                        normalize(5, 2, 56, vA[:, 88:96])

                    def ffn(e, slot):
                        if not isinstance(e, int) or e >= 2:
                            eng.wait_ge(S.down, e - 1)
                        for c in range(2):
                            product(act[:, slot, c, :], c, e * 2 + c + 1)
                        eng.wait_ge(S.prod, e * 2 + 2)
                        eng.sem_inc(S.act, 1)
                    for e in range(3):
                        ffn(base + e, (base + e) % 2)
                    with eng.Fori(0, 2) as i:
                        for j in range(4):
                            if f == 0:
                                ada_unit(1, l, ADA_2[4 + j], i * 4 + 4 + j, j % 2, KD, i * 2)
                            ffn(i * 4 + base + 3 + j, (base + 3 + j) % 2)
                            if f == 0:
                                mod2(i * 4 + 4 + j)
                    post(1 if f == 0 else 6, 2 * f, 0.5, 16 + 48 * f)
                    if f:
                        continue
                    invert(2)
                    normalize(2, 1, 32, vA[:, 80:88])
                    eng.wait_ge(S.qk, 3)
                    for hf in range(TH):
                        last = v_.tensor_tensor(va[:, hf, :], ps[:, 2, T + hf * P:T + (hf + 1) * P], vbias[:, 0:P],
                                                ALU.add)
                    last.then_inc(S.vv, 1)
                    for hf in range(TH):
                        eng.wait_ge(S.mm, 8 + hf)
                        v_.tensor_tensor(vb[:, hf, :], ps[:, 3 * (1 - hf), :], vbias[:, P:], ALU.add
                                         ).then_inc(S.vv, 1)
                    for i in range(NH + 1):
                        if i < NH:
                            st = stat[:, i % 4, :]
                            bank = ps[:, 4 + i % 2, :]
                            eng.wait_ge(S.S, i + 1)
                            own(v_.scalar_tensor_tensor(sc[:, i % 4, 0:T], bank[:, 0:T], HD ** -0.5, bias[:, i, :],
                                                        ALU.mult, ALU.add))
                            v_.scalar_tensor_tensor(sc[:, i % 4, T:384], bank[:, T:384], HD ** -0.5,
                                                    bias[:, i, P:T], ALU.mult, ALU.add).then_inc(S.sc, 1)
                            eng.wait_ge(S.sc, i + 1)
                            own(v_.tensor_reduce(st[:, 0:1], sc[:, i % 4, 0:T], X, ALU.max))
                            own.link(v_.tensor_reduce(st[:, 1:2], sc[:, i % 4, T:384], X, ALU.max))
                            if i < SWA:
                                last = v_.tensor_scalar(st[:, 2:4], st[:, 0:2], sinks[:, i:i + 1], -1.0,
                                                        ALU.max, ALU.mult)
                            else:
                                last = v_.tensor_scalar(st[:, 2:4], st[:, 0:2], -1.0, None, ALU.mult)
                            last.then_inc(S.nm, 1)
                        t = i - 1
                        if t >= 0:
                            st = stat[:, t % 4, :]
                            eng.wait_ge(S.e, t + 1)
                            if t < SWA:
                                own.link(v_.tensor_tensor(st[:, 4:6], st[:, 4:6], st[:, 6:8], ALU.add))
                            own.link(v_.reciprocal(st[:, 4:6], st[:, 4:6]))
                            v_.tensor_scalar(pr[:, t % 4, 0:T], pr[:, t % 4, 0:T], st[:, 4:5], None, ALU.mult)
                            v_.tensor_scalar(pr[:, t % 4, T:384], pr[:, t % 4, T:384], st[:, 5:6], None, ALU.mult
                                             ).then_inc(S.p, 1)
                    invert(3, 2 * T)
                    eng.wait_ge(S.rstd, 4)
                    for k in range(KD):
                        v_.scalar_tensor_tensor(yT[:, k, :], yT[:, k, :], row(vB, ROWS_3, "gain", k),
                                                rstd[:, k // 4 * T:k // 4 * T + T], ALU.mult, ALU.mult
                                                ).then_inc(S.yn, 1)
                    post(4, 1, 1.0, 40)
                boundary(eng, own, l + L + 2, clears=True)

        @block.gpsimd
        def _(eng):
            g_ = nc.gpsimd
            own = Own(eng, pool_own)
            tmp = act[:].rearrange("p a b t -> p (a b t)")[:, 0:P]
            own(g_.memset(ident[:], 0.0))
            own(g_.memset(tmp, 0.0))
            own.wait()
            g_.affine_select(out=ident[:], in_=ident[:], compare_op=ALU.not_equal, fill=1.0, base=0,
                             pattern=[[-1, P]], channel_multiplier=1).then_inc(consts, 1)
            g_.affine_select(out=tmp, in_=tmp, compare_op=ALU.not_equal, fill=1.0, base=-(P - 1),
                             pattern=[[1, P]], channel_multiplier=1).then_inc(consts, 1)
            for g, w in enumerate(WINDOWS):
                own.link(g_.memset(invc[:, g, :], 1.0 / w))
                for t in range(w - 1):
                    own(g_.memset(invc[:, g, t:t + 1], 1.0 / (t + 1)))
            for e in range(EPG):
                own(g_.memset(iota[:, e:e + 1], float(e)))
            boundary(eng, own, 0)

            with eng.Fori(0, L) as l:
                g_.memset(upad[:, :, 0:UPAD], 0.0).then_inc(S.upad, 1)
                eng.wait_ge(S.upad, 1)
                own(g_.memset(w1[:, :, 0:UPAD], 0.0))
                own(g_.memset(w2[:, :, 0:UPAD], 0.0))
                eng.wait_ge(S.ev, 4)
                src = upad
                for s in range(KC):
                    dst = (w1, w2)[s % 2]
                    own.wait()
                    own(g_.tensor_tensor(dst[:, s:, 1 << s:], src[:, s:, 1 << s:], src[:, s:, 0:UPAD + T - (1 << s)],
                                         ALU.add))
                    src = dst
                own.wait()
                for g, w in enumerate(WINDOWS):
                    s = (w1, w2)[g % 2]
                    own(g_.tensor_tensor(w1[:, g, UPAD:2 * UPAD], s[:, g, UPAD:2 * UPAD], invc[:, g, :], ALU.mult))
                    own(g_.tensor_scalar(w1[:, g, 2 * UPAD:], s[:, g, 2 * UPAD:], 1.0 / w, 1.0, ALU.mult, ALU.mult))
                own.wait()
                g_.tensor_tensor(w1[:, :, UPAD:], w1[:, :, UPAD:], upad[:, :, UPAD:], ALU.subtract
                                 ).then_inc(S.pooled, 1)
                for j in range(4):
                    eng.wait_ge(S.ya, 2 * j + 2)
                    g_.tensor_tensor(ga[:, 2 * j:2 * j + 2, :], ga[:, 2 * j:2 * j + 2, :], gb[:, 2 * j:2 * j + 2, :],
                                     ALU.add).then_inc(S.mix, 1)
                boundary(eng, own, l + 1)
            boundary(eng, own, L + 1)
            with eng.Fori(0, L) as l:
                for n in range(3):
                    for k in range(KD):
                        eng.wait_ge(S.post, KD * n + k + 1)
                        g_.tensor_tensor(x[:, k, :], x[:, k, :], h[:, k, :], ALU.add).then_inc(S.xp, 1)
                boundary(eng, own, l + L + 2)


_INS = ["x", "c", "mixer_norm_g", "w_ada", "b_ada", "w_in", "conv_w", "conv_b", "conv_ln_g", "conv_ln_b",
        "w_conv_out", "b_conv_out", "pool_w", "pool_scale", "w_out", "ffn_norm_g", "w_router_group",
        "b_router_group", "w_router_expert", "b_router_expert", "w_expert_gate", "w_expert_up", "w_expert_down",
        "final_norm_g", "c_2", "rel_bias_2", "ada_w_2", "ada_b_2", "norm_pre_2", "norm_post_2", "ffn_w_gate_2",
        "ffn_w_up_2", "ffn_w_down_2", "mix_w_in_2", "mix_b_in_2", "mix_w_out_2", "attn_sinks_2", "group_gain_2"]


def shape_constants():
    dist = 2 * P - 1 - np.arange(384)
    n = np.maximum(dist, 0)
    exact = BUCKETS // 2
    large = exact + (np.log(np.maximum(n, 1).astype(np.float32) / np.float32(exact))
                     / math.log(MAX_DIST / exact) * (BUCKETS - exact)).astype(np.int32)
    bucket = np.where(n < exact, n, np.minimum(large, BUCKETS - 1))
    onehot = ((bucket[None] == np.arange(BUCKETS)[:, None]) & (dist >= 0)[None]).astype(np.float32)
    mask = np.where(dist >= 0, 0.0, NEG)[None].repeat(NH, 0)
    mask[:SWA, dist >= WIN] = NEG
    return onehot, mask.astype(np.float32)


def kernel(**inputs):
    import concourse.bacc as _bacc
    from concourse.bass_utils import run_bass_kernel_spmd as _run

    nc = _bacc.Bacc("TRN2", target_bir_lowering=False, num_devices=1)
    onehot, mask = shape_constants()
    given = {name: np.ascontiguousarray(inputs[name]) for name in _INS}
    given["bucket_onehot"], given["mask"] = onehot, mask
    arrays, aps = {}, {}
    for name, v in given.items():
        arrays[f"in_{name}_dram"] = v
        aps[name] = nc.dram_tensor(f"in_{name}_dram", v.shape, mybir.dt.from_np(v.dtype), kind="ExternalInput").ap()
    out = nc.dram_tensor("out_0_dram", (1, T, D), F32, kind="ExternalOutput").ap()
    scratch = nc.dram_tensor("bias_rows", (NH, 384), F32, kind="Internal").ap()
    build(nc, Named(**aps), out, scratch)
    r = _run(nc, [arrays], core_ids=[0])
    return r.results[0]["out_0_dram"]
```

```python
import math
from contextlib import ExitStack

import numpy as np

import concourse.bass as bass
from concourse import mybir

F32 = mybir.dt.float32
ALU = mybir.AluOpType
ACT = mybir.ActivationFunctionType
X = mybir.AxisListType.X

P = 128
T = 256
D = 1024
KD = D // P
TH = T // P
L = 2
EPS = 1e-6

DC = 512
KC = DC // P
TAPS = 31
PAD = TAPS - 1
WINDOWS = (2, 4, 8, 16)
UPAD = 16
GRP = 4
EPG = 8
NE = GRP * EPG
NL = GRP + NE

HD = 64
NH = 16
SWA = 8
WIN = 128
BUCKETS = 32
MAX_DIST = 128
NEG = -1e30
UNITS_FF = 2816 // 256

RING = 4
BUF = 3 * KD * 256
COLS = 768
AC = COLS // P

ARENA = 10560

WINDOWS_MAX = T // P
SLOTS = GRP * P

ADA_1 = [0, 1, 2, 4, 6, 8, 10, 12]
WIN_1 = [3, 5, 7, 9, 11]
BRANCH_1, OUT_1, EXPERT_1 = 13, [14, 15], 16
UNITS_1 = 48
ADA_2 = [0, 1, 2, 3] + [6 + 2 * i for i in range(8)]
FFN_2A = [4, 5] + [7 + 2 * i for i in range(8)] + [22]
MIX_2, OUT_2, FFN_2B = [23, 24, 25], [26, 27, 28], 29
UNITS_2 = 40
assert UNITS_1 % RING == 0 and UNITS_2 % RING == 0

WIN_GROUPS = [[0, 2, 1], [3, 4, 5], [6, 7, 8], [9, 10, 11], [12, 13]]

ROWS_1 = dict(norm1=(0, 8), ada=(8, 48), conv_b=(56, 4), ln_g=(60, 4), ln_b=(64, 4), out_b=(68, 8),
              pool_s=(76, 8), norm2=(84, 8))
NR_1 = 92
ROWS_2 = dict(ada=(0, 72), pre=(72, 24), post=(96, 24))
NR_2 = 120
ROWS_3 = dict(q=(0, 4), k=(4, 1), qb=(5, 4), kb=(9, 4), gain=(13, 8))
NR_3 = 21
SMALL_1, SMALL_2 = 13, 14

NAMES = ("vec_t vec ada_acc ada_sum ada_mod sq sum std rstd hn h proj ev v conv ln1 lnc lnq ln2 lnd lnr lnz lns "
         "upad pooled yb_t yb ya_t ya mix o_t xm log_t log ada_part lexp pad ht_t ht sel rank route gath_t gath "
         "gt_t gt cs_t cs gu sil act at_t at down yg sc_t xs xe mm qk vv S sc nm e p T pt pv y yn post xp end").split()


class Named(dict):

    def __getattr__(self, name):
        return self[name]


def build(nc, a, out, scratch):
    with ExitStack() as ctx:
        def sb(name, shape):
            return ctx.enter_context(nc.sbuf_tensor(name, shape, F32))

        def sem(name):
            return ctx.enter_context(nc.semaphore(name))

        ring = sb("ring", [P, RING, BUF])
        x = sb("x", [P, KD, T])
        arena = sb("arena", [P, ARENA + 2 * KD * T])
        h = arena[:, ARENA:ARENA + KD * T].rearrange("p (k t) -> p k t", k=KD)
        tA = arena[:, ARENA + KD * T:].rearrange("p (k t) -> p k t", k=KD)
        silu = sb("silu", [P, 2, 2, T])
        act = sb("act", [P, 2, 2, T])
        bias = sb("bias", [P, NH, T])
        acc = sb("acc", [P, 2, COLS])
        std = sb("std", [P, 2 * T])
        rstd = std
        ident = sb("ident", [P, P])
        ones = sb("ones", [P, P])
        eps = sb("eps", [P, 1])
        invc = sb("invc", [P, KC, UPAD])
        stg = sb("stg", [P, 2, P])
        vec = sb("vec", [P, 2, P])
        mod = sb("mod", [P, 72])
        gs = sb("gs", [P, KD])
        cvec = sb("cvec", [P, 2 * KD])
        fvec = sb("fvec", [P, KD])
        wr = sb("wr", [P, KD, NL])
        rb = sb("rb", [P, NL])
        vbias = sb("vbias", [P, 640])
        sinks = sb("sinks", [P, SWA])
        rt = sb("rt", [P, 664])
        iota = sb("iota", [P, SLOTS])
        before = sb("before", [P, P])
        most = ctx.enter_context(nc.sbuf_tensor("most", [1, 1], mybir.dt.int32))
        cslot = sb("cslot", [P, WINDOWS_MAX, NE])
        stat = sb("stat", [P, 4, 8])
        ps = ctx.enter_context(nc.psum_tensor("ps", [P, 8, 512], F32))

        def carve(at, *shape):
            n = int(np.prod(shape))
            v = arena[:, at:at + n]
            if len(shape) == 2:
                v = v.rearrange("p (a b) -> p a b", a=shape[0])
            return v, at + n
        ga, at = carve(0, KD, T)
        gb, at = carve(at, KD, T)
        vpad, at = carve(at, KC, PAD + T)
        cv, at = carve(at, KC, T)
        sg, at = carve(at, KC, T)
        upad, at = carve(at, KC, UPAD + T)
        w1, at = carve(at, KC, UPAD + T)
        w2, at = carve(at, KC, UPAD + T)
        assert at <= ARENA
        hg, at = carve(0, WINDOWS_MAX, KD * SLOTS)
        hg = hg.rearrange("p w (k s) -> p w k s", k=KD)
        gsel, _ = carve(at, WINDOWS_MAX, TH * SLOTS)
        gsel = gsel.rearrange("p w (h s) -> p w h s", h=TH)
        yg, at = carve(at, WINDOWS_MAX, D)
        gselT, at = carve(at, WINDOWS_MAX, GRP * T)
        gselT = gselT.rearrange("p w (g t) -> p w g t", g=GRP)
        actT, at = carve(at, 2, WINDOWS_MAX * 2 * P)
        actT = actT.rearrange("p s (w c n) -> p s w c n", w=WINDOWS_MAX, c=2)
        assert at <= ARENA + 2 * KD * T
        htok = tA.rearrange("p k t -> p (k t)").rearrange("p (h d) -> p h d", h=TH)
        qa, at = carve(0, 4, T)
        ka, at = carve(at, 1, T)
        va, at = carve(at, TH, P)
        qb, at = carve(at, 4, T)
        kb, at = carve(at, 4, T)
        vb, at = carve(at, TH, 2 * T)
        yT, at = carve(at, KD, T)
        sc, at = carve(at, 4, 384)
        pr, at = carve(at, 4, 384)
        pt, at = carve(at, 2, 384)
        assert at <= ARENA

        landed = [sem(f"landed{i}") for i in range(RING)]
        free = [sem(f"free{i}") for i in range(RING)]
        small = [sem("small1"), sem("small2")]
        first_in, consts, init_t, init_v, bias_w, bias_r, bias_m, out_s, out_e, fin = (
            sem(n) for n in "first_in consts init_t init_v bias_w bias_r bias_m out_s out_e fin".split())
        arrived, all_in, layer_go = sem("arrived"), sem("all_in"), sem("layer_go")
        cleared = [sem(n) for n in NAMES] + [sem(n) for n in ("act_own", "dve_own", "pool_own", "pe_own")]
        S = Named(**{n: s for n, s in zip(NAMES, cleared)})
        act_own, dve_own, pool_own, pe_own = cleared[-4:]

        block = ctx.enter_context(nc.Block())

        class Own:

            def __init__(self, eng, s):
                self.eng, self.s, self.n = eng, s, 0

            def __call__(self, ins):
                self.n += 1
                ins.then_inc(self.s, 1)

            def wait(self):
                self.eng.wait_ge(self.s, self.n)

            def link(self, ins):
                self(ins)
                self.wait()

        def turn(blk, l, unit):
            return l * ((UNITS_1, UNITS_2)[blk] // RING) + (0, L * UNITS_1 // RING)[blk] + unit // RING

        def wait_landed(eng, blk, l, unit, extra=0):
            eng.wait_ge(landed[unit % RING], (turn(blk, l, unit) + extra + 1) * 48)

        def boundary(eng, own, n, clears=False):
            eng.drain().then_inc(arrived, 1)
            if clears:
                eng.wait_ge(arrived, (n + 1) * 4)
                eng.sem_inc(all_in, 1)
                first, last = cleared[0].num, cleared[-1].num
                assert last - first == len(cleared) - 1
                eng.sem_clear(range(first, last + 1))
                eng.drain().then_inc(layer_go, 1)
            eng.wait_ge(layer_go, n + 1)
            own.n = 0

        def w3(unit):
            return ring[:, unit % RING, :].rearrange("p (g k n) -> p g k n", g=3, k=KD)

        def wada(unit):
            return ring[:, unit % RING, :].rearrange("p (k n) -> p k n", k=KD)

        def wdown(unit):
            return ring[:, unit % RING, 2 * KD * 256:].rearrange("p (c n) -> p c n", c=2)

        def row(v, blk_rows, name, i=0, n=1):
            at = blk_rows[name][0] + i
            return v[:, at:at + n]

        vA, vB = vec[:, 0, :], vec[:, 1, :]

        @block.sync
        def _(sp):
            def acquire(blk, l, unit, extra=0):
                sp.wait_ge(free[unit % RING], turn(blk, l, unit) + extra + 1)

            def send(unit, dst, src):
                sp.dma_start(dst, src).then_inc(landed[unit % RING], 16)

            def kpn(w, cols, k0=0, k1=KD):
                return w[:, k0 * P:k1 * P, cols].rearrange("a (k p) n -> p (a k) n", p=P)

            THIRDS = ((0, 3), (3, 6), (6, 8))

            def ada_unit(blk, l, w, u, extra=0, col=None):
                unit = (ADA_1, ADA_2)[blk][u]
                acquire(blk, l, unit, extra)
                cols = slice(u * COLS, (u + 1) * COLS) if col is None else bass.ds(col, COLS)
                for k0, k1 in THIRDS:
                    send(unit, wada(unit)[:, k0:k1, :], kpn(w[bass.ds(l, 1)], cols, k0, k1))

            def group_unit(blk, l, unit, w, groups):
                acquire(blk, l, unit)
                wl = w[bass.ds(l, 1)]
                for g, col in enumerate(groups):
                    cols = slice(col * 256, (col + 1) * 256)
                    last = g == len(groups) - 1
                    parts = ((0, KD),) if not last or len(groups) == 3 else (
                        ((0, 4), (4, 8)) if len(groups) == 2 else THIRDS)
                    for k0, k1 in parts:
                        send(unit, w3(unit)[:, g, k0:k1, :], kpn(wl, cols, k0, k1))

            def expert_unit(blk, l, unit, e, extra=0):
                acquire(blk, l, unit, extra)
                for g, w in enumerate((a.w_expert_gate, a.w_expert_up)):
                    send(unit, w3(unit)[:, g], w[bass.ds(l, 1), bass.ds(e, 1)].rearrange(
                        "a b (k p) n -> p (a b k) n", p=P))
                send(unit, wdown(unit), a.w_expert_down[bass.ds(l, 1), bass.ds(e, 1)].rearrange(
                    "a b (k p) n -> p (a b k) n", p=P))

            def ffn_unit(l, f, unit, e, extra=0):
                acquire(1, l, unit, extra)
                for g, w in enumerate((a.ffn_w_gate_2, a.ffn_w_up_2)):
                    send(unit, w3(unit)[:, g], w[bass.ds(l, 1), f, :, bass.ds(e * 256, 256)].rearrange(
                        "a (k p) n -> p (a k) n", p=P))
                send(unit, wdown(unit), a.ffn_w_down_2[bass.ds(l, 1), f, bass.ds(e * 256, 256), :].rearrange(
                    "a (k p) n -> p (a k) n", p=P))

            xin = tA.rearrange("p k t -> p (k t)").rearrange("p (h d) -> p h d", h=TH)
            sp.dma_start(stg[0:8, 0, :], a.c[0].rearrange("(k p) -> k p", p=P)).then_inc(first_in, 16)
            sp.dma_start(stg[8:16, 0, :], a.c_2[0].rearrange("(k p) -> k p", p=P)).then_inc(first_in, 16)
            sp.dma_start(stg[16:24, 0, :], a.final_norm_g.rearrange("(k p) -> k p", p=P)).then_inc(first_in, 16)
            sp.dma_start(xin, a.x[0].rearrange("(h p) d -> p h d", p=P)).then_inc(first_in, 16)
            sp.dma_start(rt[0:BUCKETS, 0:NH], a.rel_bias_2).then_inc(first_in, 16)
            sp.dma_start(rt[0:BUCKETS, 16:16 + 384], a.bucket_onehot).then_inc(first_in, 16)
            sp.dma_start(gb.rearrange("p k t -> p (k t)")[0:NH, 0:384], a.mask).then_inc(first_in, 16)
            with sp.Fori(0, L) as l:
                for u in range(3):
                    ada_unit(0, l, a.w_ada, u)
                group_unit(0, l, WIN_1[0], a.w_in, WIN_GROUPS[0])
                sp.wait_ge(layer_go, l + 1)
                lc = bass.ds(l, 1)

                def rows(name, src):
                    at, n = ROWS_1[name]
                    sp.dma_start(stg[at:at + n, 0, :], src[lc, :].rearrange("a (k p) -> (a k) p", p=P)
                                 ).then_inc(small[0], 16)
                rows("norm1", a.mixer_norm_g)
                rows("ada", a.b_ada)
                rows("conv_b", a.conv_b)
                rows("ln_g", a.conv_ln_g)
                rows("ln_b", a.conv_ln_b)
                rows("out_b", a.b_conv_out)
                rows("pool_s", a.pool_scale)
                rows("norm2", a.ffn_norm_g)
                sp.dma_start(stg[0:TAPS * KC, 1, :], a.conv_w[lc].rearrange("a j (c p) -> (a j c) p", p=P)
                             ).then_inc(small[0], 16)
                sp.dma_start(wr[:, :, 0:GRP], a.w_router_group[lc].rearrange("a (k p) n -> p (a k) n", p=P)
                             ).then_inc(small[0], 16)
                sp.dma_start(wr[:, :, GRP:NL], a.w_router_expert[lc].rearrange("a (k p) n -> p (a k) n", p=P)
                             ).then_inc(small[0], 16)
                sp.dma_start(rb[:, 0:GRP], a.b_router_group[lc, :].to_broadcast([P, GRP])).then_inc(small[0], 16)
                sp.dma_start(rb[:, GRP:NL], a.b_router_expert[lc, :].to_broadcast([P, NE])).then_inc(small[0], 16)
                for u in range(3, 8):
                    ada_unit(0, l, a.w_ada, u)
                    if u < 7:
                        group_unit(0, l, WIN_1[u - 2], a.w_in, WIN_GROUPS[u - 2])
                acquire(0, l, BRANCH_1)
                wo = ring[:, BRANCH_1 % RING, 0:4 * D].rearrange("p (k n) -> p k n", k=KC)
                for half in range(2):
                    cols = slice(half * 512, half * 512 + 512)
                    send(BRANCH_1, wo[:, :, cols], kpn(a.w_conv_out[lc], cols, 0, KC))
                send(BRANCH_1, ring[:, BRANCH_1 % RING, 4 * D:5 * D].rearrange("p (g n) -> p g n", g=KC),
                     a.pool_w[lc].rearrange("a g p n -> p (a g) n"))
                for j in range(2):
                    group_unit(0, l, OUT_1[j], a.w_out, [2 * j, 2 * j + 1])
                with sp.Fori(0, NE // RING) as i:
                    for j in range(RING):
                        expert_unit(0, l, EXPERT_1 + j, i * RING + j, i)

            with sp.Fori(0, L) as l:
                for u in range(4):
                    ada_unit(1, l, a.ada_w_2, u)
                sp.wait_ge(layer_go, l + L + 2)
                lc = bass.ds(l, 1)

                def put(dst, src):
                    sp.dma_start(dst, src).then_inc(small[1], 16)
                kp = "a (k p) -> (a k) p"
                put(stg[0:72, 0, :], a.ada_b_2[lc, :].rearrange(kp, p=P))
                put(stg[72:96, 0, :], a.norm_pre_2[lc].rearrange("a j (k p) -> (a j k) p", p=P))
                put(stg[96:120, 0, :], a.norm_post_2[lc].rearrange("a j (k p) -> (a j k) p", p=P))
                mb = a.mix_b_in_2
                put(stg[0:4, 1, 0:HD], mb[lc, 0:256].rearrange(kp, p=HD))
                put(stg[0:4, 1, HD:P], mb[lc, 256:512].rearrange(kp, p=HD))
                put(stg[4:5, 1, :], mb[lc, 512:640].rearrange(kp, p=P))
                put(stg[5:9, 1, :], mb[lc, 768:1280].rearrange(kp, p=P))
                put(stg[9:13, 1, :], mb[lc, 1280:1792].rearrange(kp, p=P))
                put(stg[13:21, 1, :], a.group_gain_2[lc, :].rearrange(kp, p=P))
                put(vbias[:, 0:P], mb[lc, 640:768].to_broadcast([P, P]))
                put(vbias[:, P:384], mb[lc, 1792:2048].to_broadcast([P, 256]))
                put(vbias[:, 384:640], mb[lc, 2048:2304].to_broadcast([P, 256]))
                put(sinks[:, 0:4], a.attn_sinks_2[lc, 0:4].to_broadcast([P, 4]))
                put(sinks[:, 4:8], a.attn_sinks_2[lc, 4:8].to_broadcast([P, 4]))
                ffn_unit(l, 0, FFN_2A[0], 0)
                ffn_unit(l, 0, FFN_2A[1], 1)
                with sp.Fori(0, 2) as i:
                    for j in range(4):
                        ada_unit(1, l, a.ada_w_2, 4 + j, i * 2, (i * 4 + 4 + j) * COLS)
                        ffn_unit(l, 0, FFN_2A[2 + j], i * 4 + 2 + j, i * 2)
                ffn_unit(l, 0, FFN_2A[10], 10)
                for u in range(3):
                    group_unit(1, l, MIX_2[u], a.mix_w_in_2, [3 * u, 3 * u + 1, 3 * u + 2])
                group_unit(1, l, OUT_2[0], a.mix_w_out_2, [0, 1])
                group_unit(1, l, OUT_2[1], a.mix_w_out_2, [2])
                group_unit(1, l, OUT_2[2], a.mix_w_out_2, [3])
                with sp.Fori(0, 2) as i:
                    for j in range(4):
                        ffn_unit(l, 1, FFN_2B + j, i * 4 + j, i)
                for e in range(8, UNITS_FF):
                    ffn_unit(l, 1, FFN_2B + e, e)
            sp.wait_ge(out_e, 4)
            otile = tA.rearrange("p k t -> p (k t)").rearrange("p (h d) -> p h d", h=TH)
            sp.dma_start(out[0].rearrange("(h p) d -> p h d", p=P), otile).then_inc(fin, 16)
            sp.wait_ge(fin, 16)

        @block.tensor
        def _(pe):
            own = Own(pe, pe_own)
            mm = nc.tensor.matmul

            def project(dst, wk, rhs, n=KD):
                for k in range(n):
                    last = mm(dst, wk(k), rhs(k), start=(k == 0), stop=(k == n - 1))
                return last

            def hk(k):
                return h[:, k, :]

            def sum_squares(n, parts=1, bank=2):
                for k in range(KD):
                    pe.wait_ge(S.sq, 8 * n + k + 1)
                    half = k * parts // KD
                    per = KD // parts
                    last = mm(ps[:, bank, half * T:half * T + T], ones[:], tA[:, k, :],
                              start=(k % per == 0), stop=(k % per == per - 1))
                last.then_inc(S.sum, 1)

            def ada_sum(n, slot, bank):
                pe.wait_ge(S.ada_acc, n + 1)
                for c in range(AC):
                    last = mm(ps[:, bank, c:c + 1], acc[:, slot, c * P:(c + 1) * P], ones[:, 0:1],
                              start=True, stop=True)
                last.then_inc(S.ada_sum, 1)

            def vectors(n_a, n_b):
                pe.transpose(ps[:, 4, 0:n_a], stg[0:n_a, 0, :], ident[0:n_a, 0:n_a])
                pe.transpose(ps[:, 4, 128:128 + n_b], stg[0:n_b, 1, :], ident[0:n_b, 0:n_b]).then_inc(S.vec_t, 1)

            def gate_up(unit, banks, n, rhs):
                w = w3(unit)
                for k in range(KD):
                    r = rhs(k)
                    for c in range(2):
                        for g in range(2):
                            last = mm(ps[:, banks + c, g * n:(g + 1) * n], w[:, g, k, c * P:(c + 1) * P], r,
                                      start=(k == 0 and g == 0), stop=(k == KD - 1), skip_group_check=True)
                last.then_inc(S.gu, 1)

            def down(unit, slot, n, out_at, first, final):
                w = wdown(unit)
                for d in range(KD):
                    bank, col, opens = out_at(d)
                    for c in range(2):
                        last = mm(ps[:, bank, col:col + n], w[:, c, d * P:(d + 1) * P],
                                  act[:, slot, c, 0:n], start=(first and c == 0 and opens),
                                  stop=(final and c == 1), skip_group_check=True)
                last.then_inc(S.down, 1)

            def free_after(s, count, unit):
                pe.wait_ge(s, count)
                pe.sem_inc(free[unit % RING], 1)

            def by_pairs(d):
                return 4 + d // 2, d % 2 * T, d % 2 == 0

            def experts(l, nw):
                def up(e, k0, k1):
                    unit = EXPERT_1 + e
                    if k0 == 0:
                        wait_landed(pe, 0, l, unit)
                        need = e - 1 if nw == 1 else e
                        if need > 0:
                            pe.wait_ge(S.act, need)
                    g = e // EPG
                    for k in range(k0, k1):
                        for w in range(nw):
                            last = mm(ps[:, e % 2 if nw == 1 else w, :], hg[:, w, k, g * P:(g + 1) * P],
                                      w3(unit)[:, 0:2, k, :], start=(k == 0), stop=(k == KD - 1))
                    if k1 == KD:
                        last.then_inc(S.gu, 1)

                def turn_act(e):
                    pe.wait_ge(S.act, e + 1)
                    if e:
                        pe.wait_ge(S.at, e)
                    if e % EPG == 0 and e:
                        pe.wait_ge(S.xs, 4 * (e // EPG))
                    for w in range(nw):
                        for c in range(2):
                            last = pe.transpose(ps[:, 2, (2 * w + c) * P:(2 * w + c + 1) * P],
                                                act[:, e % 2, w, c * P:(c + 1) * P], ident[:])
                    last.then_inc(S.at_t, 1)

                def down_slots(e):
                    unit = EXPERT_1 + e
                    pe.wait_ge(S.at, e + 1)
                    if e % EPG == 0 and e:
                        pe.wait_ge(S.yg, e // EPG)
                    for w in range(nw):
                        for c in range(2):
                            for n in range(2):
                                last = mm(ps[:, 4 + 2 * w + n, :], actT[:, e % 2, w, c, :],
                                          wdown(unit)[:, c, n * 512:(n + 1) * 512],
                                          start=(e % EPG == 0 and c == 0), stop=(e % EPG == EPG - 1 and c == 1))
                    last.then_inc(S.down, 1)
                    free_after(S.down, e + 1, unit)

                def scatter(g):
                    pe.wait_ge(S.yg, g + 1)
                    for p in range(4):
                        if 4 * g + p >= 2:
                            pe.wait_ge(S.xs, 4 * g + p - 1)
                        for c in range(2):
                            for w in range(nw):
                                at = (2 * p + c) * P
                                last = mm(ps[:, 3 - p % 2, c * T:(c + 1) * T], yg[:, w, at:at + P],
                                          gselT[:, w, g, :], start=(w == 0), stop=(w == nw - 1))
                        last.then_inc(S.sc_t, 1)
                up(0, 0, KD)
                for e in range(NE):
                    if e + 1 < NE:
                        up(e + 1, 0, KD // 2)
                    turn_act(e)
                    if e + 1 < NE:
                        up(e + 1, KD // 2, KD)
                    down_slots(e)
                    if e % EPG == EPG - 1:
                        scatter(e // EPG)

            for b in free[:3]:
                pe.sem_inc(b, 1)
            pe.wait_ge(first_in, 16 * 7)
            pe.wait_ge(consts, 4)
            pe.transpose(ps[:, 4, 0:24], stg[0:24, 0, :], ident[0:24, 0:24]).then_inc(init_t, 1)
            for k in range(KD):
                for hf in range(TH):
                    at = k * T + hf * P
                    last = pe.transpose(ps[:, at // 512, at % 512:at % 512 + P],
                                        tA.rearrange("p k t -> p (k t)")[:, hf * D + k * P:hf * D + (k + 1) * P],
                                        ident[:])
            last.then_inc(init_t, 1)
            mm(ps[0:NH, 5, 0:384], rt[0:BUCKETS, 0:NH], rt[0:BUCKETS, 16:400], start=True, stop=True
               ).then_inc(init_t, 1)
            pe.wait_ge(bias_r, 32)
            pe.wait_ge(init_v, 4)
            for i in range(NH // 2):
                if i >= 4:
                    pe.wait_ge(bias_m, i - 3)
                mm(ps[:, 4 + i % 4, :], act[:].rearrange("p a b t -> p (a b t)")[:, 0:P],
                   ring[:, 3, i * 512:(i + 1) * 512], start=True, stop=True).then_inc(init_t, 1)
            pe.wait_ge(init_t, 3 + NH // 2)
            pe.sem_inc(free[3], 1)
            boundary(pe, own, 0)

            with pe.Fori(0, L) as l:
                sum_squares(0, bank=6)
                pe.wait_ge(small[0], (l + 1) * (16 * SMALL_1))
                vectors(NR_1, TAPS * KC)
                for u in range(3):
                    if u:
                        pe.wait_ge(S.ada_mod, u)
                    ada_sum(u, u % 2, 5)

                def ada_later(u):
                    pe.wait_ge(S.ada_mod, u)
                    ada_sum(u, u % 2, 5)

                for i in range(14):
                    u, g = divmod(i, 3)
                    unit = WIN_1[u]
                    if g == 0:
                        wait_landed(pe, 0, l, unit)
                    if i == 4:
                        pe.wait_ge(S.v, 1)
                    elif i == 5:
                        pe.wait_ge(S.ev, 1)
                    elif i == 6:
                        pe.wait_ge(S.v, 2)
                    elif i == 7:
                        pe.wait_ge(S.ev, 2)
                    elif i >= 8:
                        pe.wait_ge(S.ev, i - 5)
                    for c in range(2):
                        if i == 0 and c == 0:
                            for k in range(KD):
                                pe.wait_ge(S.h, k + 1)
                                mm(ps[:, 0, 0:T], w3(unit)[:, 0, k, 0:P], hk(k), start=(k == 0), stop=(k == KD - 1))
                        else:
                            last = project(ps[:, i % 4, c * T:(c + 1) * T],
                                           lambda k: w3(unit)[:, g, k, c * P:(c + 1) * P], hk)
                    last.then_inc(S.proj, 1)
                    if g == 2 or i == 13:
                        pe.wait_ge(S.proj, i + 1)
                        pe.sem_inc(free[unit % RING], 1)
                    if i in (8, 12):
                        ada_later(3 + (i == 12))
                ada_later(5)
                pe.wait_ge(S.ev, 12)
                wait_landed(pe, 0, l, BRANCH_1)
                pw = ring[:, BRANCH_1 % RING, 4 * D:5 * D].rearrange("p (g n) -> p g n", g=KC)
                pe.wait_ge(S.pooled, 1)
                for g in range(KC):
                    for c in range(2):
                        last = mm(ps[:, g, c * T:(c + 1) * T], pw[:, g, c * P:(c + 1) * P], w1[:, g, UPAD:],
                                  start=True, stop=True)
                    last.then_inc(S.yb_t, 1)
                for c in range(KC):
                    pe.wait_ge(S.conv, c + 1)
                    last = mm(ps[:, 6, 0:T], ones[:], cv[:, c, :], start=(c == 0), stop=(c == KC - 1))
                last.then_inc(S.ln1, 1)
                for c in range(KC):
                    pe.wait_ge(S.lnq, c + 1)
                    last = mm(ps[:, 7, 0:T], ones[:], sg[:, c, :], start=(c == 0), stop=(c == KC - 1))
                last.then_inc(S.ln2, 1)
                wo = ring[:, BRANCH_1 % RING, 0:4 * D].rearrange("p (k n) -> p k n", k=KC)
                pe.wait_ge(S.lns, KC)
                for j in range(4):
                    pe.wait_ge(S.yb, 2 * j + 2)
                    for c in range(2):
                        at = (2 * j + c) * P
                        last = project(ps[:, j, c * T:(c + 1) * T], lambda k: wo[:, k, at:at + P],
                                       lambda k: cv[:, k, :], KC)
                    last.then_inc(S.ya_t, 1)
                pe.wait_ge(S.ya_t, 4)
                pe.sem_inc(free[BRANCH_1 % RING], 1)
                pe.wait_ge(S.mix, 4)
                for j in range(4):
                    unit = OUT_1[j // 2]
                    if j % 2 == 0:
                        wait_landed(pe, 0, l, unit)
                    for c in range(2):
                        last = project(ps[:, j, c * T:(c + 1) * T],
                                       lambda k: w3(unit)[:, j % 2, k, c * P:(c + 1) * P], lambda k: ga[:, k, :])
                    last.then_inc(S.o_t, 1)
                    if j % 2:
                        pe.wait_ge(S.o_t, j + 1)
                        pe.sem_inc(free[unit % RING], 1)
                sum_squares(1, bank=6)
                for u in (6, 7):
                    ada_later(u)
                for k in range(KD):
                    pe.wait_ge(S.h, KD + k + 1)
                for hf in range(TH):
                    last = project(ps[:, 4, hf * NL:(hf + 1) * NL], lambda k: h[:, k, hf * P:(hf + 1) * P],
                                   lambda k: wr[:, k, :])
                last.then_inc(S.log_t, 1)
                for hf in range(TH):
                    for k in range(KD):
                        at = hf * D + k * P
                        last = pe.transpose(ps[:, at // 512, at % 512:at % 512 + P], h[:, k, hf * P:(hf + 1) * P],
                                            ident[:])
                        if k % 4 == 3:
                            last.then_inc(S.ht_t, 1)
                pe.wait_ge(S.sel, 1)
                og = rt[:, 112:120].rearrange("p (h n) -> p h n", h=TH)
                mm(ps[:, 4, 0:GRP], before[:], og[:, 0, :], start=True, stop=True)
                mm(ps[:, 4, GRP:2 * GRP], before[:], og[:, 1, :], start=True, stop=False)
                mm(ps[:, 4, GRP:2 * GRP], ones[:], og[:, 0, :], start=False, stop=True)
                mm(ps[:, 4, 2 * GRP:3 * GRP], ones[:], og[:, 0, :], start=True, stop=False)
                mm(ps[:, 4, 2 * GRP:3 * GRP], ones[:], og[:, 1, :], start=False, stop=True).then_inc(S.rank, 1)

                def gather(nw):
                    for w in range(nw):
                        for g in range(GRP):
                            for hf in range(TH):
                                last = pe.transpose(ps[:, 6 + g // 2, g % 2 * T + hf * P:g % 2 * T + (hf + 1) * P],
                                                    gsel[:, w, hf, g * P:(g + 1) * P], ident[:])
                        last.then_inc(S.gt_t, 1)
                        for k in range(KD):
                            n = w * KD + k
                            if n >= 4:
                                pe.wait_ge(S.gath, n - 3)
                            for hf in range(TH):
                                last = mm(ps[:, k % 4, :], htok[:, hf, k * P:(k + 1) * P], gsel[:, w, hf, :],
                                          start=(hf == 0), stop=(hf == TH - 1))
                            last.then_inc(S.gath_t, 1)
                        pe.wait_ge(S.gt, 2 * w + 2)
                    pe.wait_ge(S.cs_t, 1)
                    for w in range(nw):
                        for g in range(GRP):
                            for hf in range(TH):
                                at = w * NE + g * EPG
                                last = mm(ps[:, 4, at:at + EPG], gsel[:, w, hf, g * P:(g + 1) * P],
                                          rt[:, 184 + hf * EPG:184 + (hf + 1) * EPG], start=(hf == 0),
                                          stop=(hf == TH - 1))
                    last.then_inc(S.cs, 1)
                    pe.wait_ge(S.gath, KD * nw)
                pe.wait_ge(S.ht, 4)
                pe.wait_ge(S.route, 1)
                fullest = pe.value_load(most[0:1, 0:1], min_val=0, max_val=T)
                before_moe = own.n
                with pe.If(fullest > P):
                    gather(2)
                    experts(l, 2)
                after_moe, own.n = own.n, before_moe
                with pe.Else():
                    gather(1)
                    experts(l, 1)
                assert own.n == after_moe
                boundary(pe, own, l + 1)

            sum_squares(0)
            boundary(pe, own, L + 1)

            with pe.Fori(0, L) as l:
                sum_squares(0)
                pe.wait_ge(small[1], (l + 1) * (16 * SMALL_2))
                vectors(NR_2, NR_3)
                for u in range(4):
                    if u:
                        pe.wait_ge(S.ada_mod, u)
                    ada_sum(u, u % 2, 3)
                for f in range(2):
                    base = UNITS_FF * f
                    units = FFN_2A if f == 0 else [FFN_2B + e for e in range(UNITS_FF)]
                    step = 2 if f == 0 else 1
                    if f:
                        sum_squares(5)
                    for k in range(KD):
                        pe.wait_ge(S.h, 16 * f + k + 1)

                    def up(unit, extra=0):
                        wait_landed(pe, 1, l, unit, extra)
                        gate_up(unit, 0, T, hk)

                    def dn(unit, slot, count, first=False, final=False):
                        pe.wait_ge(S.act, count)
                        down(unit, slot, T, by_pairs, first, final)
                        free_after(S.down, count, unit)
                    up(units[0])
                    pe.wait_ge(S.act, base + 1)
                    up(units[1])
                    dn(units[0], base % 2, base + 1, first=True)
                    with pe.Fori(0, 2) as i:
                        for j in range(4):
                            pe.wait_ge(S.act, i * 4 + base + j + 2)
                            up(units[2 + j], i * step)
                            dn(units[1 + j], (base + 1 + j) % 2, i * 4 + base + j + 2)
                            if f == 0:
                                pe.wait_ge(S.ada_mod, i * 4 + j + 4)
                                ada_sum(i * 4 + j + 4, j % 2, 3)
                    pe.wait_ge(S.act, base + 10)
                    up(units[10])
                    dn(units[9], (base + 9) % 2, base + 10)
                    dn(units[10], (base + 10) % 2, base + 11, final=True)
                    sum_squares(1 if f == 0 else 6)
                    if f:
                        continue
                    sum_squares(2)
                    for k in range(KD):
                        pe.wait_ge(S.h, KD + k + 1)
                    pe.wait_ge(S.ada_mod, 12)

                    def evicted(s, n):
                        pe.wait_ge(s, n)

                    def pair(bank, unit, g, c0):
                        for c in range(2):
                            last = project(ps[:, bank, c * T:(c + 1) * T],
                                           lambda k: w3(unit)[:, g, k, c * P:(c + 1) * P], hk)
                        last.then_inc(S.mm, 1)
                    m0, m1, m2 = MIX_2
                    wait_landed(pe, 1, l, m0)
                    for b in range(2):
                        for c in range(2):
                            at = (2 * b + c) * HD
                            for g in range(2):
                                last = project(ps[g * HD:(g + 1) * HD, b, c * T:(c + 1) * T],
                                               lambda k: w3(m0)[:, g, k, at:at + HD], hk)
                        last.then_inc(S.mm, 1)
                    project(ps[:, 2, 0:T], lambda k: w3(m0)[:, 2, k, 0:P], hk)
                    for hf in range(TH):
                        last = project(ps[:, 2, T + hf * P:T + (hf + 1) * P],
                                       lambda k: h[:, k, hf * P:(hf + 1) * P], lambda k: w3(m0)[:, 2, k, P:2 * P])
                    last.then_inc(S.mm, 1)
                    pe.wait_ge(S.mm, 3)
                    pe.sem_inc(free[m0 % RING], 1)
                    wait_landed(pe, 1, l, m1)
                    pair(3, m1, 0, 0)
                    evicted(S.qk, 1)
                    pair(0, m1, 1, 0)
                    evicted(S.qk, 2)
                    pair(1, m1, 2, 0)
                    pe.wait_ge(S.mm, 6)
                    pe.sem_inc(free[m1 % RING], 1)
                    wait_landed(pe, 1, l, m2)
                    evicted(S.vv, 1)
                    pair(2, m2, 0, 0)
                    for hf in range(TH):
                        evicted(S.qk, 4 + hf)
                        project(ps[:, 3 * (1 - hf), :], lambda k: h[:, k, hf * P:(hf + 1) * P],
                                lambda k: w3(m2)[:, 1:3, k, :]).then_inc(S.mm, 1)
                    pe.wait_ge(S.mm, 9)
                    pe.sem_inc(free[m2 % RING], 1)

                    def head(i):
                        if i < SWA:
                            r = HD * (i // 4)
                            return qa[r:r + HD, i % 4, :], ka[r:r + HD, 0, :], lambda b: va[:, b, r:r + HD]
                        m = i - SWA
                        r = HD * (m % 2)
                        return qb[r:r + HD, m // 2, :], kb[r:r + HD, m // 2, :], lambda b: vb[:, b, m * HD:(m + 1) * HD]

                    evicted(S.qk, 7)
                    evicted(S.vv, 3)
                    for i in range(NH + 3):
                        if i < NH:
                            q, k, _ = head(i)
                            if i >= 2:
                                pe.wait_ge(S.sc, i - 1)
                            mm(ps[:, 4 + i % 2, 0:T], q[:, P:T], k, start=True, stop=True)
                            mm(ps[:, 4 + i % 2, T:384], q[:, 0:P], k[:, 0:P], start=True, stop=True).then_inc(S.S, 1)
                        t = i - 2
                        if 0 <= t < NH:
                            pe.wait_ge(S.p, t + 1)
                            if t >= 2:
                                pe.wait_ge(S.pt, t - 1)
                            for n, at in enumerate((T, 0, P)):
                                last = pe.transpose(ps[:, 6 + t % 2, n * P:(n + 1) * P], pr[:, t % 4, at:at + P],
                                                    ident[:])
                            last.then_inc(S.T, 1)
                        t = i - 3
                        if t >= 0:
                            _, _, v = head(t)
                            pe.wait_ge(S.pt, t + 1)
                            if t % 2 == 0 and t >= 4:
                                pe.wait_ge(S.y, t // 2 - 1)
                            r = HD * (t % 2)
                            bank = t // 2 % 2
                            mm(ps[r:r + HD, bank, 0:T], v(0), pt[:, t % 2, 0:T], start=True, stop=False)
                            mm(ps[r:r + HD, bank, P:T], v(1), pt[:, t % 2, T:384], start=False, stop=True
                               ).then_inc(S.pv, 1)
                    sum_squares(3, 2)
                    for k in range(KD):
                        pe.wait_ge(S.yn, k + 1)
                    for c in range(KD):
                        unit, g = ((OUT_2[0], c // 2), (OUT_2[1], 0), (OUT_2[2], 0))[max(0, c // 2 - 1)]
                        if c in (0, 4, 6):
                            wait_landed(pe, 1, l, unit)
                        project(ps[:, 4 + c // 2, c % 2 * T:c % 2 * T + T],
                                lambda k: w3(unit)[:, g, k, c % 2 * P:c % 2 * P + P], lambda k: yT[:, k, :]
                                ).then_inc(S.mm, 1)
                        if c in (3, 5, 7):
                            pe.wait_ge(S.mm, 9 + c + 1)
                            pe.sem_inc(free[unit % RING], 1)
                    sum_squares(4)
                boundary(pe, own, l + L + 2)

            for hf in range(TH):
                for k in range(KD):
                    at = hf * D + k * P
                    last = pe.transpose(ps[:, at // 512, at % 512:at % 512 + P], x[:, k, hf * P:(hf + 1) * P], ident[:])
                    if k % 4 == 3:
                        last.then_inc(out_s, 1)

        @block.scalar
        def _(eng):
            own = Own(eng, act_own)
            act_ = nc.scalar.activation

            def squares(n, src, ready, first, each=1):
                for k in range(KD):
                    if ready is not None:
                        eng.wait_ge(ready, first + k * each)
                    act_(tA[:, k, :], src(k), ACT.Square).then_inc(S.sq, 1)

            def root(n, width=D, bank=2, cols=T):
                eng.wait_ge(S.sum, n + 1)
                act_(std[:, 0:cols], ps[:, bank, 0:cols], ACT.Sqrt, bias=eps[:, 0:1], scale=1.0 / width
                     ).then_inc(S.std, 1)

            def shift(p, at, mods):
                eng.wait_ge(S.ada_mod, mods)
                for k in range(KD):
                    eng.wait_ge(S.hn, KD * p + k + 1)
                    act_(h[:, k, :], h[:, k, :], ACT.Identity, bias=mod[:, at + k:at + k + 1]).then_inc(S.h, 1)

            def xk(k):
                return x[:, k, :]

            def gate_silu(slot, banks, n, count):
                eng.wait_ge(S.gu, count)
                act_(silu[:, slot, :, 0:n], ps[:, banks:banks + 2, 0:n], ACT.Silu).then_inc(S.sil, 1)

            def gather(nw):
                for w in range(nw):
                    eng.wait_ge(S.gt_t, w + 1)
                    for j in range(2):
                        act_(gselT[:, w, 2 * j:2 * j + 2, :], ps[:, 6 + j, :].rearrange("p (g t) -> p g t", g=2),
                             ACT.Identity).then_inc(S.gt, 1)
                    for k in range(KD):
                        eng.wait_ge(S.gath_t, w * KD + k + 1)
                        act_(hg[:, w, k, :], ps[:, k % 4, :], ACT.Identity).then_inc(S.gath, 1)

            def experts(nw):
                def silu_slots(e):
                    eng.wait_ge(S.gu, e + 1)
                    for w in range(nw):
                        last = act_(silu[:, e % 2, w, :], ps[:, e % 2 if nw == 1 else w, 0:256], ACT.Silu)
                    last.then_inc(S.sil, 1)

                silu_slots(0)
                for e in range(NE):
                    eng.wait_ge(S.at_t, e + 1)
                    act_(actT[:, e % 2, 0:nw], ps[:, 2, 0:nw * 256].rearrange("p (w c n) -> p w c n", w=nw, c=2),
                         ACT.Identity).then_inc(S.at, 1)
                    if e + 1 < NE:
                        silu_slots(e + 1)
                    if e % EPG == EPG - 1:
                        eng.wait_ge(S.down, e + 1)
                        for w in range(nw):
                            last = act_(yg[:, w, :].rearrange("p (n m) -> p n m", n=2), ps[:, 4 + 2 * w:6 + 2 * w, :],
                                        ACT.Identity)
                        last.then_inc(S.yg, 1)

            eng.wait_ge(init_t, 1)
            act_(cvec[:], ps[:, 4, 0:16], ACT.Silu).then_inc(init_v, 1)
            eng.wait_ge(init_v, 1)
            act_(fvec[:], ps[:, 4, 16:24], ACT.Identity).then_inc(init_v, 1)
            eng.wait_ge(bias_w, 1)
            eng.dma_start(scratch, ga.rearrange("p k t -> p (k t)")[0:NH, 0:384]).then_inc(bias_r, 16)
            eng.wait_ge(bias_r, 16)
            toeplitz = bass.AP(scratch.tensor, 0, [[1, P], [384, NH], [1, T]])
            eng.dma_start(ring[:, 3, 0:NH * T].rearrange("p (h t) -> p h t", h=NH), toeplitz).then_inc(bias_r, 16)
            boundary(eng, own, 0)

            with eng.Fori(0, L) as l:
                squares(0, xk, None, 0)
                root(0, bank=6)
                shift(0, 0, 3)
                n = 0
                for pair in range(2):
                    eng.wait_ge(S.proj, 2 + 2 * pair)
                    act_(sg[:, 2 * pair:2 * pair + 2, :], ps[:, 1 + 2 * pair, :].rearrange("p (c t) -> p c t", c=2),
                         ACT.Sigmoid).then_inc(S.ev, 1)
                for pair in range(2):
                    eng.wait_ge(S.proj, 5 + pair)
                    eng.wait_ge(S.upad, 1)
                    act_(upad[:, 2 * pair:2 * pair + 2, UPAD:], ps[:, pair, :].rearrange("p (c t) -> p c t", c=2),
                         ACT.Identity).then_inc(S.ev, 1)
                for i in range(6, 14):
                    eng.wait_ge(S.proj, i + 1)
                    gate, j = (ga, i - 6) if i < 10 else (gb, i - 10)
                    act_(gate[:, 2 * j:2 * j + 2, :], ps[:, i % 4, :].rearrange("p (c t) -> p c t", c=2),
                         ACT.Sigmoid).then_inc(S.ev, 1)
                for c in range(KC):
                    eng.wait_ge(S.lnc, c + 1)
                    act_(sg[:, c, :], cv[:, c, :], ACT.Square).then_inc(S.lnq, 1)
                eng.wait_ge(S.ln2, 1)
                act_(std[:, 0:T], ps[:, 7, 0:T], ACT.Sqrt, bias=eps[:, 0:1], scale=1.0 / DC).then_inc(S.lnd, 1)
                for c in range(KC):
                    eng.wait_ge(S.lnz, c + 1)
                    act_(cv[:, c, :], cv[:, c, :], ACT.Silu, bias=row(vA, ROWS_1, "ln_b", c),
                         scale=row(vA, ROWS_1, "ln_g", c)).then_inc(S.lns, 1)
                squares(1, xk, S.xm, 1)
                root(1, bank=6)
                shift(1, 24, 6)
                for j in range(4):
                    eng.wait_ge(S.ht_t, j + 1)
                    act_(tA.rearrange("p k t -> p (k t)")[:, j * 512:(j + 1) * 512], ps[:, j, :], ACT.Identity
                         ).then_inc(S.ht, 1)
                eng.wait_ge(S.log, 1)
                act_(rt[:, 80:88], rt[:, 72:80], ACT.Exp).then_inc(S.lexp, 1)
                eng.wait_ge(S.log, 2)
                act_(rt[:, 90:92], rt[:, 88:90], ACT.Exp).then_inc(S.lexp, 1)
                eng.wait_ge(S.route, 1)
                fullest = eng.value_load(most[0:1, 0:1], min_val=0, max_val=T)
                before_moe = own.n
                with eng.If(fullest > P):
                    gather(2)
                    experts(2)
                after_moe, own.n = own.n, before_moe
                with eng.Else():
                    gather(1)
                    experts(1)
                assert own.n == after_moe
                boundary(eng, own, l + 1)

            squares(0, xk, None, 0)
            root(0)
            boundary(eng, own, L + 1)

            with eng.Fori(0, L) as l:
                squares(0, xk, None, 0)
                root(0)
                shift(0, 0, 3)
                for f in range(2):
                    if f:
                        squares(5, xk, S.xp, 9)
                        root(5)
                        shift(2, 48, 12)
                    base = UNITS_FF * f
                    gate_silu(base % 2, 0, T, base + 1)
                    with eng.Fori(0, UNITS_FF // 2) as i:
                        for j in range(2):
                            gate_silu((base + 1 + j) % 2, 0, T, i * 2 + base + j + 2)
                    eng.wait_ge(S.down, UNITS_FF * (f + 1))
                    n = 6 * f + (1 - f)
                    squares(n, lambda k: ps[:, 4 + k // 2, k % 2 * T:k % 2 * T + T], None, 0)
                    root(n)
                    if f:
                        continue
                    squares(2, xk, S.xp, 1)
                    root(2)
                    shift(1, 24, 7)
                    tiles = [(qa, 0, 0, "q"), (qa, 2, 1, "q"), (ka, 0, 2, "k"), (qb, 0, 3, "qb"), (qb, 2, 0, "qb"),
                             (kb, 0, 1, "kb"), (kb, 2, 2, "kb")]
                    for n, (dst, c0, bank, name) in enumerate(tiles):
                        eng.wait_ge(S.mm, n + 1)
                        cs = range(1 if name == "k" else 2)
                        for c in cs:
                            last = act_(dst[:, c0 + c, :], ps[:, bank, c * T:(c + 1) * T], ACT.Identity,
                                        bias=row(vB, ROWS_3, name, c0 + c))
                        last.then_inc(S.qk, 1)
                    for i in range(NH + 3):
                        if i < NH:
                            st = stat[:, i % 4, :]
                            eng.wait_ge(S.nm, i + 1)
                            act_(pr[:, i % 4, 0:T], sc[:, i % 4, 0:T], ACT.Exp, bias=st[:, 2:3], accum_out=st[:, 4:5])
                            last = act_(pr[:, i % 4, T:384], sc[:, i % 4, T:384], ACT.Exp, bias=st[:, 3:4],
                                        accum_out=st[:, 5:6])
                            if i < SWA:
                                own(last)
                                last = act_(st[:, 6:8], st[:, 2:4], ACT.Exp, bias=sinks[:, i:i + 1])
                            last.then_inc(S.e, 1)
                        t = i - 2
                        if 0 <= t < NH:
                            eng.wait_ge(S.T, t + 1)
                            if t >= 2:
                                eng.wait_ge(S.pv, t - 1)
                            act_(pt[:, t % 2, :], ps[:, 6 + t % 2, 0:384], ACT.Identity).then_inc(S.pt, 1)
                        t = i - 3
                        if t >= 0 and t % 2:
                            eng.wait_ge(S.pv, t + 1)
                            act_(yT[:, t // 2, :], ps[:, t // 2 % 2, 0:T], ACT.Identity).then_inc(S.y, 1)
                    squares(3, lambda k: yT[:, k, :], S.y, 1)
                    root(3, DC, 2, 2 * T)
                    squares(4, lambda k: ps[:, 4 + k // 2, k % 2 * T:k % 2 * T + T], S.mm, 9 + 8, 0)
                    root(4)
                boundary(eng, own, l + L + 2)

            for j in range(4):
                eng.wait_ge(out_s, j + 1)
                act_(tA.rearrange("p k t -> p (k t)")[:, j * 512:(j + 1) * 512], ps[:, j, :], ACT.Identity
                     ).then_inc(out_e, 1)

        @block.vector
        def _(eng):
            v_ = nc.vector
            own = Own(eng, dve_own)

            def ada_unit(blk, l, unit, n, slot, cond, extra=0):
                wait_landed(eng, blk, l, unit, extra)
                w = wada(unit)
                if not isinstance(n, int) or n >= 2:
                    eng.wait_ge(S.ada_sum, n - 1)
                last = v_.tensor_scalar(acc[:, slot, :], w[:, 0, :], cvec[:, cond:cond + 1], None, ALU.mult)
                for k in range(1, KD):
                    last.then_inc(S.ada_part, 1)
                    eng.wait_ge(S.ada_part, n * (KD - 1) + k)
                    last = v_.scalar_tensor_tensor(acc[:, slot, :], w[:, k, :], cvec[:, cond + k:cond + k + 1],
                                                   acc[:, slot, :], ALU.mult, ALU.add)
                last.then_inc(S.ada_acc, 1)
                eng.wait_ge(S.ada_acc, n + 1)
                eng.sem_inc(free[unit % RING], 1)

            def ada_mod(n, bias_at, bank):
                eng.wait_ge(S.ada_sum, n + 1)
                v_.tensor_tensor(mod[:, bass.ds(n * AC, AC)], ps[:, bank, 0:AC], vA[:, bass.ds(n * AC + bias_at, AC)],
                                 ALU.add).then_inc(S.ada_mod, 1)

            def invert(n, cols=T):
                eng.wait_ge(S.std, n + 1)
                v_.reciprocal(rstd[:, 0:cols], std[:, 0:cols]).then_inc(S.rstd, 1)

            def normalize(n, p, scale_at, gain):
                own.link(v_.scalar_tensor_tensor(gs[:], mod[:, scale_at:scale_at + KD], 1.0, gain, ALU.add, ALU.mult))
                eng.wait_ge(S.rstd, n + 1)
                for k in range(KD):
                    v_.scalar_tensor_tensor(h[:, k, :], x[:, k, :], gs[:, k:k + 1], rstd[:, 0:T], ALU.mult, ALU.mult
                                            ).then_inc(S.hn, 1)

            def product(slot, banks, n, count):
                eng.wait_ge(S.sil, count)
                if not isinstance(count, int) or count >= 3:
                    eng.wait_ge(S.down, count - 2)
                v_.tensor_tensor(act[:, slot, :, 0:n], silu[:, slot, :, 0:n], ps[:, banks:banks + 2, n:2 * n],
                                 ALU.mult).then_inc(S.act, 1)

            def copy_vectors(n_a, n_b):
                eng.wait_ge(S.vec_t, 1)
                own(v_.tensor_copy(vA[:, 0:n_a], ps[:, 4, 0:n_a]))
                own(v_.tensor_copy(vB[:, 0:n_b], ps[:, 4, 128:128 + n_b]))
                own.wait()

            v_.memset(ones[:], 1.0).then_inc(consts, 1)
            v_.memset(eps[:], EPS).then_inc(consts, 1)
            eng.wait_ge(init_t, 2)
            xf = x[:].rearrange("p k t -> p (k t)")
            eng.wait_ge(init_v, 2)
            for j in range(4):
                last = v_.tensor_copy(xf[:, j * 512:(j + 1) * 512], ps[:, j, :])
            last.then_inc(init_v, 1)
            eng.wait_ge(init_t, 3)
            v_.tensor_tensor(ga.rearrange("p k t -> p (k t)")[0:NH, 0:384], ps[0:NH, 5, 0:384],
                             gb.rearrange("p k t -> p (k t)")[0:NH, 0:384], ALU.add).then_inc(bias_w, 1)
            eng.wait_ge(bias_w, 1)
            eng.sem_inc(init_v, 1)
            for i in range(NH // 2):
                eng.wait_ge(init_t, 4 + i)
                v_.tensor_copy(bias[:, 2 * i:2 * i + 2, :], ps[:, 4 + i % 4, :].rearrange("p (c t) -> p c t", c=2)
                               ).then_inc(bias_m, 1)
            boundary(eng, own, 0, clears=True)

            with eng.Fori(0, L) as l:
                def ada1(u):
                    ada_unit(0, l, ADA_1[u], u, u % 2, 0)

                def mod1(u):
                    ada_mod(u, ROWS_1["ada"][0], 5)

                v_.memset(vpad[:, :, 0:PAD], 0.0)
                ada1(0)
                invert(0)
                copy_vectors(NR_1, TAPS * KC)
                mod1(0)
                ada1(1)
                mod1(1)
                ada1(2)
                mod1(2)
                eng.wait_ge(S.ada_mod, 3)
                normalize(0, 0, 8, row(vA, ROWS_1, "norm1", 0, KD))

                def glu(pair):
                    eng.wait_ge(S.ev, 1 + pair)
                    v_.tensor_tensor(vpad[:, 2 * pair:2 * pair + 2, PAD:], sg[:, 2 * pair:2 * pair + 2, :],
                                     ps[:, 2 * pair, :].rearrange("p (c t) -> p c t", c=2), ALU.mult
                                     ).then_inc(S.v, 1)
                    eng.wait_ge(S.v, pair + 1)

                def conv(c):
                    own(v_.tensor_scalar(cv[:, c, :], vpad[:, c, 0:T], vB[:, c:c + 1],
                                         row(vA, ROWS_1, "conv_b", c), ALU.mult, ALU.add))
                    for j in range(1, TAPS):
                        own.wait()
                        last = v_.scalar_tensor_tensor(cv[:, c, :], vpad[:, c, j:j + T],
                                                       vB[:, j * KC + c:j * KC + c + 1], cv[:, c, :],
                                                       ALU.mult, ALU.add)
                        if j < TAPS - 1:
                            own(last)
                    last.then_inc(S.conv, 1)
                glu(0)
                conv(0)
                glu(1)
                ada1(3)
                conv(1)
                mod1(3)
                ada1(4)
                conv(2)
                mod1(4)
                ada1(5)
                conv(3)
                mod1(5)
                for j in range(KD):
                    eng.wait_ge(S.yb_t, j // 2 + 1)
                    v_.scalar_tensor_tensor(gb[:, j, :], ps[:, j // 2, j % 2 * T:j % 2 * T + T],
                                            row(vA, ROWS_1, "pool_s", j), gb[:, j, :], ALU.mult, ALU.mult
                                            ).then_inc(S.yb, 1)
                eng.wait_ge(S.ln1, 1)
                for c in range(KC):
                    v_.scalar_tensor_tensor(cv[:, c, :], ps[:, 6, 0:T], -1.0 / DC, cv[:, c, :], ALU.mult, ALU.add
                                            ).then_inc(S.lnc, 1)
                ada1(6)
                eng.wait_ge(S.lnd, 1)
                own.link(v_.reciprocal(rstd[:, 0:T], std[:, 0:T]))
                for c in range(KC):
                    v_.tensor_tensor(cv[:, c, :], cv[:, c, :], rstd[:, 0:T], ALU.mult).then_inc(S.lnz, 1)
                for j in range(KD):
                    eng.wait_ge(S.ya_t, j // 2 + 1)
                    v_.scalar_tensor_tensor(ga[:, j, :], ps[:, j // 2, j % 2 * T:j % 2 * T + T],
                                            row(vA, ROWS_1, "out_b", j), ga[:, j, :], ALU.add, ALU.mult
                                            ).then_inc(S.ya, 1)
                eng.wait_ge(S.ada_mod, 6)
                for j in range(KD):
                    eng.wait_ge(S.o_t, j // 2 + 1)
                    v_.scalar_tensor_tensor(x[:, j, :], ps[:, j // 2, j % 2 * T:j % 2 * T + T],
                                            mod[:, 16 + j:17 + j], x[:, j, :], ALU.mult, ALU.add
                                            ).then_inc(S.xm, 1)
                invert(1)
                mod1(6)
                eng.wait_ge(S.ada_mod, 7)
                normalize(1, 1, 32, row(vA, ROWS_1, "norm2", 0, KD))
                ada1(7)
                mod1(7)

                lg = rt[:, 0:72].rearrange("p (h n) -> p h n", h=TH)
                dg, eg = rt[:, 72:80], rt[:, 80:88]
                d2, e2 = rt[:, 88:90], rt[:, 90:92]
                gmax, gsum, gmin = rt[:, 92:94], rt[:, 94:96], rt[:, 96:98]
                m1, c1, m2, c2 = (rt[:, 98 + 2 * i:100 + 2 * i] for i in range(4))
                wa, wb = rt[:, 106:108], rt[:, 108:110]
                og = rt[:, 112:120].rearrange("p (h n) -> p h n", h=TH)
                o1, o2, tin, cand = (rt[:, 120 + 16 * i:136 + 16 * i].rearrange("p (h n) -> p h n", h=TH)
                                     for i in range(4))
                cm8 = rt[:, 184:200].rearrange("p (h n) -> p h n", h=TH)
                cg = rt[:, 200:208].rearrange("p (h n) -> p h n", h=TH)
                sel = rt[:, 208:272].rearrange("p (h g e) -> p h g e", h=TH, g=GRP)
                rank = rt[:, 272:280].rearrange("p (h n) -> p h n", h=TH)
                slot = rt[:, 280:280 + 2 * WINDOWS_MAX].rearrange("p (w h) -> p w h", h=TH)
                r1, r2 = rt[:, 290:292], rt[:, 292:294]

                def wide(v, n):
                    return v.unsqueeze(2).to_broadcast([P, TH, n])

                def first_of(dst, values, top, c, tmp, n):
                    own.link(v_.tensor_tensor(tmp, values, wide(top, n), ALU.is_equal))
                    for hf in range(TH):
                        own(v_.scalar_tensor_tensor(tmp[:, hf, :], tmp[:, hf, :], -64.0, iota[:, 0:n],
                                                    ALU.mult, ALU.add))
                    own.wait()
                    own.link(v_.tensor_reduce(c, tmp, X, ALU.min))
                    for hf in range(TH):
                        own(v_.tensor_scalar(tmp[:, hf, :], tmp[:, hf, :], c[:, hf:hf + 1], None, ALU.is_equal))
                    own.wait()
                    own.link(v_.tensor_copy(dst, tmp))

                eng.wait_ge(S.log_t, 1)
                for hf in range(TH):
                    own(v_.tensor_tensor(lg[:, hf, :], ps[:, 4, hf * NL:(hf + 1) * NL], rb[:], ALU.add))
                own.wait()
                own.link(v_.tensor_reduce(gmax, lg[:, :, 0:GRP], X, ALU.max))
                v_.tensor_tensor(dg.rearrange("p (h n) -> p h n", h=TH), lg[:, :, 0:GRP], wide(gmax, GRP),
                                 ALU.subtract).then_inc(S.log, 1)
                first_of(og, lg[:, :, 0:GRP], gmax, gmin, cg, GRP)
                eng.sem_inc(S.sel, 1)
                for hf in range(TH):
                    for g in range(GRP):
                        own(v_.tensor_scalar(sel[:, hf, g, :], lg[:, hf, GRP + g * EPG:GRP + (g + 1) * EPG],
                                             og[:, hf, g:g + 1], None, ALU.mult))
                eng.wait_ge(S.rank, 1)
                own(v_.tensor_reduce(rt[:, 296:297], ps[:, 4, 2 * GRP:3 * GRP], X, ALU.max))
                own.link(v_.tensor_tensor(rank, ps[:, 4, 0:2 * GRP].rearrange("p (h n) -> p h n", h=TH), og, ALU.mult))
                own(v_.tensor_copy(most[0:1, 0:1], rt[0:1, 296:297]))
                own.link(v_.tensor_reduce(r1, rank, X, ALU.add))
                own.link(v_.tensor_tensor(rank, og, iota[:, 0:GRP].unsqueeze(1).to_broadcast([P, TH, GRP]), ALU.mult))
                own.link(v_.tensor_reduce(r2, rank, X, ALU.add))
                own.link(v_.scalar_tensor_tensor(r2, r2, float(P), r1, ALU.mult, ALU.add))
                for w in range(WINDOWS_MAX):
                    own.link(v_.tensor_scalar(slot[:, w, :], r1, float(P), -8192.0 if w == 0 else 8192.0,
                                              ALU.is_ge, ALU.mult))
                    own.link(v_.scalar_tensor_tensor(slot[:, w, :], r2, -float(P) * w - (8192.0 if w else 0.0),
                                                     slot[:, w, :], ALU.add, ALU.add))
                for w in range(WINDOWS_MAX):
                    for hf in range(TH):
                        last = v_.tensor_scalar(gsel[:, w, hf, :], iota[:], slot[:, w, hf:hf + 1], None, ALU.is_equal)
                last.then_inc(S.route, 1)
                own.link(v_.tensor_reduce(tin, sel.rearrange("p h g e -> p h e g"), X, ALU.add))
                own.link(v_.tensor_reduce(m1, tin, X, ALU.max))
                first_of(o1, tin, m1, c1, cand, EPG)
                own.link(v_.scalar_tensor_tensor(tin, o1, -3e38, tin, ALU.mult, ALU.add))
                own.link(v_.tensor_reduce(m2, tin, X, ALU.max))
                v_.tensor_tensor(d2, m2, m1, ALU.subtract).then_inc(S.log, 1)
                first_of(o2, tin, m2, c2, cand, EPG)
                eng.wait_ge(S.lexp, 2)
                own.link(v_.tensor_reduce(gsum, eg.rearrange("p (h n) -> p h n", h=TH), X, ALU.add))
                own.link(v_.scalar_tensor_tensor(wa, e2, 1.0, gsum, ALU.add, ALU.mult))
                own.link(v_.reciprocal(wa, wa))
                own.link(v_.tensor_tensor(wb, wa, e2, ALU.mult))
                for hf in range(TH):
                    own.link(v_.tensor_scalar(cm8[:, hf, :], o1[:, hf, :], wa[:, hf:hf + 1], None, ALU.mult))
                    last = v_.scalar_tensor_tensor(cm8[:, hf, :], o2[:, hf, :], wb[:, hf:hf + 1], cm8[:, hf, :],
                                                   ALU.mult, ALU.add)
                    if hf == 0:
                        own(last)
                last.then_inc(S.cs_t, 1)

                def experts(nw):
                    eng.wait_ge(S.cs, 1)
                    own.link(v_.tensor_copy(cslot[:, 0:nw, :], ps[:, 4, 0:nw * NE].rearrange("p (w n) -> p w n", w=nw)))

                    def weigh(e):
                        eng.wait_ge(S.sil, e + 1)
                        if e >= 2:
                            eng.wait_ge(S.at_t, e - 1)
                        for w in range(nw):
                            last = v_.scalar_tensor_tensor(act[:, e % 2, w, :], silu[:, e % 2, w, :],
                                                           cslot[:, w, e:e + 1],
                                                           ps[:, e % 2 if nw == 1 else w, 256:512],
                                                           ALU.mult, ALU.mult)
                        last.then_inc(S.act, 1)
                    for e in range(NE + 1):
                        if e < NE:
                            weigh(e)
                        if e and e % EPG == 0:
                            g = e // EPG - 1
                            for p in range(4):
                                eng.wait_ge(S.sc_t, 4 * g + p + 1)
                                if g:
                                    eng.wait_ge(S.xs, 4 * g + p - 3)
                                for c in range(2):
                                    k = 2 * p + c
                                    last = v_.scalar_tensor_tensor(x[:, k, :], ps[:, 3 - p % 2, c * T:(c + 1) * T],
                                                                   mod[:, 40 + k:41 + k], x[:, k, :],
                                                                   ALU.mult, ALU.add)
                                    if c == 0:
                                        own(last)
                                last.then_inc(S.xs, 1)
                eng.wait_ge(S.ada_mod, 8)
                fullest = eng.value_load(most[0:1, 0:1], min_val=0, max_val=T)
                before_moe = own.n
                with eng.If(fullest > P):
                    experts(2)
                after_moe, own.n = own.n, before_moe
                with eng.Else():
                    experts(1)
                assert own.n == after_moe
                boundary(eng, own, l + 1, clears=True)

            invert(0)
            eng.wait_ge(S.rstd, 1)
            for k in range(KD):
                v_.scalar_tensor_tensor(x[:, k, :], x[:, k, :], fvec[:, k:k + 1], rstd[:, 0:T], ALU.mult, ALU.mult)
            boundary(eng, own, L + 1, clears=True)

            with eng.Fori(0, L) as l:
                def mod2(n):
                    ada_mod(n, 0, 3)

                def post(n, j, factor, gate_at, ready=None):
                    own.link(v_.scalar_tensor_tensor(gs[:], mod[:, gate_at:gate_at + KD], factor,
                                                     vA[:, 96 + 8 * j:104 + 8 * j], ALU.mult, ALU.mult))
                    invert(n)
                    eng.wait_ge(S.rstd, n + 1)
                    for k in range(KD):
                        v_.scalar_tensor_tensor(h[:, k, :], ps[:, 4 + k // 2, k % 2 * T:k % 2 * T + T],
                                                gs[:, k:k + 1], rstd[:, 0:T], ALU.mult, ALU.mult
                                                ).then_inc(S.post, 1)

                ada_unit(1, l, ADA_2[0], 0, 0, KD)
                invert(0)
                copy_vectors(NR_2, NR_3)
                mod2(0)
                for u in range(1, 4):
                    ada_unit(1, l, ADA_2[u], u, u % 2, KD)
                    mod2(u)
                eng.wait_ge(S.ada_mod, 3)
                normalize(0, 0, 8, vA[:, 72:80])
                for f in range(2):
                    base = UNITS_FF * f
                    if f:
                        invert(5)
                        normalize(5, 2, 56, vA[:, 88:96])

                    for e in range(base, base + 3):
                        product(e % 2, 0, T, e + 1)
                    with eng.Fori(0, 2) as i:
                        for j in range(4):
                            if f == 0:
                                ada_unit(1, l, ADA_2[4 + j], i * 4 + 4 + j, j % 2, KD, i * 2)
                            product((base + 3 + j) % 2, 0, T, i * 4 + base + 4 + j)
                            if f == 0:
                                mod2(i * 4 + 4 + j)
                    post(1 if f == 0 else 6, 2 * f, 0.5, 16 + 48 * f)
                    if f:
                        continue
                    invert(2)
                    normalize(2, 1, 32, vA[:, 80:88])
                    eng.wait_ge(S.qk, 3)
                    for hf in range(TH):
                        last = v_.tensor_tensor(va[:, hf, :], ps[:, 2, T + hf * P:T + (hf + 1) * P], vbias[:, 0:P],
                                                ALU.add)
                    last.then_inc(S.vv, 1)
                    for hf in range(TH):
                        eng.wait_ge(S.mm, 8 + hf)
                        v_.tensor_tensor(vb[:, hf, :], ps[:, 3 * (1 - hf), :], vbias[:, P:], ALU.add
                                         ).then_inc(S.vv, 1)
                    for i in range(NH + 1):
                        if i < NH:
                            st = stat[:, i % 4, :]
                            bank = ps[:, 4 + i % 2, :]
                            eng.wait_ge(S.S, i + 1)
                            own(v_.scalar_tensor_tensor(sc[:, i % 4, 0:T], bank[:, 0:T], HD ** -0.5, bias[:, i, :],
                                                        ALU.mult, ALU.add))
                            v_.scalar_tensor_tensor(sc[:, i % 4, T:384], bank[:, T:384], HD ** -0.5,
                                                    bias[:, i, P:T], ALU.mult, ALU.add).then_inc(S.sc, 1)
                            eng.wait_ge(S.sc, i + 1)
                            own(v_.tensor_reduce(st[:, 0:1], sc[:, i % 4, 0:T], X, ALU.max))
                            own.link(v_.tensor_reduce(st[:, 1:2], sc[:, i % 4, T:384], X, ALU.max))
                            if i < SWA:
                                last = v_.tensor_scalar(st[:, 2:4], st[:, 0:2], sinks[:, i:i + 1], -1.0,
                                                        ALU.max, ALU.mult)
                            else:
                                last = v_.tensor_scalar(st[:, 2:4], st[:, 0:2], -1.0, None, ALU.mult)
                            last.then_inc(S.nm, 1)
                        t = i - 1
                        if t >= 0:
                            st = stat[:, t % 4, :]
                            eng.wait_ge(S.e, t + 1)
                            if t < SWA:
                                own.link(v_.tensor_tensor(st[:, 4:6], st[:, 4:6], st[:, 6:8], ALU.add))
                            own.link(v_.reciprocal(st[:, 4:6], st[:, 4:6]))
                            v_.tensor_scalar(pr[:, t % 4, 0:T], pr[:, t % 4, 0:T], st[:, 4:5], None, ALU.mult)
                            v_.tensor_scalar(pr[:, t % 4, T:384], pr[:, t % 4, T:384], st[:, 5:6], None, ALU.mult
                                             ).then_inc(S.p, 1)
                    invert(3, 2 * T)
                    eng.wait_ge(S.rstd, 4)
                    for k in range(KD):
                        v_.scalar_tensor_tensor(yT[:, k, :], yT[:, k, :], row(vB, ROWS_3, "gain", k),
                                                rstd[:, k // 4 * T:k // 4 * T + T], ALU.mult, ALU.mult
                                                ).then_inc(S.yn, 1)
                    post(4, 1, 1.0, 40)
                boundary(eng, own, l + L + 2, clears=True)

        @block.gpsimd
        def _(eng):
            g_ = nc.gpsimd
            own = Own(eng, pool_own)
            tmp = act[:].rearrange("p a b t -> p (a b t)")[:, 0:P]
            own(g_.memset(ident[:], 0.0))
            own(g_.memset(tmp, 0.0))
            own.wait()
            g_.affine_select(out=ident[:], in_=ident[:], compare_op=ALU.not_equal, fill=1.0, base=0,
                             pattern=[[-1, P]], channel_multiplier=1).then_inc(consts, 1)
            g_.affine_select(out=tmp, in_=tmp, compare_op=ALU.not_equal, fill=1.0, base=-(P - 1),
                             pattern=[[1, P]], channel_multiplier=1).then_inc(consts, 1)
            for g, w in enumerate(WINDOWS):
                own.link(g_.memset(invc[:, g, :], 1.0 / w))
                for t in range(w - 1):
                    own(g_.memset(invc[:, g, t:t + 1], 1.0 / (t + 1)))
            own(g_.iota(iota[:], [[1, SLOTS]], base=0, channel_multiplier=0, allow_small_or_imprecise_dtypes=True))
            own.link(g_.memset(before[:], 1.0))
            own(g_.affine_select(out=before[:], in_=before[:], compare_op=ALU.is_gt, fill=0.0, base=0,
                                 pattern=[[1, P]], channel_multiplier=-1))
            boundary(eng, own, 0)

            with eng.Fori(0, L) as l:
                g_.memset(upad[:, :, 0:UPAD], 0.0).then_inc(S.upad, 1)
                eng.wait_ge(S.upad, 1)
                own(g_.memset(w1[:, :, 0:UPAD], 0.0))
                own(g_.memset(w2[:, :, 0:UPAD], 0.0))
                eng.wait_ge(S.ev, 4)
                src = upad
                for s in range(KC):
                    dst = (w1, w2)[s % 2]
                    own.wait()
                    own(g_.tensor_tensor(dst[:, s:, 1 << s:], src[:, s:, 1 << s:], src[:, s:, 0:UPAD + T - (1 << s)],
                                         ALU.add))
                    src = dst
                own.wait()
                for g, w in enumerate(WINDOWS):
                    s = (w1, w2)[g % 2]
                    own(g_.tensor_tensor(w1[:, g, UPAD:2 * UPAD], s[:, g, UPAD:2 * UPAD], invc[:, g, :], ALU.mult))
                    own(g_.tensor_scalar(w1[:, g, 2 * UPAD:], s[:, g, 2 * UPAD:], 1.0 / w, 1.0, ALU.mult, ALU.mult))
                own.wait()
                g_.tensor_tensor(w1[:, :, UPAD:], w1[:, :, UPAD:], upad[:, :, UPAD:], ALU.subtract
                                 ).then_inc(S.pooled, 1)
                for j in range(4):
                    eng.wait_ge(S.ya, 2 * j + 2)
                    g_.tensor_tensor(ga[:, 2 * j:2 * j + 2, :], ga[:, 2 * j:2 * j + 2, :], gb[:, 2 * j:2 * j + 2, :],
                                     ALU.add).then_inc(S.mix, 1)
                boundary(eng, own, l + 1)
            boundary(eng, own, L + 1)
            with eng.Fori(0, L) as l:
                for n in range(3):
                    for k in range(KD):
                        eng.wait_ge(S.post, KD * n + k + 1)
                        g_.tensor_tensor(x[:, k, :], x[:, k, :], h[:, k, :], ALU.add).then_inc(S.xp, 1)
                boundary(eng, own, l + L + 2)


_INS = ["x", "c", "mixer_norm_g", "w_ada", "b_ada", "w_in", "conv_w", "conv_b", "conv_ln_g", "conv_ln_b",
        "w_conv_out", "b_conv_out", "pool_w", "pool_scale", "w_out", "ffn_norm_g", "w_router_group",
        "b_router_group", "w_router_expert", "b_router_expert", "w_expert_gate", "w_expert_up", "w_expert_down",
        "final_norm_g", "c_2", "rel_bias_2", "ada_w_2", "ada_b_2", "norm_pre_2", "norm_post_2", "ffn_w_gate_2",
        "ffn_w_up_2", "ffn_w_down_2", "mix_w_in_2", "mix_b_in_2", "mix_w_out_2", "attn_sinks_2", "group_gain_2"]


def shape_constants():
    dist = 2 * P - 1 - np.arange(384)
    n = np.maximum(dist, 0)
    exact = BUCKETS // 2
    large = exact + (np.log(np.maximum(n, 1).astype(np.float32) / np.float32(exact))
                     / math.log(MAX_DIST / exact) * (BUCKETS - exact)).astype(np.int32)
    bucket = np.where(n < exact, n, np.minimum(large, BUCKETS - 1))
    onehot = ((bucket[None] == np.arange(BUCKETS)[:, None]) & (dist >= 0)[None]).astype(np.float32)
    mask = np.where(dist >= 0, 0.0, NEG)[None].repeat(NH, 0)
    mask[:SWA, dist >= WIN] = NEG
    return onehot, mask.astype(np.float32)


def kernel(**inputs):
    import concourse.bacc as _bacc
    from concourse.bass_utils import run_bass_kernel_spmd as _run

    nc = _bacc.Bacc("TRN2", target_bir_lowering=False, num_devices=1)
    onehot, mask = shape_constants()
    given = {name: np.ascontiguousarray(inputs[name]) for name in _INS}
    given["bucket_onehot"], given["mask"] = onehot, mask
    arrays, aps = {}, {}
    for name, v in given.items():
        arrays[f"in_{name}_dram"] = v
        aps[name] = nc.dram_tensor(f"in_{name}_dram", v.shape, mybir.dt.from_np(v.dtype), kind="ExternalInput").ap()
    out = nc.dram_tensor("out_0_dram", (1, T, D), F32, kind="ExternalOutput").ap()
    scratch = nc.dram_tensor("bias_rows", (NH, 384), F32, kind="Internal").ap()
    build(nc, Named(**aps), out, scratch)
    r = _run(nc, [arrays], core_ids=[0])
    return r.results[0]["out_0_dram"]
```

```python
import math
from contextlib import ExitStack

import numpy as np

import concourse.bass as bass
from concourse import mybir

F32 = mybir.dt.float32
F32R = mybir.dt.float32r
ALU = mybir.AluOpType
ACT = mybir.ActivationFunctionType
X = mybir.AxisListType.X

P = 128
T = 256
D = 1024
KD = D // P
TH = T // P
L = 2
EPS = 1e-6

DC = 512
KC = DC // P
TAPS = 31
PAD = TAPS - 1
WINDOWS = (2, 4, 8, 16)
UPAD = 16
GRP = 4
EPG = 8
NE = GRP * EPG
NL = GRP + NE

HD = 64
NH = 16
SWA = 8
WIN = 128
BUCKETS = 32
MAX_DIST = 128
NEG = -1e30
UNITS_FF = 2816 // 256

RING = 4
BUF = 3 * KD * 256
COLS = 768
AC = COLS // P

ARENA = 10560

WINDOWS_MAX = T // P
SLOTS = GRP * P

AHEAD = 3
WIN_1 = [3, 4, 5, 6, 7]
ADA_1 = [None] * AHEAD + [8, 10, 11, 14, 15]
BRANCH_1, OUT_1 = 9, [12, 13]
EXPERT_1 = [16 + e for e in range(28)] + [45, 46, 48, 50]
AHEAD_1 = [44, 47, 49]
AHEAD_AT = {26: 0, 29: 1, 30: 2}
AHEAD_SUM = {28: 0, 30: 1, 31: 2}
UNITS_1 = 48
ADA_2 = [None] * AHEAD + [5 + 2 * i for i in range(9)]
FFN_2A = [3, 4] + [6 + 2 * i for i in range(9)]
MIX_2, OUT_2 = [23, 24, 25], [26, 27, 28]
AHEAD_2 = [29, 31, 32]
FFN_2B = [30] + [33 + e for e in range(10)]
UNITS_2 = 40
assert UNITS_1 % RING == 0 and UNITS_2 % RING == 0

PIECE = 1024
SPLITS = 3
PIECES_FF = 6 * UNITS_FF
PIECE_1 = 2 * 256

WIN_GROUPS = [[0, 2, 1], [3, 4, 5], [6, 7, 8], [9, 10, 11], [12, 13]]

ROWS_1 = dict(norm1=(0, 8), ada=(8, 48), conv_b=(56, 4), ln_g=(60, 4), ln_b=(64, 4), out_b=(68, 8),
              pool_s=(76, 8), norm2=(84, 8))
NR_1 = 92
ROWS_2 = dict(ada=(0, 72), pre=(72, 24), post=(96, 24))
NR_2 = 120
ROWS_3 = dict(q=(0, 4), k=(4, 1), qb=(5, 4), kb=(9, 4), gain=(13, 8))
NR_3 = 21
ROW_LOADS = 9
SMALL_1, SMALL_2 = 4, 5

NAMES = ("vec_t vec ada_acc ada_sum ada_mod sq sum std rstd hn h proj ev v conv ln1 lnc lnq ln2 lnd lnr lnz lns "
         "upad pooled yb_t yb ya_t ya mix o_t xm log_t log ada_part lexp pad ht_t ht sel rank route gath_t gath "
         "gt_t gt cs_t cs gathl whi wlo wused prod ph hl gu sil act at_t at down yg sc_t xs xe mm qk vv S sc nm e p T pt pv y yn post xp end").split()


class Named(dict):

    def __getattr__(self, name):
        return self[name]


def build(nc, a, out, scratch):
    with ExitStack() as ctx:
        def sb(name, shape):
            return ctx.enter_context(nc.sbuf_tensor(name, shape, F32))

        def sem(name):
            return ctx.enter_context(nc.semaphore(name))

        ring = sb("ring", [P, RING, BUF])
        x = sb("x", [P, KD, T])
        arena_at = nc.sbuf_base
        arena = sb("arena", [P, ARENA + 2 * KD * T])
        h = arena[:, ARENA:ARENA + KD * T].rearrange("p (k t) -> p k t", k=KD)
        tA = arena[:, ARENA + KD * T:].rearrange("p (k t) -> p k t", k=KD)
        silu = sb("silu", [P, 2, 2, T])
        act = sb("act", [P, 2, 2, T])
        bias = sb("bias", [P, NH, T])
        acc = sb("acc", [P, 2, COLS])
        std = sb("std", [P, 2 * T])
        rstd = std
        ident = sb("ident", [P, P])
        ones = sb("ones", [P, P])
        eps = sb("eps", [P, 1])
        invc = sb("invc", [P, KC, UPAD])
        stg = sb("stg", [P, 2, P])
        vec = sb("vec", [P, 2, P])
        mod = sb("mod", [P, 72])
        gs = sb("gs", [P, KD])
        cvec = sb("cvec", [P, 2 * KD])
        fvec = sb("fvec", [P, KD])
        wr = sb("wr", [P, KD, NL])
        rb = sb("rb", [P, NL])
        vbias = sb("vbias", [P, 640])
        sinks = sb("sinks", [P, SWA])
        rt = sb("rt", [P, 664])
        iota = sb("iota", [P, SLOTS])
        before = sb("before", [P, P])
        ahead = sb("ahead", [P, AHEAD * AC])
        cnext = sb("cnext", [P, KD])
        most = ctx.enter_context(nc.sbuf_tensor("most", [1, 1], mybir.dt.int32))
        cslot = sb("cslot", [P, WINDOWS_MAX, NE])
        stat = sb("stat", [P, 4, 8])
        ps = ctx.enter_context(nc.psum_tensor("ps", [P, 8, 512], F32))

        wsp = nc.alloc_sbuf_tensor_at("wsp", [P, SPLITS, 2, PIECE], F32R, offset=arena_at)
        at = arena_at + 4 * SPLITS * 2 * PIECE
        hsp = nc.alloc_sbuf_tensor_at("hsp", [P, 2, KD, T], F32R, offset=at)
        at += 4 * 2 * KD * T
        asp = nc.alloc_sbuf_tensor_at("asp", [P, 2, 2, 2, T], F32R, offset=at)
        assert at + 4 * 8 * T <= arena_at + 4 * (ARENA + KD * T)

        def carve(at, *shape):
            n = int(np.prod(shape))
            v = arena[:, at:at + n]
            if len(shape) == 2:
                v = v.rearrange("p (a b) -> p a b", a=shape[0])
            return v, at + n
        ga, at = carve(0, KD, T)
        gb, at = carve(at, KD, T)
        vpad, at = carve(at, KC, PAD + T)
        cv, at = carve(at, KC, T)
        sg, at = carve(at, KC, T)
        upad, at = carve(at, KC, UPAD + T)
        w1, at = carve(at, KC, UPAD + T)
        w2, at = carve(at, KC, UPAD + T)
        assert at <= ARENA
        hg, at = carve(0, WINDOWS_MAX, KD * SLOTS)
        hg = hg.rearrange("p w (k s) -> p w k s", k=KD)
        gsel, _ = carve(at, WINDOWS_MAX, TH * SLOTS)
        gsel = gsel.rearrange("p w (h s) -> p w h s", h=TH)
        yg, at = carve(at, WINDOWS_MAX, D)
        gselT, at = carve(at, WINDOWS_MAX, GRP * T)
        gselT = gselT.rearrange("p w (g t) -> p w g t", g=GRP)
        actT, at = carve(at, 2, WINDOWS_MAX * 2 * P)
        actT = actT.rearrange("p s (w c n) -> p s w c n", w=WINDOWS_MAX, c=2)
        assert at <= ARENA + 2 * KD * T
        htok = tA.rearrange("p k t -> p (k t)").rearrange("p (h d) -> p h d", h=TH)
        hsg = nc.alloc_sbuf_tensor_at("hsg", [P, 2, KD, SLOTS], F32R, offset=arena_at)
        at_yg = WINDOWS_MAX * KD * SLOTS
        at_gt = at_yg + WINDOWS_MAX * D
        at_act = at_gt + WINDOWS_MAX * GRP * T
        free_at = (at_yg + D, at_gt + GRP * T, at_act + 2 * WINDOWS_MAX * 2 * P)
        assert ARENA + KD * T <= free_at[2] and free_at[2] + 2 * PIECE_1 <= ARENA + 2 * KD * T
        wsg = [nc.alloc_sbuf_tensor_at(f"wsg{i}", [P, 2, 2, 256], F32R, offset=arena_at + 4 * v)
               for i, v in enumerate(free_at)]
        qa, at = carve(0, 4, T)
        ka, at = carve(at, 1, T)
        va, at = carve(at, TH, P)
        qb, at = carve(at, 4, T)
        kb, at = carve(at, 4, T)
        vb, at = carve(at, TH, 2 * T)
        yT, at = carve(at, KD, T)
        sc, at = carve(at, 4, 384)
        pr, at = carve(at, 4, 384)
        pt, at = carve(at, 2, 384)
        assert at <= ARENA

        landed = [(sem(f"landed{i}"), sem(f"landed_low{i}")) for i in range(RING)]
        free = [(sem(f"free{i}"), sem(f"free_low{i}")) for i in range(RING)]
        small = [sem("small1"), sem("small2")]
        rows_in, rows_read = sem("rows_in"), sem("rows_read")
        first_in, consts, init_t, init_v, bias_w, bias_r, bias_m, out_s, out_e, fin = (
            sem(n) for n in "first_in consts init_t init_v bias_w bias_r bias_m out_s out_e fin".split())
        arrived, all_in, layer_go = sem("arrived"), sem("all_in"), sem("layer_go")
        cleared = [sem(n) for n in NAMES] + [sem(n) for n in ("act_own", "dve_own", "pool_own", "pe_own")]
        S = Named(**{n: s for n, s in zip(NAMES, cleared)})
        act_own, dve_own, pool_own, pe_own = cleared[-4:]

        block = ctx.enter_context(nc.Block())

        class Own:

            def __init__(self, eng, s):
                self.eng, self.s, self.n = eng, s, 0

            def __call__(self, ins):
                self.n += 1
                ins.then_inc(self.s, 1)

            def wait(self):
                self.eng.wait_ge(self.s, self.n)

            def link(self, ins):
                self(ins)
                self.wait()

        def turn(blk, l, unit):
            return l * ((UNITS_1, UNITS_2)[blk] // RING) + (0, L * UNITS_1 // RING)[blk] + unit // RING

        def wait_landed(eng, blk, l, unit, extra=0, parts=(0, 1)):
            for part in parts:
                eng.wait_ge(landed[unit % RING][part], (turn(blk, l, unit) + extra + 1) * (32, 16)[part])

        def release(eng, unit, parts=(0, 1)):
            for part in parts:
                eng.sem_inc(free[unit % RING][part], 1)

        def units_in(u):
            return u - 1 if u >= AHEAD else 1

        def boundary(eng, own, n, clears=False):
            eng.drain().then_inc(arrived, 1)
            if clears:
                eng.wait_ge(arrived, (n + 1) * 4)
                eng.sem_inc(all_in, 1)
                first, last = cleared[0].num, cleared[-1].num
                assert last - first == len(cleared) - 1
                eng.sem_clear(range(first, last + 1))
                eng.drain().then_inc(layer_go, 1)
            eng.wait_ge(layer_go, n + 1)
            own.n = 0

        def w3(unit):
            return ring[:, unit % RING, :].rearrange("p (g k n) -> p g k n", g=3, k=KD)

        def wada(unit):
            return ring[:, unit % RING, :].rearrange("p (k n) -> p k n", k=KD)

        def wdown(unit):
            return ring[:, unit % RING, 2 * KD * 256:].rearrange("p (c n) -> p c n", c=2)

        def piece(unit, n):
            if n < 4:
                return w3(unit)[:, 0:2, 2 * n:2 * n + 2, :]
            return wdown(unit)[:, n - 4, :]

        def split_part(slot, part, n, view=None):
            v = wsp[:, slot, part, :]
            v = v if view is None else v.bitcast(view)
            return v.rearrange("p (g k n) -> p g k n", g=2, k=2) if n < 4 else v

        def row(v, blk_rows, name, i=0, n=1):
            at = blk_rows[name][0] + i
            return v[:, at:at + n]

        vA, vB = vec[:, 0, :], vec[:, 1, :]

        @block.sync
        def _(sp):
            def acquire(blk, l, unit, extra=0, parts=(0, 1)):
                for part in parts:
                    sp.wait_ge(free[unit % RING][part], turn(blk, l, unit) + extra + 1)

            def send(unit, i, dst, src):
                sp.dma_start(dst, src).then_inc(landed[unit % RING][i // 2], 16)

            def kpn(w, cols, k0=0, k1=KD):
                return w[:, k0 * P:k1 * P, cols].rearrange("a (k p) n -> p (a k) n", p=P)

            THIRDS = ((0, 3), (3, 6), (6, 8))

            def ada_columns(unit, w, l, cols):
                for i, (k0, k1) in enumerate(THIRDS):
                    send(unit, i, wada(unit)[:, k0:k1, :], kpn(w[bass.ds(l, 1)], cols, k0, k1))

            def ada_unit(blk, l, w, u, extra=0, col=None):
                unit = (ADA_1, ADA_2)[blk][u]
                acquire(blk, l, unit, extra)
                ada_columns(unit, w, l, slice(u * COLS, (u + 1) * COLS) if col is None else bass.ds(col, COLS))

            def ahead_unit(blk, l, u):
                unit = (AHEAD_1, AHEAD_2)[blk][u]
                cols = slice(u * COLS, (u + 1) * COLS)
                with sp.If(l < L - 1):
                    acquire(blk, l, unit)
                    after = nc.s_assert_within(l + 1, 1, L - 1, skip_runtime_bounds_check_because=
                                               "this way is taken only where l < L - 1")
                    ada_columns(unit, (a.w_ada, a.ada_w_2)[blk], after, cols)
                with sp.Else():
                    acquire(blk, l, unit)
                    if blk == 0:
                        ada_columns(unit, a.ada_w_2, 0, cols)
                    else:
                        sp.sem_inc(landed[unit % RING][0], 32)
                        sp.sem_inc(landed[unit % RING][1], 16)

            def group_unit(blk, l, unit, w, groups):
                acquire(blk, l, unit)
                wl = w[bass.ds(l, 1)]
                i = 0
                for g, col in enumerate(groups):
                    cols = slice(col * 256, (col + 1) * 256)
                    last = g == len(groups) - 1
                    parts = ((0, KD),) if not last or len(groups) == 3 else (
                        ((0, 4), (4, 8)) if len(groups) == 2 else THIRDS)
                    for k0, k1 in parts:
                        send(unit, i, w3(unit)[:, g, k0:k1, :], kpn(wl, cols, k0, k1))
                        i += 1

            def expert_unit(blk, l, unit, e, extra=0):
                acquire(blk, l, unit, extra, (0,))
                for g, w in enumerate((a.w_expert_gate, a.w_expert_up)):
                    send(unit, g, w3(unit)[:, g], w[bass.ds(l, 1), bass.ds(e, 1)].rearrange(
                        "a b (k p) n -> p (a b k) n", p=P))
                acquire(blk, l, unit, extra, (1,))
                send(unit, 2, wdown(unit), a.w_expert_down[bass.ds(l, 1), bass.ds(e, 1)].rearrange(
                    "a b (k p) n -> p (a b k) n", p=P))

            def ffn_unit(l, f, unit, e, extra=0):
                acquire(1, l, unit, extra, (0,))
                for g, w in enumerate((a.ffn_w_gate_2, a.ffn_w_up_2)):
                    send(unit, g, w3(unit)[:, g], w[bass.ds(l, 1), f, :, bass.ds(e * 256, 256)].rearrange(
                        "a (k p) n -> p (a k) n", p=P))
                acquire(1, l, unit, extra, (1,))
                send(unit, 2, wdown(unit), a.ffn_w_down_2[bass.ds(l, 1), f, bass.ds(e * 256, 256), :].rearrange(
                    "a (k p) n -> p (a k) n", p=P))

            def rows_1(l):
                lc = bass.ds(l, 1)

                def rows(name, src):
                    at, n = ROWS_1[name]
                    sp.dma_start(stg[at:at + n, 0, :], src[lc, :].rearrange("a (k p) -> (a k) p", p=P)
                                 ).then_inc(rows_in, 16)
                rows("norm1", a.mixer_norm_g)
                rows("ada", a.b_ada)
                rows("conv_b", a.conv_b)
                rows("ln_g", a.conv_ln_g)
                rows("ln_b", a.conv_ln_b)
                rows("out_b", a.b_conv_out)
                rows("pool_s", a.pool_scale)
                rows("norm2", a.ffn_norm_g)
                sp.dma_start(stg[0:TAPS * KC, 1, :], a.conv_w[lc].rearrange("a j (c p) -> (a j c) p", p=P)
                             ).then_inc(rows_in, 16)

            def rows_2(l):
                lc = bass.ds(l, 1)

                def put(dst, src):
                    sp.dma_start(dst, src).then_inc(rows_in, 16)
                kp = "a (k p) -> (a k) p"
                put(stg[0:72, 0, :], a.ada_b_2[lc, :].rearrange(kp, p=P))
                put(stg[72:96, 0, :], a.norm_pre_2[lc].rearrange("a j (k p) -> (a j k) p", p=P))
                put(stg[96:120, 0, :], a.norm_post_2[lc].rearrange("a j (k p) -> (a j k) p", p=P))
                mb = a.mix_b_in_2
                put(stg[0:4, 1, 0:HD], mb[lc, 0:256].rearrange(kp, p=HD))
                put(stg[0:4, 1, HD:P], mb[lc, 256:512].rearrange(kp, p=HD))
                put(stg[4:5, 1, :], mb[lc, 512:640].rearrange(kp, p=P))
                put(stg[5:9, 1, :], mb[lc, 768:1280].rearrange(kp, p=P))
                put(stg[9:13, 1, :], mb[lc, 1280:1792].rearrange(kp, p=P))
                put(stg[13:21, 1, :], a.group_gain_2[lc, :].rearrange(kp, p=P))

            def next_rows(blk, l):
                with sp.If(l < L - 1):
                    sp.wait_ge(rows_read, l + L * blk + 1)
                    (rows_1, rows_2)[blk](nc.s_assert_within(l + 1, 1, L - 1, skip_runtime_bounds_check_because=
                                                             "this way is taken only where l < L - 1"))
                if blk == 0:
                    with sp.Else():
                        sp.wait_ge(rows_read, L)
                        rows_2(0)

            xin = tA.rearrange("p k t -> p (k t)").rearrange("p (h d) -> p h d", h=TH)
            sp.dma_start(stg[0:8, 0, :], a.c[0].rearrange("(k p) -> k p", p=P)).then_inc(first_in, 16)
            sp.dma_start(stg[8:16, 0, :], a.c_2[0].rearrange("(k p) -> k p", p=P)).then_inc(first_in, 16)
            sp.dma_start(stg[16:24, 0, :], a.final_norm_g.rearrange("(k p) -> k p", p=P)).then_inc(first_in, 16)
            sp.dma_start(rt[0:BUCKETS, 0:NH], a.rel_bias_2).then_inc(first_in, 16)
            sp.dma_start(rt[0:BUCKETS, 16:16 + 384], a.bucket_onehot).then_inc(first_in, 16)
            sp.dma_start(gb.rearrange("p k t -> p (k t)")[0:NH, 0:384], a.mask).then_inc(first_in, 16)
            sp.dma_start(xin, a.x[0].rearrange("(h p) d -> p h d", p=P)).then_inc(first_in, 16)
            for u in range(AHEAD):
                acquire(0, 0, u)
                ada_columns(u, a.w_ada, 0, slice(u * COLS, (u + 1) * COLS))
                if u == 0:
                    sp.wait_ge(init_t, 1)
                    rows_1(0)
                    sp.wait_ge(bias_r, 16)
                    toeplitz = bass.AP(scratch.tensor, 0, [[1, P], [384, NH], [1, T]])
                    sp.dma_start(ring[:, 3, 0:NH * T].rearrange("p (h t) -> p h t", h=NH), toeplitz
                                 ).then_inc(bias_r, 16)
            with sp.Fori(0, L) as l:
                group_unit(0, l, WIN_1[0], a.w_in, WIN_GROUPS[0])
                sp.wait_ge(layer_go, l + 1)
                lc = bass.ds(l, 1)
                sp.dma_start(wr[:, :, 0:GRP], a.w_router_group[lc].rearrange("a (k p) n -> p (a k) n", p=P)
                             ).then_inc(small[0], 16)
                sp.dma_start(wr[:, :, GRP:NL], a.w_router_expert[lc].rearrange("a (k p) n -> p (a k) n", p=P)
                             ).then_inc(small[0], 16)
                sp.dma_start(rb[:, 0:GRP], a.b_router_group[lc, :].to_broadcast([P, GRP])).then_inc(small[0], 16)
                sp.dma_start(rb[:, GRP:NL], a.b_router_expert[lc, :].to_broadcast([P, NE])).then_inc(small[0], 16)
                for u in range(1, 5):
                    group_unit(0, l, WIN_1[u], a.w_in, WIN_GROUPS[u])
                ada_unit(0, l, a.w_ada, 3)
                acquire(0, l, BRANCH_1)
                wo = ring[:, BRANCH_1 % RING, 0:4 * D].rearrange("p (k n) -> p k n", k=KC)
                for half in range(2):
                    cols = slice(half * 512, half * 512 + 512)
                    send(BRANCH_1, half, wo[:, :, cols], kpn(a.w_conv_out[lc], cols, 0, KC))
                send(BRANCH_1, 2, ring[:, BRANCH_1 % RING, 4 * D:5 * D].rearrange("p (g n) -> p g n", g=KC),
                     a.pool_w[lc].rearrange("a g p n -> p (a g) n"))
                for u in (4, 5):
                    ada_unit(0, l, a.w_ada, u)
                for j in range(2):
                    group_unit(0, l, OUT_1[j], a.w_out, [2 * j, 2 * j + 1])
                for u in (6, 7):
                    ada_unit(0, l, a.w_ada, u)
                with sp.Fori(0, NE // RING - 1) as i:
                    for j in range(RING):
                        expert_unit(0, l, EXPERT_1[j], i * RING + j, i)
                for e in range(NE - RING, NE):
                    if e == NE - 1:
                        next_rows(0, l)
                    if EXPERT_1[e] - 1 in AHEAD_1:
                        ahead_unit(0, l, AHEAD_1.index(EXPERT_1[e] - 1))
                    expert_unit(0, l, EXPERT_1[e], e)

            with sp.Fori(0, L) as l:
                ffn_unit(l, 0, FFN_2A[0], 0)
                ffn_unit(l, 0, FFN_2A[1], 1)
                sp.wait_ge(layer_go, l + L + 2)
                lc = bass.ds(l, 1)

                def put(dst, src):
                    sp.dma_start(dst, src).then_inc(small[1], 16)
                mb = a.mix_b_in_2
                put(vbias[:, 0:P], mb[lc, 640:768].to_broadcast([P, P]))
                put(vbias[:, P:384], mb[lc, 1792:2048].to_broadcast([P, 256]))
                put(vbias[:, 384:640], mb[lc, 2048:2304].to_broadcast([P, 256]))
                put(sinks[:, 0:4], a.attn_sinks_2[lc, 0:4].to_broadcast([P, 4]))
                put(sinks[:, 4:8], a.attn_sinks_2[lc, 4:8].to_broadcast([P, 4]))
                with sp.Fori(0, 2) as i:
                    for j in range(4):
                        ada_unit(1, l, a.ada_w_2, 3 + j, i * 2, (i * 4 + 3 + j) * COLS)
                        ffn_unit(l, 0, FFN_2A[2 + j], i * 4 + 2 + j, i * 2)
                ada_unit(1, l, a.ada_w_2, 11)
                ffn_unit(l, 0, FFN_2A[10], 10)
                for u in range(3):
                    group_unit(1, l, MIX_2[u], a.mix_w_in_2, [3 * u, 3 * u + 1, 3 * u + 2])
                group_unit(1, l, OUT_2[0], a.mix_w_out_2, [0, 1])
                group_unit(1, l, OUT_2[1], a.mix_w_out_2, [2])
                group_unit(1, l, OUT_2[2], a.mix_w_out_2, [3])
                ahead_unit(1, l, 0)
                ffn_unit(l, 1, FFN_2B[0], 0)
                for u in range(1, AHEAD):
                    ahead_unit(1, l, u)
                with sp.Fori(0, 2) as i:
                    for j in range(4):
                        ffn_unit(l, 1, FFN_2B[1 + j], i * 4 + 1 + j, i)
                for e in range(9, UNITS_FF):
                    if e == UNITS_FF - 1:
                        next_rows(1, l)
                    ffn_unit(l, 1, FFN_2B[e], e)
            sp.wait_ge(out_e, 4)
            otile = tA.rearrange("p k t -> p (k t)").rearrange("p (h d) -> p h d", h=TH)
            sp.dma_start(out[0].rearrange("(h p) d -> p h d", p=P), otile).then_inc(fin, 16)
            sp.wait_ge(fin, 16)

        @block.tensor
        def _(pe):
            own = Own(pe, pe_own)
            mm = nc.tensor.matmul

            def project(dst, wk, rhs, n=KD):
                for k in range(n):
                    last = mm(dst, wk(k), rhs(k), start=(k == 0), stop=(k == n - 1))
                return last

            def hk(k):
                return h[:, k, :]

            def sum_squares(n, parts=1, bank=2):
                for k in range(KD):
                    pe.wait_ge(S.sq, 8 * n + k + 1)
                    half = k * parts // KD
                    per = KD // parts
                    last = mm(ps[:, bank, half * T:half * T + T], ones[:], tA[:, k, :],
                              start=(k % per == 0), stop=(k % per == per - 1))
                last.then_inc(S.sum, 1)

            def ada_sum(n, slot, bank, col=0):
                pe.wait_ge(S.ada_acc, n + 1)
                for c in range(AC):
                    last = mm(ps[:, bank, col + c:col + c + 1], acc[:, slot, c * P:(c + 1) * P], ones[:, 0:1],
                              start=True, stop=True)
                last.then_inc(S.ada_sum, 1)

            def vectors(n_a, n_b):
                pe.transpose(ps[:, 4, 0:n_a], stg[0:n_a, 0, :], ident[0:n_a, 0:n_a])
                pe.transpose(ps[:, 4, 128:128 + n_b], stg[0:n_b, 1, :], ident[0:n_b, 0:n_b]).then_inc(S.vec_t, 1)
                pe.wait_ge(S.vec_t, 1)
                pe.sem_inc(rows_read, 1)

            def thrice(dst, slot, n, w, v_hi, v_lo, start, stop):
                hi, lo = (w(split_part(slot, part, n)) for part in range(2))
                mm(dst, hi, v_hi, start=start, stop=False, skip_group_check=True)
                mm(dst, hi, v_lo, start=False, stop=False, skip_group_check=True)
                return mm(dst, lo, v_hi, start=False, stop=stop, skip_group_check=True)

            def gate_up(at, count, ready=None):
                for q in range(4):
                    pe.wait_ge(S.wlo, count + q + 1)
                    for k in (2 * q, 2 * q + 1):
                        if ready is not None:
                            pe.wait_ge(S.hl, ready + k + 1)
                        for c in range(2):
                            for g in range(2):
                                last = thrice(ps[:, c, g * T:(g + 1) * T], (at + q) % SPLITS, q,
                                              lambda w: w[:, g, k % 2, c * P:(c + 1) * P],
                                              hsp[:, 0, k, :], hsp[:, 1, k, :],
                                              start=(k == 0 and g == 0), stop=(k == KD - 1))
                    last.then_inc(S.wused, 1)

            def down(at, count, slot, first, final):
                for c in range(2):
                    pe.wait_ge(S.wlo, count + c + 1)
                    for d in range(KD):
                        last = thrice(ps[:, 4 + d // 2, d % 2 * T:(d % 2 + 1) * T], (at + c) % SPLITS, 4 + c,
                                      lambda w: w[:, d * P:(d + 1) * P],
                                      asp[:, slot, 0, c, :], asp[:, slot, 1, c, :],
                                      start=(first and c == 0 and d % 2 == 0), stop=(final and c == 1))
                    last.then_inc(S.wused, 1)

            def free_after(s, count, unit):
                pe.wait_ge(s, count)
                release(pe, unit)

            def free_behind(count, unit, following, first=False):
                pe.wait_ge(S.down, count)
                release(pe, unit, (0, 1) if first else (1,))
                if following is not None:
                    release(pe, following, (0,))

            def experts(l, nw):
                def up(e, k0, k1):
                    unit = EXPERT_1[e]
                    if k0 == 0:
                        if nw == 2:
                            wait_landed(pe, 0, l, unit, parts=(0,))
                        need = e - 1 if nw == 1 else e
                        if need > 0:
                            pe.wait_ge(S.act, need)
                    g = e // EPG
                    if nw == 1:
                        for k in range(k0, k1):
                            n = KD * e + k
                            w, dst = wsg[n % SPLITS], ps[:, e % 2, :]
                            hi, lo = (hsg[:, part, k, g * P:(g + 1) * P] for part in range(2))
                            pe.wait_ge(S.wlo, n + 1)
                            mm(dst, hi, w[:, 0], start=(k == 0), stop=False)
                            mm(dst, lo, w[:, 0], start=False, stop=False)
                            mm(dst, hi, w[:, 1], start=False, stop=(k == KD - 1)).then_inc(S.wused, 1)
                        return
                    for k in range(k0, k1):
                        for w in range(nw):
                            last = mm(ps[:, e % 2 if nw == 1 else w, :], hg[:, w, k, g * P:(g + 1) * P],
                                      w3(unit)[:, 0:2, k, :], start=(k == 0), stop=(k == KD - 1))
                    if k1 == KD:
                        last.then_inc(S.gu, 1)

                def turn_act(e):
                    pe.wait_ge(S.act, e + 1)
                    if e:
                        pe.wait_ge(S.at, e)
                    if e % EPG == 0 and e:
                        pe.wait_ge(S.xs, 4 * (e // EPG))
                    for w in range(nw):
                        for c in range(2):
                            last = pe.transpose(ps[:, 2, (2 * w + c) * P:(2 * w + c + 1) * P],
                                                act[:, e % 2, w, c * P:(c + 1) * P], ident[:])
                    last.then_inc(S.at_t, 1)

                def down_slots(e):
                    unit = EXPERT_1[e]
                    wait_landed(pe, 0, l, unit, parts=(1,))
                    pe.wait_ge(S.at, e + 1)
                    if e % EPG == 0 and e:
                        pe.wait_ge(S.yg, e // EPG)
                    for w in range(nw):
                        for c in range(2):
                            for n in range(2):
                                last = mm(ps[:, 4 + 2 * w + n, :], actT[:, e % 2, w, c, :],
                                          wdown(unit)[:, c, n * 512:(n + 1) * 512],
                                          start=(e % EPG == 0 and c == 0), stop=(e % EPG == EPG - 1 and c == 1))
                    last.then_inc(S.down, 1)
                    if nw == 1:
                        pe.wait_ge(S.down, e + 1)
                        release(pe, unit, (1,))
                    else:
                        free_behind(e + 1, unit, EXPERT_1[e + 1] if e + 1 < NE else None, e == 0)

                def scatter(g):
                    pe.wait_ge(S.yg, g + 1)
                    if g == 0 or g == GRP - 1:
                        pe.wait_ge(S.ada_mod, units_in(7) + (g > 0))
                    for p in range(4):
                        if 4 * g + p >= 2:
                            pe.wait_ge(S.xs, 4 * g + p - 1)
                        for c in range(2):
                            for w in range(nw):
                                at = (2 * p + c) * P
                                last = mm(ps[:, 3 - p % 2, c * T:(c + 1) * T], yg[:, w, at:at + P],
                                          gselT[:, w, g, :], start=(w == 0), stop=(w == nw - 1))
                        last.then_inc(S.sc_t, 1)
                up(0, 0, KD)
                for e in range(NE):
                    if e + 1 < NE:
                        up(e + 1, 0, KD // 2)
                    turn_act(e)
                    if e + 1 < NE:
                        up(e + 1, KD // 2, KD)
                    down_slots(e)
                    if e == 1:
                        ada_sum(7 - AHEAD, (7 - AHEAD) % 2, 3)
                    if e in AHEAD_SUM:
                        u = AHEAD_SUM[e]
                        ada_sum(8 - AHEAD + u, (8 - AHEAD + u) % 2, 3, u * AC)
                    if e % EPG == EPG - 1:
                        scatter(e // EPG)

            for b in range(3):
                release(pe, b)
            pe.wait_ge(first_in, 16 * 7)
            pe.wait_ge(consts, 4)
            pe.transpose(ps[:, 4, 0:24], stg[0:24, 0, :], ident[0:24, 0:24]).then_inc(init_t, 1)
            mm(ps[0:NH, 5, 0:384], rt[0:BUCKETS, 0:NH], rt[0:BUCKETS, 16:400], start=True, stop=True
               ).then_inc(init_t, 1)
            for k in range(KD):
                for hf in range(TH):
                    at = k * T + hf * P
                    last = pe.transpose(ps[:, at // 512, at % 512:at % 512 + P],
                                        tA.rearrange("p k t -> p (k t)")[:, hf * D + k * P:hf * D + (k + 1) * P],
                                        ident[:])
            last.then_inc(init_t, 1)
            pe.wait_ge(init_v, 4)
            pe.wait_ge(bias_r, 32)
            for i in range(NH // 2):
                if i >= 4:
                    pe.wait_ge(bias_m, i - 3)
                mm(ps[:, 4 + i % 4, :], act[:].rearrange("p a b t -> p (a b t)")[:, 0:P],
                   ring[:, 3, i * 512:(i + 1) * 512], start=True, stop=True).then_inc(init_t, 1)
            pe.wait_ge(init_t, 3 + NH // 2)
            release(pe, 3)
            for u in range(AHEAD):
                ada_sum(u, u % 2, 0, u * AC)
            boundary(pe, own, 0)

            with pe.Fori(0, L) as l:
                sum_squares(0, bank=6)
                pe.wait_ge(rows_in, (l + 1) * (16 * ROW_LOADS))
                vectors(NR_1, TAPS * KC)

                def ada_later(u):
                    pe.wait_ge(S.ada_mod, units_in(u - 1))
                    ada_sum(u - AHEAD, (u - AHEAD) % 2, 5)

                for i in range(14):
                    u, g = divmod(i, 3)
                    unit = WIN_1[u]
                    if g != 1:
                        wait_landed(pe, 0, l, unit, parts=(g // 2,))
                    if i == 13:
                        wait_landed(pe, 0, l, unit, parts=(1,))
                    if i == 4:
                        pe.wait_ge(S.v, 1)
                    elif i == 5:
                        pe.wait_ge(S.ev, 1)
                    elif i == 6:
                        pe.wait_ge(S.v, 2)
                    elif i == 7:
                        pe.wait_ge(S.ev, 2)
                    elif i >= 8:
                        pe.wait_ge(S.ev, i - 5)
                    for c in range(2):
                        if i == 0 and c == 0:
                            for k in range(KD):
                                pe.wait_ge(S.h, k + 1)
                                mm(ps[:, 0, 0:T], w3(unit)[:, 0, k, 0:P], hk(k), start=(k == 0), stop=(k == KD - 1))
                        else:
                            last = project(ps[:, i % 4, c * T:(c + 1) * T],
                                           lambda k: w3(unit)[:, g, k, c * P:(c + 1) * P], hk)
                    last.then_inc(S.proj, 1)
                    if g == 2 or i == 13:
                        pe.wait_ge(S.proj, i + 1)
                        release(pe, unit)
                    if i == 10:
                        for c in range(KC):
                            pe.wait_ge(S.conv, c + 1)
                            last = mm(ps[:, 6, 0:T], ones[:], cv[:, c, :], start=(c == 0), stop=(c == KC - 1))
                        last.then_inc(S.ln1, 1)
                    elif i == 11:
                        for c in range(KC):
                            pe.wait_ge(S.lnq, c + 1)
                            last = mm(ps[:, 7, 0:T], ones[:], sg[:, c, :], start=(c == 0), stop=(c == KC - 1))
                        last.then_inc(S.ln2, 1)
                ada_later(3)
                pe.wait_ge(S.ev, 12)
                wait_landed(pe, 0, l, BRANCH_1)
                pw = ring[:, BRANCH_1 % RING, 4 * D:5 * D].rearrange("p (g n) -> p g n", g=KC)
                pe.wait_ge(S.pooled, 1)
                for g in range(KC):
                    for c in range(2):
                        last = mm(ps[:, g, c * T:(c + 1) * T], pw[:, g, c * P:(c + 1) * P], w1[:, g, UPAD:],
                                  start=True, stop=True)
                    last.then_inc(S.yb_t, 1)
                wo = ring[:, BRANCH_1 % RING, 0:4 * D].rearrange("p (k n) -> p k n", k=KC)
                pe.wait_ge(S.lns, KC)
                for j in range(4):
                    pe.wait_ge(S.yb, 2 * j + 2)
                    for c in range(2):
                        at = (2 * j + c) * P
                        last = project(ps[:, j, c * T:(c + 1) * T], lambda k: wo[:, k, at:at + P],
                                       lambda k: cv[:, k, :], KC)
                    last.then_inc(S.ya_t, 1)
                pe.wait_ge(S.ya_t, 4)
                release(pe, BRANCH_1)
                ada_later(4)
                pe.wait_ge(S.mix, 4)
                for j in range(4):
                    unit = OUT_1[j // 2]
                    if j % 2 == 0:
                        wait_landed(pe, 0, l, unit)
                    for c in range(2):
                        last = project(ps[:, j, c * T:(c + 1) * T],
                                       lambda k: w3(unit)[:, j % 2, k, c * P:(c + 1) * P], lambda k: ga[:, k, :])
                    last.then_inc(S.o_t, 1)
                    if j % 2:
                        pe.wait_ge(S.o_t, j + 1)
                        release(pe, unit)
                    if j == 1:
                        ada_later(5)
                ada_later(6)
                sum_squares(1, bank=6)
                pe.wait_ge(small[0], (l + 1) * (16 * SMALL_1))
                for k in range(KD):
                    pe.wait_ge(S.h, KD + k + 1)
                for hf in range(TH):
                    last = project(ps[:, 4, hf * NL:(hf + 1) * NL], lambda k: h[:, k, hf * P:(hf + 1) * P],
                                   lambda k: wr[:, k, :])
                last.then_inc(S.log_t, 1)
                for hf in range(TH):
                    for k in range(KD):
                        at = hf * D + k * P
                        last = pe.transpose(ps[:, at // 512, at % 512:at % 512 + P], h[:, k, hf * P:(hf + 1) * P],
                                            ident[:])
                        if k % 4 == 3:
                            last.then_inc(S.ht_t, 1)
                pe.wait_ge(S.sel, 1)
                og = rt[:, 112:120].rearrange("p (h n) -> p h n", h=TH)
                mm(ps[:, 4, 0:GRP], before[:], og[:, 0, :], start=True, stop=True)
                mm(ps[:, 4, GRP:2 * GRP], before[:], og[:, 1, :], start=True, stop=False)
                mm(ps[:, 4, GRP:2 * GRP], ones[:], og[:, 0, :], start=False, stop=True)
                mm(ps[:, 4, 2 * GRP:3 * GRP], ones[:], og[:, 0, :], start=True, stop=False)
                mm(ps[:, 4, 2 * GRP:3 * GRP], ones[:], og[:, 1, :], start=False, stop=True).then_inc(S.rank, 1)

                def gather(nw):
                    for w in range(nw):
                        for g in range(GRP):
                            for hf in range(TH):
                                last = pe.transpose(ps[:, 6 + g // 2, g % 2 * T + hf * P:g % 2 * T + (hf + 1) * P],
                                                    gsel[:, w, hf, g * P:(g + 1) * P], ident[:])
                        last.then_inc(S.gt_t, 1)
                        for k in range(KD):
                            n = w * KD + k
                            if n >= 4:
                                pe.wait_ge(S.gathl if nw == 1 else S.gath, n - 3)
                            for hf in range(TH):
                                last = mm(ps[:, k % 4, :], htok[:, hf, k * P:(k + 1) * P], gsel[:, w, hf, :],
                                          start=(hf == 0), stop=(hf == TH - 1))
                            last.then_inc(S.gath_t, 1)
                        pe.wait_ge(S.gt, 2 * w + 2)
                    pe.wait_ge(S.cs_t, 1)
                    for w in range(nw):
                        for g in range(GRP):
                            for hf in range(TH):
                                at = w * NE + g * EPG
                                last = mm(ps[:, 4, at:at + EPG], gsel[:, w, hf, g * P:(g + 1) * P],
                                          rt[:, 184 + hf * EPG:184 + (hf + 1) * EPG], start=(hf == 0),
                                          stop=(hf == TH - 1))
                    last.then_inc(S.cs, 1)
                    pe.wait_ge(S.gathl if nw == 1 else S.gath, KD * nw)
                pe.wait_ge(S.ht, 4)
                pe.wait_ge(S.route, 1)
                fullest = pe.value_load(most[0:1, 0:1], min_val=0, max_val=T)
                before_moe = own.n
                with pe.If(fullest > P):
                    gather(2)
                    experts(l, 2)
                after_moe, own.n = own.n, before_moe
                with pe.Else():
                    gather(1)
                    experts(l, 1)
                assert own.n == after_moe
                boundary(pe, own, l + 1)

            sum_squares(0)
            boundary(pe, own, L + 1)

            with pe.Fori(0, L) as l:
                sum_squares(0)
                pe.wait_ge(rows_in, (l + L + 1) * (16 * ROW_LOADS))
                vectors(NR_2, NR_3)
                for f in range(2):
                    base, pb = UNITS_FF * f, PIECES_FF * f
                    if f:
                        sum_squares(5)
                        ada_sum(9, 1, 3, 0)

                    def dn(e, at, count, done, first=False, final=False):
                        pe.wait_ge(S.act, done)
                        down(at, count, (base + e) % 2, first, final)
                    if f:
                        pe.wait_ge(S.prod, base)
                    gate_up(0, pb, KD * f)
                    pe.wait_ge(S.prod, base + 1)
                    gate_up(4, pb + 4)
                    dn(0, 8, pb + 8, base + 1, first=True)
                    if f:
                        ada_sum(10, 0, 3, AC)
                        ada_sum(11, 1, 3, 2 * AC)
                    with pe.Fori(0, 2) as i:
                        for j in range(4):
                            pe.wait_ge(S.prod, i * 4 + base + j + 2)
                            gate_up(10 + 6 * j, i * 24 + pb + 10 + 6 * j)
                            dn(1 + j, 14 + 6 * j, i * 24 + pb + 14 + 6 * j, i * 4 + base + j + 2)
                            if f == 0:
                                pe.wait_ge(S.ada_mod, i * 4 + j + units_in(2))
                                ada_sum(i * 4 + j, j % 2, 3)
                    pe.wait_ge(S.prod, base + 10)
                    gate_up(58, pb + 58)
                    dn(9, 62, pb + 62, base + 10)
                    if f == 0:
                        pe.wait_ge(S.ada_mod, units_in(10))
                        ada_sum(8, 0, 3)
                    dn(10, 64, pb + 64, base + 11, final=True)
                    sum_squares(1 if f == 0 else 6)
                    if f:
                        continue
                    sum_squares(2)
                    for k in range(KD):
                        pe.wait_ge(S.h, KD + k + 1)
                    pe.wait_ge(S.ada_mod, units_in(11))

                    def evicted(s, n):
                        pe.wait_ge(s, n)

                    def pair(bank, unit, g, c0):
                        for c in range(2):
                            last = project(ps[:, bank, c * T:(c + 1) * T],
                                           lambda k: w3(unit)[:, g, k, c * P:(c + 1) * P], hk)
                        last.then_inc(S.mm, 1)
                    m0, m1, m2 = MIX_2
                    wait_landed(pe, 1, l, m0)
                    for b in range(2):
                        for c in range(2):
                            at = (2 * b + c) * HD
                            for g in range(2):
                                last = project(ps[g * HD:(g + 1) * HD, b, c * T:(c + 1) * T],
                                               lambda k: w3(m0)[:, g, k, at:at + HD], hk)
                        last.then_inc(S.mm, 1)
                    project(ps[:, 2, 0:T], lambda k: w3(m0)[:, 2, k, 0:P], hk)
                    for hf in range(TH):
                        last = project(ps[:, 2, T + hf * P:T + (hf + 1) * P],
                                       lambda k: h[:, k, hf * P:(hf + 1) * P], lambda k: w3(m0)[:, 2, k, P:2 * P])
                    last.then_inc(S.mm, 1)
                    pe.wait_ge(S.mm, 3)
                    release(pe, m0)
                    wait_landed(pe, 1, l, m1)
                    pair(3, m1, 0, 0)
                    evicted(S.qk, 1)
                    pair(0, m1, 1, 0)
                    evicted(S.qk, 2)
                    pair(1, m1, 2, 0)
                    pe.wait_ge(S.mm, 6)
                    release(pe, m1)
                    wait_landed(pe, 1, l, m2)
                    evicted(S.vv, 1)
                    pair(2, m2, 0, 0)
                    for hf in range(TH):
                        evicted(S.qk, 4 + hf)
                        project(ps[:, 3 * (1 - hf), :], lambda k: h[:, k, hf * P:(hf + 1) * P],
                                lambda k: w3(m2)[:, 1:3, k, :]).then_inc(S.mm, 1)
                    pe.wait_ge(S.mm, 9)
                    release(pe, m2)

                    def head(i):
                        if i < SWA:
                            r = HD * (i // 4)
                            return qa[r:r + HD, i % 4, :], ka[r:r + HD, 0, :], lambda b: va[:, b, r:r + HD]
                        m = i - SWA
                        r = HD * (m % 2)
                        return qb[r:r + HD, m // 2, :], kb[r:r + HD, m // 2, :], lambda b: vb[:, b, m * HD:(m + 1) * HD]

                    evicted(S.qk, 7)
                    evicted(S.vv, 3)
                    for i in range(NH + 3):
                        if i < NH:
                            q, k, _ = head(i)
                            if i >= 2:
                                pe.wait_ge(S.sc, i - 1)
                            mm(ps[:, 4 + i % 2, 0:T], q[:, P:T], k, start=True, stop=True)
                            mm(ps[:, 4 + i % 2, T:384], q[:, 0:P], k[:, 0:P], start=True, stop=True).then_inc(S.S, 1)
                        t = i - 2
                        if 0 <= t < NH:
                            pe.wait_ge(S.p, t + 1)
                            if t >= 2:
                                pe.wait_ge(S.pt, t - 1)
                            for n, at in enumerate((T, 0, P)):
                                last = pe.transpose(ps[:, 6 + t % 2, n * P:(n + 1) * P], pr[:, t % 4, at:at + P],
                                                    ident[:])
                            last.then_inc(S.T, 1)
                        t = i - 3
                        if t >= 0:
                            _, _, v = head(t)
                            pe.wait_ge(S.pt, t + 1)
                            if t % 2 == 0 and t >= 4:
                                pe.wait_ge(S.y, t // 2 - 1)
                            r = HD * (t % 2)
                            bank = t // 2 % 2
                            mm(ps[r:r + HD, bank, 0:T], v(0), pt[:, t % 2, 0:T], start=True, stop=False)
                            mm(ps[r:r + HD, bank, P:T], v(1), pt[:, t % 2, T:384], start=False, stop=True
                               ).then_inc(S.pv, 1)
                    sum_squares(3, 2)
                    for k in range(KD):
                        pe.wait_ge(S.yn, k + 1)
                    for c in range(KD):
                        unit, g = ((OUT_2[0], c // 2), (OUT_2[1], 0), (OUT_2[2], 0))[max(0, c // 2 - 1)]
                        if c in (0, 4, 6):
                            wait_landed(pe, 1, l, unit)
                        project(ps[:, 4 + c // 2, c % 2 * T:c % 2 * T + T],
                                lambda k: w3(unit)[:, g, k, c % 2 * P:c % 2 * P + P], lambda k: yT[:, k, :]
                                ).then_inc(S.mm, 1)
                        if c in (3, 5, 7):
                            pe.wait_ge(S.mm, 9 + c + 1)
                            release(pe, unit)
                    sum_squares(4)
                boundary(pe, own, l + L + 2)

            for hf in range(TH):
                for k in range(KD):
                    at = hf * D + k * P
                    last = pe.transpose(ps[:, at // 512, at % 512:at % 512 + P], x[:, k, hf * P:(hf + 1) * P], ident[:])
                    if k % 4 == 3:
                        last.then_inc(out_s, 1)

        @block.scalar
        def _(eng):
            own = Own(eng, act_own)
            act_ = nc.scalar.activation

            def squares(n, src, ready, first, each=1):
                for k in range(KD):
                    if ready is not None:
                        eng.wait_ge(ready, first + k * each)
                    act_(tA[:, k, :], src(k), ACT.Square).then_inc(S.sq, 1)

            def root(n, width=D, bank=2, cols=T):
                eng.wait_ge(S.sum, n + 1)
                act_(std[:, 0:cols], ps[:, bank, 0:cols], ACT.Sqrt, bias=eps[:, 0:1], scale=1.0 / width
                     ).then_inc(S.std, 1)

            def shift(p, at, mods, split=False):
                eng.wait_ge(S.ada_mod, units_in(mods - 1))
                for k in range(KD):
                    eng.wait_ge(S.hn, KD * p + k + 1)
                    act_(hsp[:, 0, k, :] if split else h[:, k, :], h[:, k, :], ACT.Identity,
                         bias=mod[:, at + k:at + k + 1]).then_inc(S.h, 1)

            def xk(k):
                return x[:, k, :]

            def high(at, count, l, unit, n, extra=0):
                if n in (0, 4):
                    wait_landed(eng, 1, l, unit, extra, (n // 4,))
                if not isinstance(count, int) or count >= SPLITS:
                    eng.wait_ge(S.wused, count - SPLITS + 1)
                act_(split_part(at % SPLITS, 0, n), piece(unit, n), ACT.Identity).then_inc(S.whi, 1)

            def gate_silu(slot, count):
                eng.wait_ge(S.wused, count)
                act_(silu[:, slot, :, :], ps[:, 0:2, 0:T], ACT.Silu).then_inc(S.sil, 1)

            def high_act(slot, count, pieces=None):
                eng.wait_ge(S.prod, count)
                if pieces is not None:
                    eng.wait_ge(S.wused, pieces)
                act_(asp[:, slot, 0], silu[:, slot, :, :], ACT.Identity).then_inc(S.ph, 1)

            def gather(nw):
                for w in range(nw):
                    eng.wait_ge(S.gt_t, w + 1)
                    for j in range(2):
                        act_(gselT[:, w, 2 * j:2 * j + 2, :], ps[:, 6 + j, :].rearrange("p (g t) -> p g t", g=2),
                             ACT.Identity).then_inc(S.gt, 1)
                    for k in range(KD):
                        eng.wait_ge(S.gath_t, w * KD + k + 1)
                        act_(hsg[:, 0, k, :] if nw == 1 else hg[:, w, k, :], ps[:, k % 4, :], ACT.Identity
                             ).then_inc(S.gath, 1)

            def experts(l, nw):
                def silu_slots(e):
                    if nw == 1:
                        eng.wait_ge(S.wused, KD * (e + 1))
                    else:
                        eng.wait_ge(S.gu, e + 1)
                    for w in range(nw):
                        last = act_(silu[:, e % 2, w, :], ps[:, e % 2 if nw == 1 else w, 0:256], ACT.Silu)
                    last.then_inc(S.sil, 1)

                def high_parts(n0, n1):
                    for n in range(n0, min(n1, KD * NE) if nw == 1 else n0):
                        e, k = divmod(n, KD)
                        if k == 0:
                            wait_landed(eng, 0, l, EXPERT_1[e], parts=(0,))
                        if n >= SPLITS:
                            eng.wait_ge(S.wused, n - SPLITS + 1)
                        act_(wsg[n % SPLITS][:, 0], w3(EXPERT_1[e])[:, 0:2, k, :], ACT.Identity).then_inc(S.whi, 1)

                def results(e):
                    eng.wait_ge(S.down, e + 1)
                    for w in range(nw):
                        last = act_(yg[:, w, :].rearrange("p (n m) -> p n m", n=2), ps[:, 4 + 2 * w:6 + 2 * w, :],
                                    ACT.Identity)
                    last.then_inc(S.yg, 1)
                high_parts(0, KD + 2)
                for e in range(NE):
                    silu_slots(e)
                    high_parts(KD * e + 10, KD * e + 11)
                    if e and e % EPG == 0:
                        results(e - 1)
                    high_parts(KD * e + 11, KD * e + 15)
                    eng.wait_ge(S.at_t, e + 1)
                    act_(actT[:, e % 2, 0:nw], ps[:, 2, 0:nw * 256].rearrange("p (w c n) -> p w c n", w=nw, c=2),
                         ACT.Identity).then_inc(S.at, 1)
                    high_parts(KD * e + 15, KD * e + 18)
                results(NE - 1)

            eng.wait_ge(init_t, 1)
            act_(cvec[:], ps[:, 4, 0:16], ACT.Silu).then_inc(init_v, 1)
            eng.wait_ge(init_v, 1)
            act_(fvec[:], ps[:, 4, 16:24], ACT.Identity).then_inc(init_v, 1)
            eng.wait_ge(bias_w, 1)
            eng.dma_start(scratch, ga.rearrange("p k t -> p (k t)")[0:NH, 0:384]).then_inc(bias_r, 16)
            boundary(eng, own, 0)

            with eng.Fori(0, L) as l:
                squares(0, xk, None, 0)
                root(0, bank=6)
                shift(0, 0, 3)
                n = 0
                for pair in range(2):
                    eng.wait_ge(S.proj, 2 + 2 * pair)
                    act_(sg[:, 2 * pair:2 * pair + 2, :], ps[:, 1 + 2 * pair, :].rearrange("p (c t) -> p c t", c=2),
                         ACT.Sigmoid).then_inc(S.ev, 1)
                for pair in range(2):
                    eng.wait_ge(S.proj, 5 + pair)
                    eng.wait_ge(S.upad, 1)
                    act_(upad[:, 2 * pair:2 * pair + 2, UPAD:], ps[:, pair, :].rearrange("p (c t) -> p c t", c=2),
                         ACT.Identity).then_inc(S.ev, 1)
                for i in range(6, 14):
                    eng.wait_ge(S.proj, i + 1)
                    gate, j = (ga, i - 6) if i < 10 else (gb, i - 10)
                    act_(gate[:, 2 * j:2 * j + 2, :], ps[:, i % 4, :].rearrange("p (c t) -> p c t", c=2),
                         ACT.Sigmoid).then_inc(S.ev, 1)
                    if i == 10:
                        for c in range(KC):
                            eng.wait_ge(S.lnc, c + 1)
                            act_(sg[:, c, :], cv[:, c, :], ACT.Square).then_inc(S.lnq, 1)
                    elif i == 11:
                        eng.wait_ge(S.ln2, 1)
                        act_(std[:, 0:T], ps[:, 7, 0:T], ACT.Sqrt, bias=eps[:, 0:1], scale=1.0 / DC
                             ).then_inc(S.lnd, 1)
                for c in range(KC):
                    eng.wait_ge(S.lnz, c + 1)
                    act_(cv[:, c, :], cv[:, c, :], ACT.Silu, bias=row(vA, ROWS_1, "ln_b", c),
                         scale=row(vA, ROWS_1, "ln_g", c)).then_inc(S.lns, 1)
                squares(1, xk, S.xm, 1)
                root(1, bank=6)
                shift(1, 24, 6)
                for j in range(4):
                    eng.wait_ge(S.ht_t, j + 1)
                    act_(tA.rearrange("p k t -> p (k t)")[:, j * 512:(j + 1) * 512], ps[:, j, :], ACT.Identity
                         ).then_inc(S.ht, 1)
                eng.wait_ge(S.log, 1)
                act_(rt[:, 80:88], rt[:, 72:80], ACT.Exp).then_inc(S.lexp, 1)
                eng.wait_ge(S.log, 2)
                act_(rt[:, 90:92], rt[:, 88:90], ACT.Exp).then_inc(S.lexp, 1)
                eng.wait_ge(S.route, 1)
                fullest = eng.value_load(most[0:1, 0:1], min_val=0, max_val=T)
                before_moe = own.n
                with eng.If(fullest > P):
                    gather(2)
                    experts(l, 2)
                after_moe, own.n = own.n, before_moe
                with eng.Else():
                    gather(1)
                    experts(l, 1)
                assert own.n == after_moe
                boundary(eng, own, l + 1)

            squares(0, xk, None, 0)
            root(0)
            boundary(eng, own, L + 1)

            with eng.Fori(0, L) as l:
                squares(0, xk, None, 0)
                root(0)
                for f in range(2):
                    base, pb, units = UNITS_FF * f, PIECES_FF * f, (FFN_2A, FFN_2B)[f]
                    step = 2 - f

                    def hi(at, e, n, i=None):
                        count, extra = (pb + at, 0) if i is None else (i * 24 + pb + at, i * step)
                        high(at, count, l, units[e], n, extra)
                    for n in range(3):
                        hi(n, 0, n)
                    if f:
                        squares(5, xk, S.xp, 9)
                        root(5)
                        shift(2, 48, 12, split=True)
                    else:
                        shift(0, 0, 3, split=True)
                    hi(3, 0, 3)
                    hi(4, 1, 0)
                    hi(5, 1, 1)
                    gate_silu(base % 2, pb + 4)
                    hi(6, 1, 2)
                    high_act(base % 2, base + 1)
                    hi(7, 1, 3)
                    hi(8, 0, 4)
                    hi(9, 0, 5)
                    gate_silu((base + 1) % 2, pb + 8)
                    hi(10, 2, 0)
                    high_act((base + 1) % 2, base + 2)
                    hi(11, 2, 1)
                    hi(12, 2, 2)
                    with eng.Fori(0, 2) as i:
                        for j in range(4):
                            hi(13 + 6 * j, 2 + j, 3, i)
                            hi(14 + 6 * j, 1 + j, 4, i)
                            hi(15 + 6 * j, 1 + j, 5, i)
                            gate_silu((base + j) % 2, i * 24 + pb + 14 + 6 * j)
                            hi(16 + 6 * j, 3 + j, 0, i)
                            high_act((base + j) % 2, i * 4 + base + 3 + j, i * 24 + pb + 10 + 6 * j)
                            hi(17 + 6 * j, 3 + j, 1, i)
                            hi(18 + 6 * j, 3 + j, 2, i)
                    hi(61, 10, 3)
                    hi(62, 9, 4)
                    hi(63, 9, 5)
                    gate_silu((base + 10) % 2, pb + 62)
                    hi(64, 10, 4)
                    high_act((base + 10) % 2, base + 11, pb + 58)
                    hi(65, 10, 5)
                    eng.wait_ge(S.wused, pb + PIECES_FF)
                    n = 6 * f + (1 - f)
                    squares(n, lambda k: ps[:, 4 + k // 2, k % 2 * T:k % 2 * T + T], None, 0)
                    root(n)
                    if f:
                        continue
                    squares(2, xk, S.xp, 1)
                    root(2)
                    shift(1, 24, 7)
                    tiles = [(qa, 0, 0, "q"), (qa, 2, 1, "q"), (ka, 0, 2, "k"), (qb, 0, 3, "qb"), (qb, 2, 0, "qb"),
                             (kb, 0, 1, "kb"), (kb, 2, 2, "kb")]
                    for n, (dst, c0, bank, name) in enumerate(tiles):
                        eng.wait_ge(S.mm, n + 1)
                        cs = range(1 if name == "k" else 2)
                        for c in cs:
                            last = act_(dst[:, c0 + c, :], ps[:, bank, c * T:(c + 1) * T], ACT.Identity,
                                        bias=row(vB, ROWS_3, name, c0 + c))
                        last.then_inc(S.qk, 1)
                    eng.wait_ge(small[1], (l + 1) * (16 * SMALL_2))
                    for i in range(NH + 3):
                        if i < NH:
                            st = stat[:, i % 4, :]
                            eng.wait_ge(S.nm, i + 1)
                            act_(pr[:, i % 4, 0:T], sc[:, i % 4, 0:T], ACT.Exp, bias=st[:, 2:3], accum_out=st[:, 4:5])
                            last = act_(pr[:, i % 4, T:384], sc[:, i % 4, T:384], ACT.Exp, bias=st[:, 3:4],
                                        accum_out=st[:, 5:6])
                            if i < SWA:
                                own(last)
                                last = act_(st[:, 6:8], st[:, 2:4], ACT.Exp, bias=sinks[:, i:i + 1])
                            last.then_inc(S.e, 1)
                        t = i - 2
                        if 0 <= t < NH:
                            eng.wait_ge(S.T, t + 1)
                            if t >= 2:
                                eng.wait_ge(S.pv, t - 1)
                            act_(pt[:, t % 2, :], ps[:, 6 + t % 2, 0:384], ACT.Identity).then_inc(S.pt, 1)
                        t = i - 3
                        if t >= 0 and t % 2:
                            eng.wait_ge(S.pv, t + 1)
                            act_(yT[:, t // 2, :], ps[:, t // 2 % 2, 0:T], ACT.Identity).then_inc(S.y, 1)
                    squares(3, lambda k: yT[:, k, :], S.y, 1)
                    root(3, DC, 2, 2 * T)
                    squares(4, lambda k: ps[:, 4 + k // 2, k % 2 * T:k % 2 * T + T], S.mm, 9 + 8, 0)
                    root(4)
                boundary(eng, own, l + L + 2)

            for j in range(4):
                eng.wait_ge(out_s, j + 1)
                act_(tA.rearrange("p k t -> p (k t)")[:, j * 512:(j + 1) * 512], ps[:, j, :], ACT.Identity
                     ).then_inc(out_e, 1)

        @block.vector
        def _(eng):
            v_ = nc.vector
            own = Own(eng, dve_own)

            def ada_unit(blk, l, unit, n, slot, cond, extra=0, k0=0, k1=KD):
                w = wada(unit)
                if k0 == 0:
                    wait_landed(eng, blk, l, unit, extra)
                    if isinstance(n, int) and n >= 2:
                        eng.wait_ge(S.ada_sum, n - 1)
                for k in range(k0, k1):
                    if k == 0:
                        last = v_.tensor_scalar(acc[:, slot, :], w[:, 0, :], cond[:, 0:1], None, ALU.mult)
                    else:
                        eng.wait_ge(S.ada_part, n * (KD - 1) + k)
                        last = v_.scalar_tensor_tensor(acc[:, slot, :], w[:, k, :], cond[:, k:k + 1],
                                                       acc[:, slot, :], ALU.mult, ALU.add)
                    last.then_inc(S.ada_part if k < KD - 1 else S.ada_acc, 1)
                if k1 == KD:
                    eng.wait_ge(S.ada_acc, n + 1)
                    release(eng, unit)

            def ada_mod(u, bias_at, bank):
                eng.wait_ge(S.ada_sum, u - AHEAD + 1)
                v_.tensor_tensor(mod[:, bass.ds(u * AC, AC)], ps[:, bank, 0:AC], vA[:, bass.ds(u * AC + bias_at, AC)],
                                 ALU.add).then_inc(S.ada_mod, 1)

            def mod_ahead(bias_at):
                n = AHEAD * AC
                v_.tensor_tensor(mod[:, 0:n], ahead[:], vA[:, bias_at:bias_at + n], ALU.add).then_inc(S.ada_mod, 1)

            def keep_ahead(n, bank):
                eng.wait_ge(S.ada_sum, n)
                v_.tensor_copy(ahead[:], ps[:, bank, 0:AHEAD * AC]).then_inc(S.ada_mod, 1)

            def invert(n, cols=T):
                eng.wait_ge(S.std, n + 1)
                v_.reciprocal(rstd[:, 0:cols], std[:, 0:cols]).then_inc(S.rstd, 1)

            def normalize(n, p, scale_at, gain):
                own.link(v_.scalar_tensor_tensor(gs[:], mod[:, scale_at:scale_at + KD], 1.0, gain, ALU.add, ALU.mult))
                eng.wait_ge(S.rstd, n + 1)
                for k in range(KD):
                    v_.scalar_tensor_tensor(h[:, k, :], x[:, k, :], gs[:, k:k + 1], rstd[:, 0:T], ALU.mult, ALU.mult
                                            ).then_inc(S.hn, 1)

            def low(at, count, unit, n):
                eng.wait_ge(S.whi, count + 1)
                v_.tensor_tensor(split_part(at % SPLITS, 1, n), piece(unit, n), split_part(at % SPLITS, 0, n, F32),
                                 ALU.subtract).then_inc(S.wlo, 1)
                if n in (3, 5):
                    eng.wait_ge(S.wlo, count + 1)
                    release(eng, unit, (n // 4,))

            def product(slot, count):
                eng.wait_ge(S.sil, count)
                v_.tensor_tensor(silu[:, slot, :, :], silu[:, slot, :, :], ps[:, 0:2, T:2 * T], ALU.mult
                                 ).then_inc(S.prod, 1)

            def low_act(slot, count):
                eng.wait_ge(S.ph, count)
                v_.tensor_tensor(asp[:, slot, 1], silu[:, slot, :, :], asp[:, slot, 0].bitcast(F32), ALU.subtract
                                 ).then_inc(S.act, 1)

            def low_tokens(p, at, n):
                for k in range(KD):
                    eng.wait_ge(S.h, KD * n + k + 1)
                    v_.scalar_tensor_tensor(hsp[:, 1, k, :], h[:, k, :], mod[:, at + k:at + k + 1],
                                            hsp[:, 0, k, :].bitcast(F32), ALU.add, ALU.subtract
                                            ).then_inc(S.hl, 1)

            def copy_vectors(n_a, n_b):
                eng.wait_ge(S.vec_t, 1)
                own(v_.tensor_copy(vA[:, 0:n_a], ps[:, 4, 0:n_a]))
                own(v_.tensor_copy(vB[:, 0:n_b], ps[:, 4, 128:128 + n_b]))
                own.wait()

            v_.memset(ones[:], 1.0).then_inc(consts, 1)
            v_.memset(eps[:], EPS).then_inc(consts, 1)
            eng.wait_ge(init_t, 2)
            v_.tensor_tensor(ga.rearrange("p k t -> p (k t)")[0:NH, 0:384], ps[0:NH, 5, 0:384],
                             gb.rearrange("p k t -> p (k t)")[0:NH, 0:384], ALU.add).then_inc(bias_w, 1)
            eng.wait_ge(init_t, 3)
            xf = x[:].rearrange("p k t -> p (k t)")
            eng.wait_ge(init_v, 2)
            for j in range(4):
                last = v_.tensor_copy(xf[:, j * 512:(j + 1) * 512], ps[:, j, :])
            last.then_inc(init_v, 1)
            eng.wait_ge(bias_w, 1)
            eng.sem_inc(init_v, 1)
            ada_unit(0, 0, 0, 0, 0, cvec)
            for i in range(NH // 2):
                eng.wait_ge(init_t, 4 + i)
                v_.tensor_copy(bias[:, 2 * i:2 * i + 2, :], ps[:, 4 + i % 4, :].rearrange("p (c t) -> p c t", c=2)
                               ).then_inc(bias_m, 1)
            for u in range(1, AHEAD):
                ada_unit(0, 0, u, u, u % 2, cvec)
            keep_ahead(AHEAD, 0)
            boundary(eng, own, 0, clears=True)

            with eng.Fori(0, L) as l:
                def ada1(u):
                    ada_unit(0, l, ADA_1[u], u - AHEAD, (u - AHEAD) % 2, cvec)

                def mod1(u):
                    ada_mod(u, ROWS_1["ada"][0], 5)

                v_.memset(vpad[:, :, 0:PAD], 0.0)
                with eng.If(l < L - 1):
                    v_.tensor_copy(cnext[:], cvec[:, 0:KD])
                with eng.Else():
                    v_.tensor_copy(cnext[:], cvec[:, KD:2 * KD])
                copy_vectors(NR_1, TAPS * KC)
                mod_ahead(ROWS_1["ada"][0])
                invert(0)
                eng.wait_ge(S.ada_mod, units_in(2))
                normalize(0, 0, 8, row(vA, ROWS_1, "norm1", 0, KD))

                def glu(pair):
                    eng.wait_ge(S.ev, 1 + pair)
                    v_.tensor_tensor(vpad[:, 2 * pair:2 * pair + 2, PAD:], sg[:, 2 * pair:2 * pair + 2, :],
                                     ps[:, 2 * pair, :].rearrange("p (c t) -> p c t", c=2), ALU.mult
                                     ).then_inc(S.v, 1)
                    eng.wait_ge(S.v, pair + 1)

                def conv(c):
                    own(v_.tensor_scalar(cv[:, c, :], vpad[:, c, 0:T], vB[:, c:c + 1],
                                         row(vA, ROWS_1, "conv_b", c), ALU.mult, ALU.add))
                    for j in range(1, TAPS):
                        own.wait()
                        last = v_.scalar_tensor_tensor(cv[:, c, :], vpad[:, c, j:j + T],
                                                       vB[:, j * KC + c:j * KC + c + 1], cv[:, c, :],
                                                       ALU.mult, ALU.add)
                        if j < TAPS - 1:
                            own(last)
                    last.then_inc(S.conv, 1)
                glu(0)
                conv(0)
                glu(1)
                for c in range(1, KC):
                    conv(c)
                eng.wait_ge(S.ln1, 1)
                for c in range(KC):
                    v_.scalar_tensor_tensor(cv[:, c, :], ps[:, 6, 0:T], -1.0 / DC, cv[:, c, :], ALU.mult, ALU.add
                                            ).then_inc(S.lnc, 1)
                ada1(3)
                eng.wait_ge(S.lnd, 1)
                own.link(v_.reciprocal(rstd[:, 0:T], std[:, 0:T]))
                for c in range(KC):
                    v_.tensor_tensor(cv[:, c, :], cv[:, c, :], rstd[:, 0:T], ALU.mult).then_inc(S.lnz, 1)
                mod1(3)
                for j in range(KD):
                    eng.wait_ge(S.yb_t, j // 2 + 1)
                    v_.scalar_tensor_tensor(gb[:, j, :], ps[:, j // 2, j % 2 * T:j % 2 * T + T],
                                            row(vA, ROWS_1, "pool_s", j), gb[:, j, :], ALU.mult, ALU.mult
                                            ).then_inc(S.yb, 1)
                ada1(4)
                for j in range(KD):
                    eng.wait_ge(S.ya_t, j // 2 + 1)
                    v_.scalar_tensor_tensor(ga[:, j, :], ps[:, j // 2, j % 2 * T:j % 2 * T + T],
                                            row(vA, ROWS_1, "out_b", j), ga[:, j, :], ALU.add, ALU.mult
                                            ).then_inc(S.ya, 1)
                mod1(4)
                ada1(5)
                eng.wait_ge(S.ada_mod, units_in(3))
                for j in range(KD):
                    eng.wait_ge(S.o_t, j // 2 + 1)
                    v_.scalar_tensor_tensor(x[:, j, :], ps[:, j // 2, j % 2 * T:j % 2 * T + T],
                                            mod[:, 16 + j:17 + j], x[:, j, :], ALU.mult, ALU.add
                                            ).then_inc(S.xm, 1)
                    if j == 3:
                        mod1(5)
                        ada1(6)
                mod1(6)
                invert(1)
                eng.wait_ge(S.ada_mod, units_in(6))
                normalize(1, 1, 32, row(vA, ROWS_1, "norm2", 0, KD))
                eng.wait_ge(small[0], (l + 1) * (16 * SMALL_1))
                lg = rt[:, 0:72].rearrange("p (h n) -> p h n", h=TH)
                dg, eg = rt[:, 72:80], rt[:, 80:88]
                d2, e2 = rt[:, 88:90], rt[:, 90:92]
                gmax, gsum, gmin = rt[:, 92:94], rt[:, 94:96], rt[:, 96:98]
                m1, c1, m2, c2 = (rt[:, 98 + 2 * i:100 + 2 * i] for i in range(4))
                wa, wb = rt[:, 106:108], rt[:, 108:110]
                og = rt[:, 112:120].rearrange("p (h n) -> p h n", h=TH)
                o1, o2, tin, cand = (rt[:, 120 + 16 * i:136 + 16 * i].rearrange("p (h n) -> p h n", h=TH)
                                     for i in range(4))
                cm8 = rt[:, 184:200].rearrange("p (h n) -> p h n", h=TH)
                cg = rt[:, 200:208].rearrange("p (h n) -> p h n", h=TH)
                sel = rt[:, 208:272].rearrange("p (h g e) -> p h g e", h=TH, g=GRP)
                rank = rt[:, 272:280].rearrange("p (h n) -> p h n", h=TH)
                slot = rt[:, 280:280 + 2 * WINDOWS_MAX].rearrange("p (w h) -> p w h", h=TH)
                r1, r2 = rt[:, 290:292], rt[:, 292:294]

                def wide(v, n):
                    return v.unsqueeze(2).to_broadcast([P, TH, n])

                def first_of(dst, values, top, c, tmp, n):
                    own.link(v_.tensor_tensor(tmp, values, wide(top, n), ALU.is_equal))
                    for hf in range(TH):
                        own(v_.scalar_tensor_tensor(tmp[:, hf, :], tmp[:, hf, :], -64.0, iota[:, 0:n],
                                                    ALU.mult, ALU.add))
                    own.wait()
                    own.link(v_.tensor_reduce(c, tmp, X, ALU.min))
                    for hf in range(TH):
                        own(v_.tensor_scalar(tmp[:, hf, :], tmp[:, hf, :], c[:, hf:hf + 1], None, ALU.is_equal))
                    own.wait()
                    own.link(v_.tensor_copy(dst, tmp))

                eng.wait_ge(S.log_t, 1)
                for hf in range(TH):
                    own(v_.tensor_tensor(lg[:, hf, :], ps[:, 4, hf * NL:(hf + 1) * NL], rb[:], ALU.add))
                own.wait()
                own.link(v_.tensor_reduce(gmax, lg[:, :, 0:GRP], X, ALU.max))
                v_.tensor_tensor(dg.rearrange("p (h n) -> p h n", h=TH), lg[:, :, 0:GRP], wide(gmax, GRP),
                                 ALU.subtract).then_inc(S.log, 1)
                first_of(og, lg[:, :, 0:GRP], gmax, gmin, cg, GRP)
                eng.sem_inc(S.sel, 1)
                for hf in range(TH):
                    for g in range(GRP):
                        own(v_.tensor_scalar(sel[:, hf, g, :], lg[:, hf, GRP + g * EPG:GRP + (g + 1) * EPG],
                                             og[:, hf, g:g + 1], None, ALU.mult))
                eng.wait_ge(S.rank, 1)
                own(v_.tensor_reduce(rt[:, 296:297], ps[:, 4, 2 * GRP:3 * GRP], X, ALU.max))
                own.link(v_.tensor_tensor(rank, ps[:, 4, 0:2 * GRP].rearrange("p (h n) -> p h n", h=TH), og, ALU.mult))
                own(v_.tensor_copy(most[0:1, 0:1], rt[0:1, 296:297]))
                own.link(v_.tensor_reduce(r1, rank, X, ALU.add))
                own.link(v_.tensor_tensor(rank, og, iota[:, 0:GRP].unsqueeze(1).to_broadcast([P, TH, GRP]), ALU.mult))
                own.link(v_.tensor_reduce(r2, rank, X, ALU.add))
                own.link(v_.scalar_tensor_tensor(r2, r2, float(P), r1, ALU.mult, ALU.add))
                for w in range(WINDOWS_MAX):
                    own.link(v_.tensor_scalar(slot[:, w, :], r1, float(P), -8192.0 if w == 0 else 8192.0,
                                              ALU.is_ge, ALU.mult))
                    own.link(v_.scalar_tensor_tensor(slot[:, w, :], r2, -float(P) * w - (8192.0 if w else 0.0),
                                                     slot[:, w, :], ALU.add, ALU.add))
                for w in range(WINDOWS_MAX):
                    for hf in range(TH):
                        last = v_.tensor_scalar(gsel[:, w, hf, :], iota[:], slot[:, w, hf:hf + 1], None, ALU.is_equal)
                last.then_inc(S.route, 1)
                own.link(v_.tensor_reduce(tin, sel.rearrange("p h g e -> p h e g"), X, ALU.add))
                own.link(v_.tensor_reduce(m1, tin, X, ALU.max))
                first_of(o1, tin, m1, c1, cand, EPG)
                own.link(v_.scalar_tensor_tensor(tin, o1, -3e38, tin, ALU.mult, ALU.add))
                own.link(v_.tensor_reduce(m2, tin, X, ALU.max))
                v_.tensor_tensor(d2, m2, m1, ALU.subtract).then_inc(S.log, 1)
                first_of(o2, tin, m2, c2, cand, EPG)
                eng.wait_ge(S.lexp, 2)
                own.link(v_.tensor_reduce(gsum, eg.rearrange("p (h n) -> p h n", h=TH), X, ALU.add))
                own.link(v_.scalar_tensor_tensor(wa, e2, 1.0, gsum, ALU.add, ALU.mult))
                own.link(v_.reciprocal(wa, wa))
                own.link(v_.tensor_tensor(wb, wa, e2, ALU.mult))
                for hf in range(TH):
                    own.link(v_.tensor_scalar(cm8[:, hf, :], o1[:, hf, :], wa[:, hf:hf + 1], None, ALU.mult))
                    last = v_.scalar_tensor_tensor(cm8[:, hf, :], o2[:, hf, :], wb[:, hf:hf + 1], cm8[:, hf, :],
                                                   ALU.mult, ALU.add)
                    if hf == 0:
                        own(last)
                last.then_inc(S.cs_t, 1)

                def experts(nw):
                    def low_parts(n0, n1, ada=None):
                        steps = iter(range(0, KD, 2))
                        for n in range(n0, min(n1, KD * NE) if nw == 1 else n0):
                            e, k = divmod(n, KD)
                            v, w = w3(EXPERT_1[e])[:, 0:2, k, :], wsg[n % SPLITS]
                            eng.wait_ge(S.whi, n + 1)
                            v_.tensor_tensor(w[:, 1], v, w[:, 0].bitcast(F32), ALU.subtract).then_inc(S.wlo, 1)
                            if k == KD - 1:
                                eng.wait_ge(S.wlo, n + 1)
                                release(eng, EXPERT_1[e], (0,))
                            for k in steps if ada is not None else ():
                                ada(k, k + 2)
                                break
                        for k in steps if ada is not None else ():
                            ada(k, k + 2)
                    if nw == 1:
                        for k in range(KD):
                            eng.wait_ge(S.gath, k + 1)
                            v_.tensor_tensor(hsg[:, 1, k, :], ps[:, k % 4, :], hsg[:, 0, k, :].bitcast(F32),
                                             ALU.subtract).then_inc(S.gathl, 1)

                    def weigh(e):
                        eng.wait_ge(S.sil, e + 1)
                        if e >= 2:
                            eng.wait_ge(S.at_t, e - 1)
                        for w in range(nw):
                            last = v_.scalar_tensor_tensor(act[:, e % 2, w, :], silu[:, e % 2, w, :],
                                                           cslot[:, w, e:e + 1],
                                                           ps[:, e % 2 if nw == 1 else w, 256:512],
                                                           ALU.mult, ALU.mult)
                        last.then_inc(S.act, 1)
                    eng.wait_ge(S.cs, 1)
                    own.link(v_.tensor_copy(cslot[:, 0:nw, :], ps[:, 4, 0:nw * NE].rearrange("p (w n) -> p w n", w=nw)))
                    low_parts(0, KD + 2)
                    for e in range(NE + 1):
                        ada = None
                        if e < NE:
                            weigh(e)
                            low_parts(KD * e + 10, KD * e + 11)
                        if e == 0:
                            def ada(k0, k1):
                                ada_unit(0, l, ADA_1[7], 7 - AHEAD, (7 - AHEAD) % 2, cvec, 0, k0, k1)
                        elif e == 2:
                            ada_mod(7, ROWS_1["ada"][0], 3)
                            eng.wait_ge(S.ada_mod, units_in(7))
                        elif e in AHEAD_AT:
                            def ada(k0, k1, u=AHEAD_AT[e], n=8 - AHEAD + AHEAD_AT[e]):
                                ada_unit(0, l, AHEAD_1[u], n, n % 2, cnext, 0, k0, k1)
                        elif e == NE:
                            keep_ahead(8, 3)
                        if e and e % EPG == 0:
                            g = e // EPG - 1
                            for p in range(4):
                                eng.wait_ge(S.sc_t, 4 * g + p + 1)
                                if g:
                                    eng.wait_ge(S.xs, 4 * g + p - 3)
                                for c in range(2):
                                    k = 2 * p + c
                                    last = v_.scalar_tensor_tensor(x[:, k, :], ps[:, 3 - p % 2, c * T:(c + 1) * T],
                                                                   mod[:, 40 + k:41 + k], x[:, k, :],
                                                                   ALU.mult, ALU.add)
                                    if c == 0:
                                        own(last)
                                last.then_inc(S.xs, 1)
                        if e < NE:
                            low_parts(KD * e + 11, KD * e + 18, ada)
                fullest = eng.value_load(most[0:1, 0:1], min_val=0, max_val=T)
                before_moe = own.n
                with eng.If(fullest > P):
                    experts(2)
                after_moe, own.n = own.n, before_moe
                with eng.Else():
                    experts(1)
                assert own.n == after_moe
                boundary(eng, own, l + 1, clears=True)

            invert(0)
            eng.wait_ge(S.rstd, 1)
            for k in range(KD):
                v_.scalar_tensor_tensor(x[:, k, :], x[:, k, :], fvec[:, k:k + 1], rstd[:, 0:T], ALU.mult, ALU.mult)
            boundary(eng, own, L + 1, clears=True)

            with eng.Fori(0, L) as l:
                def mod2(n):
                    ada_mod(n, 0, 3)

                def post(n, j, factor, gate_at, ready=None):
                    own.link(v_.scalar_tensor_tensor(gs[:], mod[:, gate_at:gate_at + KD], factor,
                                                     vA[:, 96 + 8 * j:104 + 8 * j], ALU.mult, ALU.mult))
                    invert(n)
                    eng.wait_ge(S.rstd, n + 1)
                    for k in range(KD):
                        v_.scalar_tensor_tensor(h[:, k, :], ps[:, 4 + k // 2, k % 2 * T:k % 2 * T + T],
                                                gs[:, k:k + 1], rstd[:, 0:T], ALU.mult, ALU.mult
                                                ).then_inc(S.post, 1)

                c2 = cvec[:, KD:2 * KD]
                copy_vectors(NR_2, NR_3)
                mod_ahead(0)
                for f in range(2):
                    base, pb, units = UNITS_FF * f, PIECES_FF * f, (FFN_2A, FFN_2B)[f]

                    def lo(at, e, n, i=None):
                        low(at, pb + at if i is None else i * 24 + pb + at, units[e], n)

                    def ada_now(k0, k1, j=0, i=None):
                        if f == 0:
                            n, extra = (j, 0) if i is None else (i * 4 + j, i * 2)
                            ada_unit(1, l, ADA_2[AHEAD + j], n, j % 2, c2, extra, k0, k1)

                    def ada_next(u, k0, k1):
                        if f:
                            ada_unit(1, l, AHEAD_2[u], 9 + u, (9 + u) % 2, cnext, 0, k0, k1)
                    if f:
                        lo(0, 0, 0)
                        lo(1, 0, 1)
                        invert(5)
                        normalize(5, 2, 56, vA[:, 88:96])
                    else:
                        invert(0)
                        eng.wait_ge(S.ada_mod, units_in(2))
                        normalize(0, 0, 8, vA[:, 72:80])
                        lo(0, 0, 0)
                        lo(1, 0, 1)
                    low_tokens(2 * f, 48 * f, 2 * f)
                    lo(2, 0, 2)
                    lo(3, 0, 3)
                    ada_next(1, 0, 4)
                    lo(4, 1, 0)
                    ada_next(1, 4, KD)
                    lo(5, 1, 1)
                    product(base % 2, base + 1)
                    lo(6, 1, 2)
                    low_act(base % 2, base + 1)
                    lo(7, 1, 3)
                    ada_next(2, 0, 4)
                    lo(8, 0, 4)
                    ada_next(2, 4, KD)
                    lo(9, 0, 5)
                    product((base + 1) % 2, base + 2)
                    lo(10, 2, 0)
                    low_act((base + 1) % 2, base + 2)
                    lo(11, 2, 1)
                    lo(12, 2, 2)
                    if f:
                        keep_ahead(12, 3)
                    with eng.Fori(0, 2) as i:
                        for j in range(4):
                            ada_now(0, 2, j, i)
                            lo(13 + 6 * j, 2 + j, 3, i)
                            ada_now(2, 5, j, i)
                            lo(14 + 6 * j, 1 + j, 4, i)
                            ada_now(5, KD, j, i)
                            lo(15 + 6 * j, 1 + j, 5, i)
                            product((base + j) % 2, i * 4 + base + 3 + j)
                            lo(16 + 6 * j, 3 + j, 0, i)
                            low_act((base + j) % 2, i * 4 + base + 3 + j)
                            lo(17 + 6 * j, 3 + j, 1, i)
                            lo(18 + 6 * j, 3 + j, 2, i)
                            if f == 0:
                                mod2(i * 4 + AHEAD + j)
                    lo(61, 10, 3)
                    lo(62, 9, 4)
                    lo(63, 9, 5)
                    if f == 0:
                        ada_unit(1, l, ADA_2[11], 8, 0, c2)
                    product((base + 10) % 2, base + 11)
                    lo(64, 10, 4)
                    low_act((base + 10) % 2, base + 11)
                    lo(65, 10, 5)
                    if f == 0:
                        mod2(11)
                    post(1 if f == 0 else 6, 2 * f, 0.5, 16 + 48 * f)
                    if f:
                        continue
                    invert(2)
                    normalize(2, 1, 32, vA[:, 80:88])
                    eng.wait_ge(small[1], (l + 1) * (16 * SMALL_2))
                    eng.wait_ge(S.qk, 3)
                    for hf in range(TH):
                        last = v_.tensor_tensor(va[:, hf, :], ps[:, 2, T + hf * P:T + (hf + 1) * P], vbias[:, 0:P],
                                                ALU.add)
                    last.then_inc(S.vv, 1)
                    for hf in range(TH):
                        eng.wait_ge(S.mm, 8 + hf)
                        v_.tensor_tensor(vb[:, hf, :], ps[:, 3 * (1 - hf), :], vbias[:, P:], ALU.add
                                         ).then_inc(S.vv, 1)
                    for i in range(NH + 1):
                        if i < NH:
                            st = stat[:, i % 4, :]
                            bank = ps[:, 4 + i % 2, :]
                            eng.wait_ge(S.S, i + 1)
                            own(v_.scalar_tensor_tensor(sc[:, i % 4, 0:T], bank[:, 0:T], HD ** -0.5, bias[:, i, :],
                                                        ALU.mult, ALU.add))
                            v_.scalar_tensor_tensor(sc[:, i % 4, T:384], bank[:, T:384], HD ** -0.5,
                                                    bias[:, i, P:T], ALU.mult, ALU.add).then_inc(S.sc, 1)
                            eng.wait_ge(S.sc, i + 1)
                            own(v_.tensor_reduce(st[:, 0:1], sc[:, i % 4, 0:T], X, ALU.max))
                            own.link(v_.tensor_reduce(st[:, 1:2], sc[:, i % 4, T:384], X, ALU.max))
                            if i < SWA:
                                last = v_.tensor_scalar(st[:, 2:4], st[:, 0:2], sinks[:, i:i + 1], -1.0,
                                                        ALU.max, ALU.mult)
                            else:
                                last = v_.tensor_scalar(st[:, 2:4], st[:, 0:2], -1.0, None, ALU.mult)
                            last.then_inc(S.nm, 1)
                        t = i - 1
                        if t >= 0:
                            st = stat[:, t % 4, :]
                            eng.wait_ge(S.e, t + 1)
                            if t < SWA:
                                own.link(v_.tensor_tensor(st[:, 4:6], st[:, 4:6], st[:, 6:8], ALU.add))
                            own.link(v_.reciprocal(st[:, 4:6], st[:, 4:6]))
                            v_.tensor_scalar(pr[:, t % 4, 0:T], pr[:, t % 4, 0:T], st[:, 4:5], None, ALU.mult)
                            v_.tensor_scalar(pr[:, t % 4, T:384], pr[:, t % 4, T:384], st[:, 5:6], None, ALU.mult
                                             ).then_inc(S.p, 1)
                    invert(3, 2 * T)
                    eng.wait_ge(S.rstd, 4)
                    for k in range(KD):
                        v_.scalar_tensor_tensor(yT[:, k, :], yT[:, k, :], row(vB, ROWS_3, "gain", k),
                                                rstd[:, k // 4 * T:k // 4 * T + T], ALU.mult, ALU.mult
                                                ).then_inc(S.yn, 1)
                    ada_unit(1, l, AHEAD_2[0], 9, 1, cnext)
                    post(4, 1, 1.0, 40)
                boundary(eng, own, l + L + 2, clears=True)

        @block.gpsimd
        def _(eng):
            g_ = nc.gpsimd
            own = Own(eng, pool_own)
            tmp = act[:].rearrange("p a b t -> p (a b t)")[:, 0:P]
            own(g_.memset(ident[:], 0.0))
            own(g_.memset(tmp, 0.0))
            own.wait()
            g_.affine_select(out=ident[:], in_=ident[:], compare_op=ALU.not_equal, fill=1.0, base=0,
                             pattern=[[-1, P]], channel_multiplier=1).then_inc(consts, 1)
            g_.affine_select(out=tmp, in_=tmp, compare_op=ALU.not_equal, fill=1.0, base=-(P - 1),
                             pattern=[[1, P]], channel_multiplier=1).then_inc(consts, 1)
            for g, w in enumerate(WINDOWS):
                own.link(g_.memset(invc[:, g, :], 1.0 / w))
                for t in range(w - 1):
                    own(g_.memset(invc[:, g, t:t + 1], 1.0 / (t + 1)))
            own(g_.iota(iota[:], [[1, SLOTS]], base=0, channel_multiplier=0, allow_small_or_imprecise_dtypes=True))
            own.link(g_.memset(before[:], 1.0))
            own(g_.affine_select(out=before[:], in_=before[:], compare_op=ALU.is_gt, fill=0.0, base=0,
                                 pattern=[[1, P]], channel_multiplier=-1))
            boundary(eng, own, 0)

            with eng.Fori(0, L) as l:
                g_.memset(upad[:, :, 0:UPAD], 0.0).then_inc(S.upad, 1)
                eng.wait_ge(S.upad, 1)
                own(g_.memset(w1[:, :, 0:UPAD], 0.0))
                own(g_.memset(w2[:, :, 0:UPAD], 0.0))
                eng.wait_ge(S.ev, 4)
                src = upad
                for s in range(KC):
                    dst = (w1, w2)[s % 2]
                    own.wait()
                    own(g_.tensor_tensor(dst[:, s:, 1 << s:], src[:, s:, 1 << s:], src[:, s:, 0:UPAD + T - (1 << s)],
                                         ALU.add))
                    src = dst
                own.wait()
                for g, w in enumerate(WINDOWS):
                    s = (w1, w2)[g % 2]
                    own(g_.tensor_tensor(w1[:, g, UPAD:2 * UPAD], s[:, g, UPAD:2 * UPAD], invc[:, g, :], ALU.mult))
                    own(g_.tensor_scalar(w1[:, g, 2 * UPAD:], s[:, g, 2 * UPAD:], 1.0 / w, 1.0, ALU.mult, ALU.mult))
                own.wait()
                g_.tensor_tensor(w1[:, :, UPAD:], w1[:, :, UPAD:], upad[:, :, UPAD:], ALU.subtract
                                 ).then_inc(S.pooled, 1)
                for j in range(4):
                    eng.wait_ge(S.ya, 2 * j + 2)
                    g_.tensor_tensor(ga[:, 2 * j:2 * j + 2, :], ga[:, 2 * j:2 * j + 2, :], gb[:, 2 * j:2 * j + 2, :],
                                     ALU.add).then_inc(S.mix, 1)
                boundary(eng, own, l + 1)
            boundary(eng, own, L + 1)
            with eng.Fori(0, L) as l:
                for n in range(3):
                    for k in range(KD):
                        eng.wait_ge(S.post, KD * n + k + 1)
                        g_.tensor_tensor(x[:, k, :], x[:, k, :], h[:, k, :], ALU.add).then_inc(S.xp, 1)
                boundary(eng, own, l + L + 2)


_INS = ["x", "c", "mixer_norm_g", "w_ada", "b_ada", "w_in", "conv_w", "conv_b", "conv_ln_g", "conv_ln_b",
        "w_conv_out", "b_conv_out", "pool_w", "pool_scale", "w_out", "ffn_norm_g", "w_router_group",
        "b_router_group", "w_router_expert", "b_router_expert", "w_expert_gate", "w_expert_up", "w_expert_down",
        "final_norm_g", "c_2", "rel_bias_2", "ada_w_2", "ada_b_2", "norm_pre_2", "norm_post_2", "ffn_w_gate_2",
        "ffn_w_up_2", "ffn_w_down_2", "mix_w_in_2", "mix_b_in_2", "mix_w_out_2", "attn_sinks_2", "group_gain_2"]


def shape_constants():
    dist = 2 * P - 1 - np.arange(384)
    n = np.maximum(dist, 0)
    exact = BUCKETS // 2
    large = exact + (np.log(np.maximum(n, 1).astype(np.float32) / np.float32(exact))
                     / math.log(MAX_DIST / exact) * (BUCKETS - exact)).astype(np.int32)
    bucket = np.where(n < exact, n, np.minimum(large, BUCKETS - 1))
    onehot = ((bucket[None] == np.arange(BUCKETS)[:, None]) & (dist >= 0)[None]).astype(np.float32)
    mask = np.where(dist >= 0, 0.0, NEG)[None].repeat(NH, 0)
    mask[:SWA, dist >= WIN] = NEG
    return onehot, mask.astype(np.float32)


def kernel(**inputs):
    import concourse.bacc as _bacc
    from concourse.bass_utils import run_bass_kernel_spmd as _run

    nc = _bacc.Bacc("TRN2", target_bir_lowering=False, num_devices=1)
    onehot, mask = shape_constants()
    given = {name: np.ascontiguousarray(inputs[name]) for name in _INS}
    given["bucket_onehot"], given["mask"] = onehot, mask
    arrays, aps = {}, {}
    for name, v in given.items():
        arrays[f"in_{name}_dram"] = v
        aps[name] = nc.dram_tensor(f"in_{name}_dram", v.shape, mybir.dt.from_np(v.dtype), kind="ExternalInput").ap()
    out = nc.dram_tensor("out_0_dram", (1, T, D), F32, kind="ExternalOutput").ap()
    scratch = nc.dram_tensor("bias_rows", (NH, 384), F32, kind="Internal").ap()
    build(nc, Named(**aps), out, scratch)
    r = _run(nc, [arrays], core_ids=[0])
    return r.results[0]["out_0_dram"]
```
